# Optimizing a Trainium2 kernel written in Bass

```python
import jax, jax.numpy as jnp
from jax import lax
import numpy as np

D_MODEL = 1024
BATCH = 1
SEQ = 2048
DEPTH = 1
DEC_BATCH = 8
DEC_SEQ = 8
PAST_LEN = 2048
PAGE_SIZE = 128

CONV_DIM = 1024
CONV_WIDTH = 3
N_HEADS = 8
N_KV_HEADS = 2
HEAD_DIM = 128
ATT_DIM = N_HEADS * HEAD_DIM
N_IDX_HEADS = 8
IDX_DIM = 64
TOPK_MAX = 256
Q_BLOCK = 128
EPS = 1e-6
NEG_INF = -1e30

kernel_name = "gated_conv_dsa_parallel_hybrid_step"

def _proj_sizes():
    return (CONV_DIM, CONV_DIM, CONV_DIM, CONV_DIM,
            ATT_DIM, N_KV_HEADS * HEAD_DIM, N_KV_HEADS * HEAD_DIM,
            N_IDX_HEADS * IDX_DIM, IDX_DIM, N_IDX_HEADS, ATT_DIM,
            D_MODEL, D_MODEL)

def _split_proj(p):
    offs = np.cumsum(np.array(_proj_sizes()))[:-1].tolist()
    return jnp.split(p, offs, axis=-1)

def _rms(x, g):
    xf = x.astype(jnp.float32)
    xf = xf * lax.rsqrt(jnp.mean(xf * xf, axis=-1, keepdims=True) + EPS)
    return xf.astype(x.dtype) * g

def _adaln(x, c, norm_g, w_mod, b_mod):
    mod = jax.nn.silu(c) @ w_mod + b_mod
    shift, scale, gate = jnp.split(mod, 3, axis=-1)
    h = _rms(x, norm_g) * (1 + scale[:, None, :]) + shift[:, None, :]
    return h, gate[:, None, :]

def _short_conv(prev, u, conv_w):
    t = u.shape[1]
    buf = jnp.concatenate([prev.astype(u.dtype), u], axis=1)
    y = conv_w[0] * buf[:, 0:t]
    for j in range(1, CONV_WIDTH):
        y = y + conv_w[j] * buf[:, j:j + t]
    return y, buf[:, -(CONV_WIDTH - 1):]

def _index_scores(qi, wi, kidx):
    s = jnp.einsum('btid,bsd->btis', qi.astype(jnp.float32), kidx.astype(jnp.float32)) * (IDX_DIM ** -0.5)
    w = wi.astype(jnp.float32) * (N_IDX_HEADS ** -0.5)
    return jnp.einsum('btis,bti->bts', jax.nn.relu(s), w)

def _sparse_attend(q, k_sel, v_sel, valid):
    b, t = q.shape[:2]
    qg = q.reshape(b, t, N_KV_HEADS, N_HEADS // N_KV_HEADS, HEAD_DIM).astype(jnp.float32)
    logits = jnp.einsum('btkgd,btnkd->btkgn', qg, k_sel.astype(jnp.float32)) * (HEAD_DIM ** -0.5)
    logits = jnp.where(valid[:, :, None, None, :], logits, NEG_INF)
    p = jax.nn.softmax(logits, axis=-1)
    o = jnp.einsum('btkgn,btnkd->btkgd', p, v_sel.astype(jnp.float32))
    return o.reshape(b, t, ATT_DIM).astype(q.dtype)

def _gather_rows(a, idx):
    return jax.vmap(lambda ab, ib: ab[ib])(a, idx)

def _prompt_attention(q, qi, wi, k, v, kidx):
    b, s = q.shape[:2]
    topk = min(TOPK_MAX, s // 4)
    nb = s // Q_BLOCK
    key_pos = jnp.arange(s)

    def blk(args):
        qb, qib, wib, pos = args
        sc = _index_scores(qib, wib, kidx)
        sc = jnp.where(key_pos[None, None, :] <= pos[None, :, None], sc, NEG_INF)
        _, idx = lax.top_k(sc, topk)
        valid = idx <= pos[None, :, None]
        return _sparse_attend(qb, _gather_rows(k, idx), _gather_rows(v, idx), valid)

    def to_blocks(a):
        return jnp.moveaxis(a.reshape((b, nb, Q_BLOCK) + a.shape[2:]), 1, 0)

    out = lax.map(blk, (to_blocks(q), to_blocks(qi), to_blocks(wi),
                        jnp.arange(s).reshape(nb, Q_BLOCK)))
    return jnp.moveaxis(out, 0, 1).reshape(b, s, ATT_DIM)

def _sample_attention(q, qi, wi, k_new, v_new, kidx_new, pool_k, pool_v, pool_kidx, page_table):
    db, t = q.shape[:2]
    n_pages = page_table.shape[1]
    page = pool_k.shape[1]
    past = n_pages * page
    total = past + t
    topk = min(TOPK_MAX, total // 4)
    kidx_past = pool_kidx[page_table].reshape(db, past, IDX_DIM)
    kidx_all = jnp.concatenate([kidx_past.astype(kidx_new.dtype), kidx_new], axis=1)
    qpos = past + jnp.arange(t)
    sc = _index_scores(qi, wi, kidx_all)
    sc = jnp.where(jnp.arange(total)[None, None, :] <= qpos[None, :, None], sc, NEG_INF)
    _, idx = lax.top_k(sc, topk)
    valid = idx <= qpos[None, :, None]
    in_past = idx < past
    pidx = jnp.minimum(idx, past - 1)
    phys = jax.vmap(lambda pt, i: pt[i])(page_table, pidx // page)
    off = pidx % page
    nidx = jnp.clip(idx - past, 0, t - 1)

    def pick(pool, new):
        old = pool[phys, off]
        cur = _gather_rows(new, nidx)
        return jnp.where(in_past[..., None, None], old.astype(new.dtype), cur)

    return _sparse_attend(q, pick(pool_k, k_new), pick(pool_v, v_new), valid)

def _layer(x, c, conv_prev, attend, norm_g, w_mod, b_mod, w_in, conv_w, q_norm, k_norm, w_pa, w_pb, w_out):
    b, t, _ = x.shape
    h, gate = _adaln(x, c, norm_g, w_mod, b_mod)
    (u_h, u_b, u_c, z_a, q, k, v, qi, ki, wi, z_b, g_a, g_b) = _split_proj(h @ w_in)
    q = _rms(q.reshape(b, t, N_HEADS, HEAD_DIM), q_norm)
    k = _rms(k.reshape(b, t, N_KV_HEADS, HEAD_DIM), k_norm)
    v = v.reshape(b, t, N_KV_HEADS, HEAD_DIM)
    qi = qi.reshape(b, t, N_IDX_HEADS, IDX_DIM)
    conv_out, conv_state = _short_conv(conv_prev, u_c * u_h, conv_w)
    branch_a = (u_b * conv_out) * jax.nn.silu(z_a)
    branch_b = attend(q, qi, wi, k, v, ki) * jax.nn.silu(z_b)
    merged = jax.nn.sigmoid(g_a) * (branch_a @ w_pa) + jax.nn.sigmoid(g_b) * (branch_b @ w_pb)
    y = x + gate * (merged @ w_out)
    return y, k, v, ki, conv_state

def setup_inputs(seed: int = 0) -> dict:
    key = jax.random.key(seed)
    ks = jax.random.split(key, 24)
    f32 = jnp.float32
    n_pages = PAST_LEN // PAGE_SIZE
    n_used = DEC_BATCH * n_pages
    n_phys = n_used + max(1, n_used // 4)
    p_cols = int(sum(_proj_sizes()))
    page_table = jax.random.permutation(ks[0], n_phys)[:n_used].reshape(DEC_BATCH, n_pages).astype(jnp.int32)
    nrm = lambda k, shape, s: jax.random.normal(k, shape, f32) * s
    return {
        "x_prompt": nrm(ks[1], (BATCH, SEQ, D_MODEL), 1.0),
        "x_sample": nrm(ks[2], (DEC_BATCH, DEC_SEQ, D_MODEL), 1.0),
        "c_prompt": nrm(ks[3], (BATCH, D_MODEL), 1.0),
        "c_sample": nrm(ks[4], (DEC_BATCH, D_MODEL), 1.0),
        "cache_k": nrm(ks[5], (DEPTH, n_phys, PAGE_SIZE, N_KV_HEADS, HEAD_DIM), 1.0),
        "cache_v": nrm(ks[6], (DEPTH, n_phys, PAGE_SIZE, N_KV_HEADS, HEAD_DIM), 1.0),
        "cache_kidx": nrm(ks[7], (DEPTH, n_phys, PAGE_SIZE, IDX_DIM), 1.0),
        "state_conv": nrm(ks[8], (DEPTH, DEC_BATCH, CONV_WIDTH - 1, CONV_DIM), 1.0),
        "page_table": page_table,
        "norm_g": 1.0 + nrm(ks[9], (DEPTH, D_MODEL), 0.05),
        "w_mod": nrm(ks[10], (DEPTH, D_MODEL, 3 * D_MODEL), 0.5 * D_MODEL ** -0.5),
        "b_mod": nrm(ks[11], (DEPTH, 3 * D_MODEL), 0.02),
        "w_in": nrm(ks[12], (DEPTH, D_MODEL, p_cols), D_MODEL ** -0.5),
        "conv_w": nrm(ks[13], (DEPTH, CONV_WIDTH, CONV_DIM), CONV_WIDTH ** -0.5),
        "q_norm": 1.0 + nrm(ks[14], (DEPTH, HEAD_DIM), 0.05),
        "k_norm": 1.0 + nrm(ks[15], (DEPTH, HEAD_DIM), 0.05),
        "w_proj_a": nrm(ks[16], (DEPTH, CONV_DIM, D_MODEL), CONV_DIM ** -0.5),
        "w_proj_b": nrm(ks[17], (DEPTH, ATT_DIM, D_MODEL), ATT_DIM ** -0.5),
        "w_out": nrm(ks[18], (DEPTH, D_MODEL, D_MODEL), D_MODEL ** -0.5),
    }

def reference(x_prompt, x_sample, c_prompt, c_sample, cache_k, cache_v, cache_kidx, state_conv, page_table,
              norm_g, w_mod, b_mod, w_in, conv_w, q_norm, k_norm, w_proj_a, w_proj_b, w_out):
    yp, ys = x_prompt, x_sample
    kp, vp, kip, cp = [], [], [], []
    kss, vss, kis, css = [], [], [], []
    for l in range(DEPTH):
        wl = (norm_g[l], w_mod[l], b_mod[l], w_in[l], conv_w[l], q_norm[l], k_norm[l],
              w_proj_a[l], w_proj_b[l], w_out[l])
        prev0 = jnp.zeros((yp.shape[0], CONV_WIDTH - 1, CONV_DIM), yp.dtype)
        yp, k1, v1, ki1, c1 = _layer(yp, c_prompt, prev0, _prompt_attention, *wl)
        kp.append(k1); vp.append(v1); kip.append(ki1); cp.append(c1)
        pk, pv, pki = cache_k[l], cache_v[l], cache_kidx[l]

        def attend_s(q, qi, wi, k, v, ki, pk=pk, pv=pv, pki=pki):
            return _sample_attention(q, qi, wi, k, v, ki, pk, pv, pki, page_table)

        ys, k2, v2, ki2, c2 = _layer(ys, c_sample, state_conv[l], attend_s, *wl)
        kss.append(k2); vss.append(v2); kis.append(ki2); css.append(c2)
    return (yp, ys, jnp.stack(kp), jnp.stack(vp), jnp.stack(kip), jnp.stack(cp),
            jnp.stack(kss), jnp.stack(vss), jnp.stack(kis), jnp.stack(css))


_drawn_inputs = setup_inputs


def setup_inputs(seed=0):
    import zlib

    import numpy as np

    out = dict(_drawn_inputs(seed))
    spreads = {}
    factors = {'cache_k': 6.474, 'cache_v': 5.188, 'cache_kidx': 5.534, 'q_norm': 8.0}
    for name, (base, spread) in spreads.items():
        noise = np.random.default_rng([zlib.crc32(name.encode()), seed]).standard_normal(out[name].shape)
        drawn = base * np.exp(spread * noise) if base else spread * noise
        out[name] = __import__('jax').numpy.asarray(drawn.astype(out[name].dtype))
    for name, factor in factors.items():
        out[name] = (out[name] * factor).astype(out[name].dtype)
    return out
```

```python
from contextlib import ExitStack

import numpy as np

import concourse.bass as bass
from concourse import mybir

F32, F32R = mybir.dt.float32, mybir.dt.float32r
BF16, F16 = mybir.dt.bfloat16, mybir.dt.float16
U32, I32 = mybir.dt.uint32, mybir.dt.int32
ALU = mybir.AluOpType
ACT = mybir.ActivationFunctionType
AX_X = mybir.AxisListType.X

P = 128
D = 1024
SEQ = 2048
NSEQ, NNEW = 8, 8
PAGE = 128
NPAGES = 16
PAST = NPAGES * PAGE
RUN = PAST // P
PER_PAGE = PAGE // RUN
HEADS, KV, HD = 8, 2, 128
IH, ID = 8, 64
TOPK = 256
EPS = 1e-6
NEG = -1e30
TILE = 512
TILES = SEQ // TILE
BLOCKS = TILE // P
KC = D // P
NS = NSEQ * NNEW
HALF = NS // 2
STEPS = 28
ACT_COPIES = 3

SIZES = [("uh", 1024), ("ub", 1024), ("uc", 1024), ("za", 1024), ("q", 1024), ("k", 256), ("v", 256),
         ("qi", 512), ("ki", 64), ("wi", 8), ("zb", 1024), ("ga", 1024), ("gb", 1024)]
OFFSET = {}
_at = 0
for _name, _size in SIZES:
    OFFSET[_name] = _at
    _at += _size
WIDTH = _at

PROJ_A = [("ki", 0)] + [("k", h) for h in range(KV)] + [("v", h) for h in range(KV)] \
    + [("q", h) for h in range(HEADS)] + [("qi", i) for i in range(IH // 2)]
PROJ_B = [(n, f) for f in range(KC) for n in ("uh", "uc", "ub", "za")] \
    + [(n, f) for f in range(KC) for n in ("ga", "pa")] \
    + [("zb", f) for f in range(KC)] + [("gb", f) for f in range(KC)]
OUT_B = [("pb", f) for f in range(KC)]
OUT_Y = [("wo", f) for f in range(KC)]
GEMMS = [(t, n, f) for t in range(TILES) for n, f in PROJ_A + PROJ_B + OUT_B + OUT_Y]
NUMBER = {g: j for j, g in enumerate(GEMMS)}


def parts(t):
    return ("P", "S") if t == 0 else ("P",)


PRODUCTS = [(j, p) for j, (t, n, f) in enumerate(GEMMS) for p in parts(t)]
PBANK = {jp: i % 4 for i, jp in enumerate(PRODUCTS)}


class Signal:

    def __init__(self, sem, values, known, by=1):
        self.sem, self.values, self.known, self.by, self.n = sem, values, known, by, 0

    def mark(self, *event):
        self.n += self.by
        self.values[event] = self.n
        return self.sem, self.by

    def mark_loop(self, times, *event):
        self.n += self.by * times
        self.values[event] = self.n

    def at(self, *event):
        return self.sem, self.values[event] if self.known else 1

    def end(self):
        return self.sem, max(self.values.values(), default=1)


def program(nc, ins, outs, plan):
    known = bool(plan)
    ctx = ExitStack()

    def signal(name, by=1):
        return Signal(ctx.enter_context(nc.semaphore(name)), plan.setdefault(name, {}), known, by)

    banks = plan.setdefault("banks", {})

    def bank(*key):
        return banks[key] if known else 4

    base = (nc.sbuf_base + 63) // 64 * 64
    cursor = [base]

    def region(size):
        at = cursor[0]
        cursor[0] += (size + 63) // 64 * 64
        assert cursor[0] <= nc.sbuf_usable_end, (cursor[0], nc.sbuf_usable_end)
        return at

    def at(name, shape, dt, offset):
        return nc.alloc_sbuf_tensor_at(name, shape, dt, offset=offset)

    def own(name, shape, dt=F32):
        size = int(np.prod(shape[1:])) * (2 if dt in (BF16, F16) else 4)
        return at(name, shape, dt, region(size))

    rKT, rV, rKH, rKL = region(16384), region(16384), region(8192), region(8192)
    rH, rW, rB, rM, rS = region(32768), region(24576), region(32768), region(16384), region(32768)
    KT = at("KT", [P, KV, SEQ], F32, rKT)
    V = at("V", [P, SEQ // P, KV * HD], F32, rV)
    KIH = at("KIH", [P, SEQ], F32R, rKH)
    KIL = at("KIL", [P, SEQ], F32R, rKL)
    HTH = at("HTH", [P, KC, TILE], F32R, rH)
    HTL = at("HTL", [P, KC, TILE], F32R, rH + 16384)
    LP = at("LP", [P, 2, 2, SEQ], F32, rH)
    BBH = at("BBH", [P, KC, TILE], F32R, rH)
    BBL = at("BBL", [P, KC, TILE], F32R, rH + 16384)
    WR = [at(f"WR{i}", [P, KC, P], F32, rW + 8192 * i) for i in range(3)]
    WLH = [at(f"WLH{i}", [P, 2, KC, P], F32R, rW + 8192 * i) for i in range(3)]
    WL, WH = ([a[:, part] for a in WLH] for part in range(2))
    XN = at("XN", [P, BLOCKS, D], F32, rB)
    SQ = [at(f"SQ{i}", [P, TILE], F32, rB + 2048 * i) for i in range(2)]
    RS = [at(f"RS{i}", [P, TILE], F32, rB + 2048 * (2 + i)) for i in range(2)]
    QO = [at(f"QO{i}", [P, TILE], F32, rB + 2048 * (4 + i)) for i in range(2)]
    KO = at("KO", [P, BLOCKS, P], F32, rB + 2048 * 6)
    KIO = at("KIO", [P, BLOCKS, ID], F32, rB + 2048 * 7)
    AS = at("AS", [P, 8, TILE], F32, rB + 16384)
    BAH = at("BAH", [P, KC, TILE], F32R, rB)
    BAL = at("BAL", [P, KC, TILE], F32R, rB + 16384)
    SZB = at("SZB", [P, KC, TILE], F32, rB)
    GB = at("GB", [P, KC, TILE], F32, rB + 16384)
    XR = [at(f"XR{i}", [P, BLOCKS, P], F32, rB + 16384 + 2048 * i) for i in range(2)]
    YO = [at(f"YO{i}", [P, BLOCKS, P], F32, rB + 20480 + 2048 * i) for i in range(2)]
    QI = at("QI", [P, IH, TILE], F32R, rM)
    BB = at("BB", [P, HEADS, TILE], F32, rM)
    SC = at("SC", [P, BLOCKS, SEQ], F32, rS)
    MGH = at("MGH", [P, KC, TILE], F32R, rS)
    MGL = at("MGL", [P, KC, TILE], F32R, rS + 16384)
    MW = [at(f"MW{i}", [P, KC, P], F32, rS + 4096 * i) for i in range(8)]

    U = own("U", [P, TILE + 2])
    rT = region(5 * 2048)
    T = [at(f"T{i}", [P, TILE], F32, rT + 2048 * i) for i in range(5)]
    QL = [at(f"QL{i}", [P, 2, P], F32, rT + 3 * 2048 + 1024 * i) for i in range(2)]
    rJ = region(4224)
    JUNK = at("JUNK", [P, PAST + NS], BF16, rJ)
    RB = [at(f"RB{i}", [P, 256], F32, rJ + 1024 * i) for i in range(2)]
    DG = [at(f"DG{i}", [P, 256], F32, rJ + 2048 + 1024 * i) for i in range(2)]
    GT = own("GT", [P, TILE], F16)
    BD = own("BD", [P, TILE], F16)
    ident = own("ident", [P, P])
    ones = own("ones", [P, P])
    COL = own("COL", [P, 58])
    MOD = own("MOD", [P, 24, 9])
    AM = own("AM", [P, KC, 9])
    WI = own("WI", [P, BLOCKS, IH])
    HALO = own("HALO", [P, KC, 2])
    SMALL = own("SMALL", [P, 96])
    PFX = own("PFX", [P, TILE])

    def small(a, n):
        return SMALL[:, a:a + n]

    SS, SV, RT, R1, R2 = small(0, 4), small(4, 4), small(8, 4), small(12, 4), small(16, 4)
    EPSC = small(20, 1)
    LO, HI, MID, CNT, NEED, ABS = (small(24 + 6 * i, 5) for i in range(6))
    PM = small(60, 16).rearrange("p (u h c) -> p u h c", u=2, h=2)
    NM = small(76, 4).rearrange("p (u h) -> p u h", u=2)
    SUM = small(80, 4).rearrange("p (u h) -> p u h", u=2)
    RIN = small(84, 4).rearrange("p (u h) -> p u h", u=2)
    DUMMY = small(88, 1)
    GE = own("GE", [P, 5], U32)
    LT = own("LT", [P, 5], U32)

    free_k = [rKT + 2048, rKT + 4096, rKT + 6144, rKT + 10240, rKT + 12288, rKT + 14336,
              rKH + 2048, rKH + 4096, rKH + 6144, rKL + 2048, rKL + 4096, rKL + 6144]
    sHT, sMG = at("sHT", [P, KC, 2 * NS], F32R, free_k[0]), at("sMG", [P, KC, 2 * NS], F32R, free_k[0])
    sBA, sBB2 = at("sBA", [P, KC, 2 * NS], F32R, free_k[3]), at("sBB2", [P, KC, 2 * NS], F32R, free_k[3])
    (sHTH, sHTL), (sMGH, sMGL), (sBAH, sBAL), (sBBH, sBBL) = (
        (a[:, :, 0:NS], a[:, :, NS:2 * NS]) for a in (sHT, sMG, sBA, sBB2))
    sSZB, sGB = at("sSZB", [P, KC, NS], F32, free_k[2]), at("sGB", [P, KC, NS], F32, free_k[5])
    sMA, sBB = at("sMA", [P, KC, NS], F32, free_k[6]), at("sBB", [P, KC, NS], F32, free_k[7])
    sQ = at("sQ", [P, NSEQ, HEADS, NNEW], F32, free_k[8])
    sKT, sKIH, sKIL = (at("sKT", [P, KV, NS], F32, free_k[9]),
                       at("sKIH", [P, P], F32R, free_k[9] + 512), at("sKIL", [P, P], F32R, free_k[9] + 1024))
    sQI = at("sQI", [P, IH, NS], F32R, free_k[10])
    sWR = at("sWR", [P, NSEQ, IH, NNEW], F32, free_k[11])
    sV = at("sV", [NS, KV * HD], F32, rV + 4096)
    sSEL = [at("sSEL0", [NS, 2, P], F32, rV + 5120), at("sSEL1", [NS, 2, P], F32, rV + 11136)]
    sHS = at("sHS", [P, KC, NSEQ, 2], F32, rV + 6144)
    sUK = at("sUK", [P, KC, NSEQ, 2], F32, rV + 6656)
    sT = [at(f"sT{i}", [P, NS], F32, rV + 7168 + 256 * i) for i in range(5)]
    sU = at("sU", [P, NSEQ, NNEW + 2], F32, rV + 8448)
    sYT = [at(f"sYT{i}", [P, NS], F32, rV + 8832 + 256 * i) for i in range(2)]
    sKO = at("sKO", [NS, KV * HD], F32, rV + 9344)
    sKIO = at("sKIO", [NS, ID], F32, rV + 10368)
    sQT = at("sQT", [P, NS], F32, rV + 10624)
    sW8 = at("sW8", [IH, NS], F32, rV + 10880)
    sCO = at("sCO", [2 * NSEQ, D], F32, rM + 8192)
    CO = at("CO", [2, D], F32, rM + 12288)
    sSQ = [at(f"sSQ{i}", [P, NS], F32, rV + 13184 + 256 * i) for i in range(2)]
    sRS = [at(f"sRS{i}", [P, NS], F32, rV + 13696 + 256 * i) for i in range(2)]
    sAS = at("sAS", [P, 8, NS], F32, rV + 14208)
    sRAW = at("sRAW", [P, 2, P], F32, rV + 12160)
    PAIR = at("PAIR", [P, NS], F32, free_k[9] + 1536)
    sXN = at("sXN", [NS, D], F32, rM)
    sYO = at("sYO", [NS, D], F32, rM)
    SC0 = at("SC0", [P, BLOCKS, TILE], F32, rS)
    sST = at("sST", [P, RUN + 1, NS], F32, rS + 8192)
    sSC = at("sSC", [NS, PAST + NS], F32, rS + 8192 + 4352)
    sBX = at("sBX", [P, PAST + NS], F32, rS + 8192 + 4352 + 8448)
    sKR = [at(f"sKR{i}", [P, RUN, ID], F32, rS + 8192 + 4352 + 8448 + 4096 * i) for i in range(2)]
    sKX = [at(f"sKX{i}", [P, RUN, P], F32, rB + 8192 * i) for i in range(2)]
    sKPH = [at(f"sKPH{i}", [P, TILE], F32R, rB + 16384 + 4096 * i) for i in range(2)]
    sKPL = [at(f"sKPL{i}", [P, TILE], F32R, rB + 18432 + 4096 * i) for i in range(2)]
    sPG = [at(f"sPG{i}", [P, RUN, KV * HD], F32, a) for i, a in enumerate((rH, rH + 16384, rW))]
    sKPT = at("sKPT", [P, PAST], F32, rW + 16384)
    sL = at("sL", [P, PAST + NS], F32, rM)
    sPT = at("sPT", [P, RUN, P], F32, rT)
    sPTN = at("sPTN", [NS, P], F32, rT + 8192)
    sXR = at("sXR", [NS, D], F32, rM + 4096)
    ROWS = at("ROWS", [58, P], F32, rT)
    C9 = at("C9", [9, D], F32, rM + 4096)
    ST16 = at("ST16", [2 * NSEQ, D], F32, rM + 8192)
    SCT = at("SCT", [P, KC, 9], F32, rM + 12288)
    TABLE = own("TABLE", [P, NSEQ], I32)
    PIECE = own("PIECE", [P, 1], I32)
    TABLEF = own("TABLEF", [P, NSEQ])
    PIECEF = own("PIECEF", [P, 1])
    ROW = own("ROW", [P, NSEQ], U32)
    ps = [ctx.enter_context(nc.psum_tensor(f"ps{i}", [P, TILE], F32)) for i in range(8)]
    rows_in = signal("rows_in", 16)
    mw_in = [signal(f"mw_in{i}", 16) for i in range(8)]
    x_in, xs_in = signal("x_in", 16), signal("xs_in", 16)
    biased, conv_t, conv_store, constants_v, xs_mod = (
        signal(n) for n in ("biased", "conv_t", "conv_store", "constants_v", "xs_mod"))
    abs_values = plan.setdefault("abs_values", {})
    PAIRS = range(NSEQ // 2)
    PAGE_USES = [(what, 2 * u + e) for u in PAIRS for what in "kv" for e in range(2)]
    page_slot = lambda *use: PAGE_USES.index(use) % 3
    KEY_GROUPS = [(e, kv, c) for e in range(2) for kv in range(KV) for c in range(4)]
    first_row = lambda e, kv: 64 * e + 32 * kv
    by_slot = lambda row: row.rearrange("t (q i) -> t i q", i=RUN)
    AFTER_PAGES = range(len(PROJ_A) + len(PROJ_B), len(PROJ_A) + len(PROJ_B) + 3)
    w_in_ = [signal(f"w_in{i}", 16) for i in range(3)]
    q_in = [signal(f"q_in{i}", 16) for i in range(2)]
    ma_in = [signal(f"ma_in{i}", 16) for i in range(2)]
    xr_in = [signal(f"xr_in{i}", 16) for i in range(2)]
    table_in, table_row, piece, kx_dup = signal("table_in", 16), signal("table_row"), signal("piece"), signal("kx_dup")
    kx_in = [signal(f"kx_in{i}", 16) for i in range(2)]
    pg_in = [signal(f"pg_in{i}", 16) for i in range(3)]
    q_out = [signal(f"q_out{i}", 16) for i in range(2)]
    ma_out = [signal(f"ma_out{i}", 16) for i in range(2)]
    y_out = [signal(f"y_out{i}", 16) for i in range(2)]
    k_out, ki_out, v_out, s_out = (signal(n, 16) for n in ("k_out", "ki_out", "v_out", "s_out"))
    constants = signal("constants")
    dve_step, pool_step, act_step = signal("dve_step"), signal("pool_step"), signal("act_step")
    silu_c, prep_t, prep_c = signal("silu_c"), signal("prep_t"), signal("prep_c")
    mod_mm, mod_ready = signal("mod_mm"), signal("mod_ready")
    sumsq, var, root_x, rstd, xnorm = (signal(n) for n in ("sumsq", "var", "root_x", "rstd", "xnorm"))
    x_t, x_mod, h_high, h_ready = (signal(n) for n in ("x_t", "x_mod", "h_high", "h_ready"))
    w_high, w_split = signal("w_high"), signal("w_split")
    product, evac = signal("product"), signal("evac")
    s_parts, s_parts_copy = signal("s_parts"), signal("s_parts_copy")
    aux_done, root, kt_ready, w8_ready, a_done = (
        signal(n) for n in ("aux_done", "root", "kt_ready", "w8_ready", "a_done"))
    idx_done, relu, scored, causal, mask = (signal(n) for n in ("idx_done", "relu", "scored", "causal", "mask"))
    kx_t, kx_high, kx_split, s_idx, s_sum, s_score_t = (
        signal(n) for n in ("kx_t", "kx_high", "kx_split", "s_idx", "s_sum", "s_score_t"))
    u_ready, taps, conv, ba_high, ba_ready, gate_mul = (
        signal(n) for n in ("u_ready", "taps", "conv", "ba_high", "ba_ready", "gate_mul"))
    qk, logits, row_max, expd, diag, p_t, p_copy, p_copy_a, pv, rb, rb_copy, attn, attn_z = (
        signal(n) for n in ("qk", "logits", "row_max", "expd", "diag", "p_t", "p_copy", "p_copy_a", "pv", "rb",
                            "rb_copy", "attn", "attn_z"))
    bb_high, bb_ready = signal("bb_high"), signal("bb_ready")
    merged, mg_high, mg_ready = signal("merged"), signal("mg_high"), signal("mg_ready")
    gated, y_t, y_sum = signal("gated"), signal("y_t"), signal("y_sum")
    s_bx, s_bx_copy, s_kt, s_kt_copy, s_qk, s_logits, s_exp, s_pt, s_pt_copy, s_dg, s_pv, s_rb, s_attn, s_attn_z = (
        signal(n) for n in ("s_bx", "s_bx_copy", "s_kt", "s_kt_copy", "s_qk", "s_logits", "s_exp", "s_pt",
                            "s_pt_copy", "s_dg", "s_pv", "s_rb", "s_attn", "s_attn_z"))

    q_scratch = nc.dram_tensor("q_scratch", [TILES, P, HEADS, TILE], F32).ap()
    ma_scratch = nc.dram_tensor("ma_scratch", [TILES, KC, P, TILE], F32).ap()

    def width(i):
        return (i + 1) * P

    def pieces(w):
        return [(c, min(TILE, w - c)) for c in range(0, w, TILE)]

    def weights(t, n, f):
        if n in ("pa", "pb", "wo"):
            src, col = ins[{"pa": "w_proj_a", "pb": "w_proj_b", "wo": "w_out"}[n]], f * P
        else:
            src, col = ins["w_in"], OFFSET[n] + f * P
        return src[0].rearrange("(k p) n -> p k n", p=P)[:, :, col:col + P]

    UNITS = [(b, pr) for b in range(BLOCKS) for pr in range(HEADS // 2)]
    PT_USES = [(t, u, c) for t in range(TILES) for u, (b, pr) in enumerate(UNITS) for c in range((BLOCKS * t + b + 2) // 2)]
    PT_NUMBER = {use: n for n, use in enumerate(PT_USES)}
    p_use = lambda *use: PT_NUMBER[use]
    p_slot = lambda *use: PT_NUMBER[use] % 3
    on_act = lambda c: c < ACT_COPIES
    p_copied = lambda t, u, c: (p_copy_a if on_act(c) else p_copy).at(t, u, c)

    def p_free(engine, t, u, c):
        before = p_use(t, u, c) - 3
        if before >= 0 and PT_USES[before][0] == t:
            engine.wait_ge(*pv.at(*PT_USES[before]))

    scores = lambda t: SC0 if t == 0 else SC
    index_blocks = lambda t: [b for b in range(BLOCKS) if width(BLOCKS * t + b) > TOPK]
    NORMED = [i for i, (n, f) in enumerate(PROJ_A) if n in ("k", "q")]
    s3 = lambda ap: ap.rearrange("p (s t) -> p s t", s=NSEQ)
    last_part = lambda t: parts(t)[-1]

    block = ctx.enter_context(nc.Block())

    @block.sync
    def _(sp):
        def load_w(j):
            if j >= len(GEMMS):
                return
            if j >= 3:
                sp.wait_ge(*product.at(j - 3, last_part(GEMMS[j - 3][0])))
            sp.dma_start(WR[j % 3][:, :, :], weights(*GEMMS[j])).then_inc(*w_in_[j % 3].mark(j))

        def load_mw(f):
            if f >= 8:
                sp.wait_ge(*mod_mm.at(f - 8))
            sp.dma_start(MW[f % 8][:, :, :], ins["w_mod"][0].rearrange("(k p) n -> p k n", p=P)[:, :, f * P:f * P + P]
                         ).then_inc(*mw_in[f % 8].mark(f))

        def load_x(t):
            if t:
                sp.wait_ge(*attn_z.at(t - 1, UNITS[-1]))
            sp.dma_start(XN[:, :, :], ins["x_prompt"][0, t * TILE:(t + 1) * TILE].rearrange("(b p) d -> p b d", p=P)
                         ).then_inc(*x_in.mark(t, "P"))
            if t == 0:
                sp.dma_start(sXN[:, :], ins["x_sample"].rearrange("s t d -> (s t) d")).then_inc(*x_in.mark(t, "S"))

        def row(name):
            a = ins[name]
            return a.rearrange("a (k p) -> (a k) p", p=P)

        for a, n, src in ((0, 8, row("norm_g")), (8, 24, row("b_mod")),
                          (32, 24, ins["conv_w"][0].rearrange("w (k p) -> (w k) p", p=P)),
                          (56, 1, ins["q_norm"]), (57, 1, ins["k_norm"])):
            sp.dma_start(ROWS[a:a + n, :], src).then_inc(*rows_in.mark(a))
        sp.dma_start(C9[0:1, :], ins["c_prompt"]).then_inc(*rows_in.mark("c0"))
        sp.dma_start(C9[1:9, :], ins["c_sample"]).then_inc(*rows_in.mark("c1"))
        sp.dma_start(ST16[:, :], ins["state_conv"][0].rearrange("s w d -> (s w) d")).then_inc(*rows_in.mark("all"))
        for f in range(8):
            load_mw(f)
        load_x(0)
        for s in range(NSEQ):
            sp.dma_start(TABLE[:, s:s + 1], ins["page_table"][s].unsqueeze(1).to_broadcast([NPAGES, PER_PAGE]).unsqueeze(2),
                         allow_slow_non_contiguous=True).then_inc(*table_in.mark(s))
        for f in range(8, 16):
            load_mw(f)
        for j in range(3):
            load_w(j)
        for f in range(16, 24):
            load_mw(f)

        def store_a(t, i):
            n, f = PROJ_A[i]
            r = slice(t * TILE, (t + 1) * TILE)
            if n == "ki":
                sp.wait_ge(*a_done.at(t, i, "P"))
                sp.dma_start(outs["kidx_prompt"][0, 0, r].rearrange("(b p) d -> p b d", p=P), KIO[:, :, :]
                             ).then_inc(*ki_out.mark(t))
            if n == "k":
                sp.wait_ge(*a_done.at(t, i, "P"))
                sp.dma_start(outs["k_prompt"][0, 0, r, f].rearrange("(b p) d -> p b d", p=P), KO[:, :, :]
                             ).then_inc(*k_out.mark(t, f))
            if n == "v":
                sp.wait_ge(*a_done.at(t, i, "P"))
                sp.dma_start(outs["v_prompt"][0, 0, r, f].rearrange("(b p) d -> p b d", p=P),
                             V[:, BLOCKS * t:BLOCKS * (t + 1), f * HD:(f + 1) * HD]).then_inc(*v_out.mark(t, f))
            if n == "q":
                sp.wait_ge(*a_done.at(t, i, "P"))
                sp.dma_start(q_scratch[t, :, f], QO[f % 2][:, :]).then_inc(*q_out[f % 2].mark(t, f))
            if t == 0 and n in ("k", "v") and f == 1:
                sp.wait_ge(*a_done.at(t, i, "S"))
                name, src = ("k_sample", sKO) if n == "k" else ("v_sample", sV)
                sp.dma_start(outs[name][0].rearrange("s t h d -> (s t) (h d)"), src[:, :]).then_inc(*s_out.mark(n))
            if t == 0 and n == "ki":
                sp.wait_ge(*a_done.at(t, i, "S"))
                sp.dma_start(outs["kidx_sample"][0].rearrange("s t d -> (s t) d"), sKIO[:, :]).then_inc(*s_out.mark(n))

        def store_y(t, f):
            sp.wait_ge(*y_sum.at(t, f, "P"))
            sp.dma_start(outs["y_prompt"][0, t * TILE:(t + 1) * TILE, f * P:(f + 1) * P].rearrange("(b p) d -> p b d", p=P),
                         YO[f % 2][:, :, :]).then_inc(*y_out[f % 2].mark(t, f))

        for t in range(TILES):
            first = t * (len(GEMMS) // TILES)
            for i in range(len(PROJ_A)):
                load_w(first + i + 3)
                if i >= 3:
                    store_a(t, i - 3)
            for i in range(len(PROJ_A) - 3, len(PROJ_A)):
                store_a(t, i)
            for i in range(len(PROJ_B)):
                j = first + len(PROJ_A) + i
                if j + 3 not in AFTER_PAGES:
                    load_w(j + 3)
                n, f = GEMMS[j - 2][1:]
                if n == "pa":
                    sp.wait_ge(*gate_mul.at(t, f, "P"))
                    sp.dma_start(ma_scratch[t, f], T[3 + f % 2][:, :]).then_inc(*ma_out[f % 2].mark(t, f))
            if t == 0:
                sp.wait_ge(*s_rb.at(PAIRS[-1]))
                for j in AFTER_PAGES:
                    load_w(j)
            for u, (b, pr) in enumerate(UNITS):
                if u >= 2:
                    sp.wait_ge(*qk.at(t, u - 2))
                elif u == 0:
                    sp.wait_ge(*gate_mul.at(t, KC - 1, "P"))
                    sp.wait_ge(*ma_out[0].at(t, KC - 2))
                    sp.wait_ge(*q_out[0].at(t, 6))
                    sp.wait_ge(*q_out[1].at(t, 7))
                    if t == 0:
                        sp.wait_ge(*s_attn.at(PAIRS[-1]))
                sp.dma_start(QL[u % 2][:, :, :], q_scratch[t, :, 2 * pr:2 * pr + 2, b * P:(b + 1) * P]
                             ).then_inc(*q_in[u % 2].mark(t, u))
            if t + 1 < TILES:
                load_x(t + 1)
            j = first + len(PROJ_A) + len(PROJ_B)
            for f in range(KC):
                if f >= 2:
                    sp.wait_ge(*merged.at(t, f - 2, "P"))
                else:
                    sp.wait_ge(*pv.at(t, len(UNITS) - 1))
                    sp.wait_ge(*ma_out[f].at(t, KC - 2 + f))
                sp.dma_start(T[1 + f % 2][:, :], ma_scratch[t, f]).then_inc(*ma_in[f % 2].mark(t, f))
                load_w(j + f + 3)
            for f in range(KC):
                if f >= 2:
                    sp.wait_ge(*y_sum.at(t, f - 2, "P"))
                else:
                    sp.wait_ge(*merged.at(t, KC - 1, "P"))
                sp.dma_start(XR[f % 2][:, :, :], ins["x_prompt"][0, t * TILE:(t + 1) * TILE, f * P:(f + 1) * P]
                             .rearrange("(b p) d -> p b d", p=P)).then_inc(*xr_in[f % 2].mark(t, f))
                if t == 0 and f == 0:
                    sp.wait_ge(*bb_ready.at(t, KC - 1, "P"))
                    sp.dma_start(sXR[:, :], ins["x_sample"].rearrange("s t d -> (s t) d")).then_inc(*xs_in.mark())
                load_w(j + KC + f + 3)
                if f >= 2:
                    store_y(t, f - 2)
            for f in range(KC - 2, KC):
                store_y(t, f)
            if t == 0:
                sp.wait_ge(*y_sum.at(t, KC - 1, "S"))
                sp.dma_start(outs["y_sample"].rearrange("s t d -> (s t) d"), sYO[:, :]).then_inc(*s_out.mark("y"))
                sp.wait_ge(*conv_store.at("S"))
                sp.dma_start(outs["conv_sample"][0].rearrange("s w d -> (s w) d"), sCO[:, :]).then_inc(*s_out.mark("conv"))
        sp.wait_ge(*conv_store.at("P"))
        sp.dma_start(outs["conv_prompt"][0, 0], CO[:, :]).then_inc(*s_out.mark("last"))
        for sig in (*q_out, *ma_out, *y_out, k_out, ki_out, v_out, s_out):
            sp.wait_ge(*sig.end())


    @block.scalar
    def _(act):
        def link(ins_):
            ins_.then_inc(*act_step.mark(act_step.n))
            act.wait_ge(act_step.sem, act_step.n)

        def split_high(j):
            if j < len(GEMMS):
                act.wait_ge(*w_in_[j % 3].at(j))
                act.activation(WH[j % 3][:, :, :], WR[j % 3][:, :, :], ACT.Copy).then_inc(*w_high.mark(j))

        act.wait_ge(*rows_in.at("all"))
        act.activation(C9[:, :], C9[:, :], ACT.Silu).then_inc(*silu_c.mark())

        def norm(t):
            act.wait_ge(*x_in.at(t, last_part(t)))
            for b in range(BLOCKS - 1):
                link(act.activation(JUNK[:, 0:D], XN[:, b, :], ACT.Square, accum_out=SS[:, b:b + 1]))
            b = BLOCKS - 1
            act.activation(JUNK[:, 0:D], XN[:, b, :], ACT.Square, accum_out=SS[:, b:b + 1]).then_inc(*sumsq.mark(t, "P"))
            if t == 0:
                act.wait_ge(*sumsq.at(t, "P"))
                act.activation(JUNK[0:NS, 0:D], sXN[:, :], ACT.Square, accum_out=NEED[0:NS, 0:1]).then_inc(*sumsq.mark(t, "S"))
            for p in parts(t):
                v, r, n = (SV, RT, P) if p == "P" else (NEED[:, 1:2], NEED[:, 2:3], NS)
                act.wait_ge(*var.at(t, p))
                act.activation(r[0:n], v[0:n], ACT.Sqrt).then_inc(*root_x.mark(t, p))

        def modulate(t):
            if t == 0:
                act.wait_ge(*mod_ready.at("AM"))
            for k in range(KC):
                act.wait_ge(*x_t.at(t, k))
                if k >= 2:
                    act.wait_ge(*h_ready.at(t, k - 2, "P"))
                elif t:
                    act.wait_ge(*mg_ready.at(t - 1, KC - 2 + k, "P"))
                act.activation(T[3 + k % 2][:, :], ps[bank("x_t", t, k)][:, :], ACT.Identity,
                               bias=MOD[:, k, 0:1], scale=AM[:, k, 0:1]).then_inc(*x_mod.mark(t, k))

        def parts_out(t, j):
            if t == 0:
                act.wait_ge(*s_parts.at(j))
                act.activation(sRAW[:, :, :].rearrange("p l c -> p (l c)"), ps[bank("parts", j)][:, 0:2 * P], ACT.Copy
                               ).then_inc(*s_parts_copy.mark(j))

        def evac_a(t, i, j):
            parts_out(t, j)
            n, f = PROJ_A[i]
            for p in parts(t):
                m = TILE if p == "P" else NS
                dst = (AS if p == "P" else sAS)[:, i % 8, :]
                act.wait_ge(*product.at(j, p))
                if i >= 8:
                    act.wait_ge(*a_done.at(t, i - 8, p))
                elif t and i == 0:
                    for f_ in range(2):
                        act.wait_ge(*y_out[f_].at(t - 1, KC - 2 + f_))
                src = ps[PBANK[j, p]][:, 0:m]
                if i in NORMED:
                    act.activation(dst, src, ACT.Copy)
                    q = NORMED.index(i)
                    if q >= 2:
                        act.wait_ge(*aux_done.at(t, NORMED[q - 2], p))
                    sq = (SQ if p == "P" else sSQ)[q % 2][:, :]
                    act.activation(sq, src, ACT.Square).then_inc(*evac.mark(j, p))
                else:
                    act.activation(dst, src, ACT.Copy).then_inc(*evac.mark(j, p))

        def root_a(t, i):
            if i not in NORMED:
                return
            q = NORMED.index(i)
            for p in parts(t):
                act.wait_ge(*aux_done.at(t, i, p))
                if q >= 2:
                    act.wait_ge(*a_done.at(t, NORMED[q - 2], p))
                m = TILE if p == "P" else NS
                rs = (RS if p == "P" else sRS)[q % 2][:, :]
                act.activation(rs, ps[bank("aux", t, i, p)][:, 0:m], ACT.Sqrt, bias=EPSC, scale=1.0 / HD
                               ).then_inc(*root.mark(t, i, p))

        relus = [0]

        def index_relu(t):
            act.wait_ge(*a_done.at(t, len(PROJ_A) - 1, last_part(t)))
            for b in index_blocks(t):
                for h in range(IH):
                    for c, n in pieces(width(BLOCKS * t + b)):
                        r = relus[0]
                        relus[0] += 1
                        act.wait_ge(*idx_done.at(t, b, h, c))
                        if r >= 4:
                            act.wait_ge(*scored.at(r - 4))
                        act.activation(T[1 + r % 4][:, 0:n], ps[bank("idx", t, b, h, c)][:, 0:n], ACT.Relu
                                       ).then_inc(*relu.mark(r))

        def conv_taps(f):
            for p in parts(t):
                act.wait_ge(*u_ready.at(t, f, p))
                for w in (2, 1, 0):
                    if w == 0:
                        if f:
                            act.wait_ge(*ba_ready.at(t, f - 1, p))
                    if p == "P":
                        src, dst = U[:, w:w + TILE], (T[0], T[2], T[1])[w][:, :]
                    else:
                        src, dst = sU[:, :, w:w + NNEW], s3((sT[0], sT[2], sT[1])[w][:, :])
                    ins_ = act.activation(dst, src, ACT.Copy, scale=COL[:, 32 + 8 * w + f:33 + 8 * w + f])
                ins_.then_inc(*taps.mark(t, f, p))

        def branch_high(f):
            for p in parts(t):
                act.wait_ge(*conv.at(t, f, p))
                if f == 0 and p == "P":
                    act.wait_ge(*q_out[0].at(t, HEADS - 2))
                    act.wait_ge(*q_out[1].at(t, HEADS - 1))
                    act.wait_ge(*k_out.at(t, 1))
                    act.wait_ge(*ki_out.at(t))
                    act.wait_ge(*a_done.at(t, len(PROJ_A) - 1, last_part(t)))
                if p == "P":
                    act.activation(BAH[:, f, :], T[0][:, :], ACT.Copy).then_inc(*ba_high.mark(t, f, p))
                else:
                    act.activation(sBAH[:, f, :], sT[0][:, :], ACT.Copy).then_inc(*ba_high.mark(t, f, p))

        def evac_b(t, i, j):
            parts_out(t, j)
            n, f = PROJ_B[i]
            for p in parts(t):
                m = TILE if p == "P" else NS
                src = ps[PBANK[j, p]][:, 0:m]
                act.wait_ge(*product.at(j, p))
                tt = T if p == "P" else sT
                func = ACT.Copy
                if n == "uh":
                    if f:
                        act.wait_ge(*conv.at(t, f - 1, p))
                    elif p == "P":
                        act.wait_ge(*scored.at(relus[0] - 1)) if relus[0] else None
                    dst = tt[1][:, :]
                elif n == "uc":
                    dst = tt[2][:, :]
                elif n == "ub":
                    dst = tt[3][:, :]
                elif n == "za":
                    dst, func = tt[4][:, :], ACT.Silu
                elif n == "ga":
                    if f >= 2:
                        act.wait_ge(*gate_mul.at(t, f - 2, p))
                    else:
                        act.wait_ge(*ba_ready.at(t, KC - 1, p))
                    dst, func = tt[1 + f % 2][:, :], ACT.Sigmoid
                elif n == "pa":
                    if f >= 2 and p == "P":
                        act.wait_ge(*ma_out[f % 2].at(t, f - 2))
                    dst = tt[3 + f % 2][:, :]
                elif n == "zb":
                    dst, func = (SZB if p == "P" else sSZB)[:, f, :], ACT.Silu
                else:
                    dst, func = (GB if p == "P" else sGB)[:, f, :], ACT.Sigmoid
                act.activation(dst, src, func).then_inc(*evac.mark(j, p))

        def duplicate(s):
            if s == 0:
                act.wait_ge(*q_out[0].at(0, HEADS - 2))
                act.wait_ge(*q_out[1].at(0, HEADS - 1))
                act.wait_ge(*k_out.at(0, 1))
                act.wait_ge(*ki_out.at(0))
                act.wait_ge(*a_done.at(0, len(PROJ_A) - 1, "S"))
            if s < NSEQ:
                act.wait_ge(*kx_in[s % 2].at(s))
                if s >= 2:
                    act.wait_ge(*kx_t.at(s - 2, 3))
                act.activation(sKX[s % 2][:, :, :].rearrange("p i (c d) -> p i c d", c=2),
                               sKR[s % 2][:, :, :].unsqueeze(2).to_broadcast([P, RUN, 2, ID]), ACT.Copy).then_inc(*kx_dup.mark(s))

        def sample_keys():
            duplicate(0)
            for s in range(NSEQ):
                duplicate(s + 1)
                for c in range(4):
                    n = 4 * s + c
                    act.wait_ge(*kx_t.at(s, c))
                    if n >= 2:
                        act.wait_ge(*s_idx.at((n - 2) // 4, (n - 2) % 4))
                    act.activation(sKPH[n % 2][:, :], ps[bank("kx", s, c)][:, :], ACT.Copy).then_inc(*kx_high.mark(s, c))

        def sample_scores_out():
            for c in range(5):
                act.wait_ge(*s_score_t.at(c))
                src = ps[bank("sst", c)][0:NS, :]
                if c < 4:
                    ins_ = act.activation(by_slot(sSC[:, 0:PAST])[:, 4 * c:4 * c + 4, :], src.rearrange("t (i q) -> t i q", i=4), ACT.Copy)
                else:
                    ins_ = act.activation(sSC[:, PAST:PAST + NS], src[:, 0:NS], ACT.Copy)
                ins_.then_inc(*s_bx_copy.mark("sc", c))

        def masks(t):
            for b in index_blocks(t):
                act.wait_ge(*mask.at(t, b))
                row = scores(t)[:, b, 0:width(BLOCKS * t + b)]
                act.activation(row, row, ACT.Copy, scale=-NEG).then_inc(*biased.mark(t, b))
            if t == 0:
                act.wait_ge(*mask.at(t, "S"))
                act.activation(sSC[:, :], sSC[:, :], ACT.Copy, scale=-NEG).then_inc(*biased.mark(t, "S"))

        def sample_attention():
            for u in PAIRS:
                for c in range(5):
                    n = TILE if c < 4 else NS
                    act.wait_ge(*s_bx.at(u, c))
                    if u:
                        act.wait_ge(*s_logits.at(u - 1))
                    act.activation(sBX[:, c * TILE:c * TILE + n], ps[c][:, 0:n], ACT.Copy).then_inc(*s_bx_copy.mark(u, c))
                for m, (e, kv, c) in enumerate(KEY_GROUPS):
                    act.wait_ge(*s_kt.at(u, m))
                    if m >= 4:
                        act.wait_ge(*s_qk.at(u, m - 4))
                    elif u:
                        act.wait_ge(*s_qk.at(u - 1, 12 + m))
                    act.activation(sKPT[:, c * TILE:(c + 1) * TILE], ps[5 + m % 2][:, :], ACT.Copy).then_inc(*s_kt_copy.mark(u, m))
                act.wait_ge(*s_logits.at(u))
                act.activation(sL[:, :], sL[:, :], ACT.Exp, bias=NM[:, 0, 0:1], accum_out=SUM[:, 0, 0:1]).then_inc(*s_exp.mark(u))
                for c in range(5):
                    act.wait_ge(*s_pt.at(u, c))
                    if c < 4:
                        ins_ = act.activation(sPT[:, 4 * c:4 * c + 4, :], ps[5 + c % 2][:, :].rearrange("p (a b) -> p a b", a=4), ACT.Copy)
                    else:
                        ins_ = act.activation(sPTN[:, :], ps[5][0:NS, 0:P], ACT.Copy)
                    ins_.then_inc(*s_pt_copy.mark(u, c))
                act.wait_ge(*s_rb.at(u))
                act.activation(RB[0][:, 0:P], ps[7][:, P:2 * P], ACT.Copy).then_inc(*rb_copy.mark("S", u))

        def attend(t):
            for u in range(len(UNITS) + 1):
                if u < len(UNITS):
                    w = width(BLOCKS * t + UNITS[u][0])
                    for hh in range(2):
                        act.wait_ge(*row_max.at(t, u, hh))
                        row = LP[:, u % 2, hh, 0:w]
                        ins_ = act.activation(row, row, ACT.Exp, bias=NM[:, u % 2, hh:hh + 1],
                                              accum_out=SUM[:, u % 2, hh:hh + 1])
                        ins_.then_inc(*expd.mark(t, u, hh))
                if u >= 1:
                    v = u - 1
                    act.wait_ge(*rb.at(t, v))
                    if v >= 2:
                        act.wait_ge(*attn.at(t, v - 2))
                    act.activation(RB[v % 2][:, :], ps[6 + v % 2][:, 256:512], ACT.Copy).then_inc(*rb_copy.mark(t, v))
                if u < len(UNITS):
                    n = BLOCKS * t + UNITS[u][0] + 1
                    for c in range((n + 1) // 2):
                        if on_act(c):
                            act.wait_ge(*p_t.at(t, u, c))
                            if u == 0 and c == 0:
                                act.wait_ge(*ma_out[0].at(t, KC - 2))
                                act.wait_ge(*ma_out[1].at(t, KC - 1))
                            p_free(act, t, u, c)
                            m = 256 * min(2, n - 2 * c)
                            act.activation(T[p_slot(t, u, c)][:, 0:m], ps[bank("tr", t, u, c)][:, 0:m], ACT.Copy
                                           ).then_inc(*p_copy_a.mark(t, u, c))

        def attn_high(t):
            act.wait_ge(*pv.at(t, len(UNITS) - 1))
            for p in parts(t):
                act.wait_ge(*(attn_z.at(t, UNITS[-1]) if p == "P" else s_attn_z.at()))
            for k in range(KC):
                act.activation(BBH[:, k, :], BB[:, k, :], ACT.Copy).then_inc(*bb_high.mark(t, k, "P"))
                if t == 0:
                    act.activation(sBBH[:, k, :], sBB[:, k, :], ACT.Copy).then_inc(*bb_high.mark(t, k, "S"))

        def evac_c(t, n, f, j):
            parts_out(t, j)
            for p in parts(t):
                m = TILE if p == "P" else NS
                src = ps[PBANK[j, p]][:, 0:m]
                act.wait_ge(*product.at(j, p))
                if n == "pb":
                    if f >= 2:
                        act.wait_ge(*mg_ready.at(t, f - 2, p))
                    act.activation((T if p == "P" else sT)[3 + f % 2][:, :], src, ACT.Copy).then_inc(*evac.mark(j, p))
                elif p == "P":
                    if f >= 2:
                        act.wait_ge(*y_t.at(t, f - 2, p))
                    act.activation(T[1 + f % 2][:, :], src, ACT.Copy, scale=MOD[:, 16 + f, 0:1]).then_inc(*evac.mark(j, p))
                else:
                    if f >= 2:
                        act.wait_ge(*y_t.at(t, f - 2, p))
                    act.activation(sYT[f % 2][:, :], src, ACT.Copy).then_inc(*evac.mark(j, p))

        norm(0)
        split_high(0)
        split_high(1)
        modulate(0)
        for t in range(TILES):
            j = len(GEMMS) // TILES * t
            for i in range(len(PROJ_A)):
                split_high(j + 2)
                evac_a(t, i, j)
                if i:
                    root_a(t, i - 1)
                j += 1
            root_a(t, len(PROJ_A) - 1)
            index_relu(t)
            if t == 0:
                sample_keys()
                sample_scores_out()
            for i in range(len(PROJ_B)):
                if j + 2 not in AFTER_PAGES:
                    split_high(j + 2)
                n, f = PROJ_B[i]
                evac_b(t, i, j)
                if n == "ub":
                    conv_taps(f)
                if n == "uh" and f:
                    branch_high(f - 1)
                if n == "za" and f == KC - 1:
                    branch_high(f)
                j += 1
            masks(t)
            if t == 0:
                sample_attention()
                split_high(AFTER_PAGES[0])
                split_high(AFTER_PAGES[1])
            attend(t)
            attn_high(t)
            for f in range(KC):
                split_high(j + 2)
                evac_c(t, "pb", f, j)
                if f == 4 and t + 1 < TILES:
                    norm(t + 1)
                j += 1
            if t + 1 < TILES:
                modulate(t + 1)
            for f in range(KC):
                split_high(j + 2)
                evac_c(t, "wo", f, j)
                j += 1
            if t == 0:
                act.wait_ge(*conv_t.at("S"))
                for h in range(2):
                    ins_ = act.activation(sCO[:, h * TILE:(h + 1) * TILE], ps[bank("conv", "S", h)][0:2 * NSEQ, :], ACT.Copy)
                ins_.then_inc(*conv_store.mark("S"))
        act.wait_ge(*conv_t.at("P"))
        for h in range(2):
            ins_ = act.activation(CO[:, h * TILE:(h + 1) * TILE], ps[bank("conv", "P", h)][0:2, :], ACT.Copy)
        ins_.then_inc(*conv_store.mark("P"))

    @block.tensor
    def _(pe):
        freed = {}
        count = [0]

        def claim(b):
            if b in freed:
                pe.wait_ge(*freed.pop(b))

        def aux(*key):
            b = 4 + count[0] % 4
            count[0] += 1
            banks[key] = b
            claim(b)
            return b

        def mm(out, lhsT, rhs, start=True, stop=True, **more):
            return pe.matmul(out, lhsT, rhs, start=start, stop=stop, **more)

        def turn(out, in_):
            n = in_.shape[0]
            a = in_.base_partition() if callable(in_.base_partition) else in_.base_partition
            return pe.transpose(out, in_, ident[a:a + n, a:a + n])

        pe.wait_ge(*constants.at("all"))
        pe.wait_ge(*rows_in.at("all"))
        turn(ps[4][:, 0:58], ROWS[:, :]).then_inc(*prep_t.mark("rows"))
        for k in range(KC):
            ins_ = turn(ps[6][:, 16 * k:16 * k + 16], ST16[:, k * P:(k + 1) * P])
        ins_.then_inc(*prep_t.mark("state"))
        pe.wait_ge(*silu_c.at())
        for k in range(KC):
            ins_ = turn(ps[5][:, 9 * k:9 * k + 9], C9[:, k * P:(k + 1) * P])
        ins_.then_inc(*prep_t.mark("c"))
        pe.wait_ge(*prep_c.at("c"))

        def modulation(fs):
            for f in fs:
                pe.wait_ge(*mw_in[f % 8].at(f))
                for k in range(KC):
                    ins_ = mm(ps[7 if f < 16 else 3][:, 9 * f:9 * f + 9], MW[f % 8][:, k, :], SCT[:, k, :], k == 0, k == KC - 1)
                ins_.then_inc(*mod_mm.mark(f))

        modulation(range(16))
        freed[4] = prep_c.at("rows")
        freed[5] = prep_c.at("c")
        freed[6] = prep_c.at("state")
        freed[7] = mod_ready.at("AM")

        def turn_x(t):
            pe.wait_ge(*xnorm.at(t, last_part(t)))
            for k in range(KC):
                b = aux("x_t", t, k)
                for blk in range(BLOCKS):
                    ins_ = turn(ps[b][:, blk * P:(blk + 1) * P], XN[:, blk, k * P:(k + 1) * P])
                ins_.then_inc(*x_t.mark(t, k))
                freed[b] = x_mod.at(t, k)
            if t == 0:
                b = aux("x_t", t, "S")
                for k in range(KC):
                    ins_ = turn(ps[b][:, k * NS:(k + 1) * NS], sXN[:, k * P:(k + 1) * P])
                ins_.then_inc(*x_t.mark(t, "S"))
                freed[b] = xs_mod.at()

        def products(j):
            t, n, f = GEMMS[j]
            pe.wait_ge(*w_split.at(j))
            if t == 0:
                operand = {"pa": sBA, "pb": sBB2, "wo": sMG}.get(n, sHT)
                b = aux("parts", j)
                for k in range(KC):
                    if (n, f) == PROJ_A[0]:
                        pe.wait_ge(*h_ready.at(t, "S"))
                    elif f == 0 and n in ("pa", "pb", "wo"):
                        pe.wait_ge(*{"pa": ba_ready, "pb": bb_ready, "wo": mg_ready}[n].at(t, k, "S"))
                    ins_ = mm(ps[b][:, 0:2 * P], operand[:, k, :], WLH[j % 3][:, :, k, :], k == 0, k == KC - 1)
                ins_.then_inc(*s_parts.mark(j))
                freed[b] = s_parts_copy.at(j)
            hi, lo = {"pa": (BAH, BAL), "pb": (BBH, BBL), "wo": (MGH, MGL)}.get(n, (HTH, HTL))
            b = PBANK[j, "P"]
            claim(b)
            for k in range(KC):
                if (n, f) == PROJ_A[0]:
                    pe.wait_ge(*h_ready.at(t, k, "P"))
                elif f == 0 and n in ("pa", "pb", "wo"):
                    pe.wait_ge(*{"pa": ba_ready, "pb": bb_ready, "wo": mg_ready}[n].at(t, k, "P"))
                out = ps[b][:, :]
                mm(out, WH[j % 3][:, k, :], hi[:, k, :], k == 0, False)
                mm(out, WH[j % 3][:, k, :], lo[:, k, :], False, False)
                ins_ = mm(out, WL[j % 3][:, k, :], hi[:, k, :], False, k == KC - 1)
            ins_.then_inc(*product.mark(j, "P"))
            freed[b] = evac.at(j, "P")
            if t == 0:
                pe.wait_ge(*s_parts_copy.at(j))
                b = PBANK[j, "S"]
                claim(b)
                mm(ps[b][:, 0:NS], sRAW[:, 0, :], PAIR[:, :], True, False)
                mm(ps[b][:, 0:NS], sRAW[:, 1, :], PAIR[:, :], False, True).then_inc(*product.mark(j, "S"))
                freed[b] = evac.at(j, "S")

        def after_a(t, i, j):
            n, f = PROJ_A[i]
            for p in parts(t):
                m, blocks = (TILE, BLOCKS) if p == "P" else (NS, 1)
                src = (AS if p == "P" else sAS)[:, i % 8, :]
                rows = m // blocks
                pe.wait_ge(*evac.at(j, p))
                if i in NORMED:
                    b = aux("aux", t, i, p)
                    q = NORMED.index(i)
                    mm(ps[b][:, 0:m], ones[:, :], (SQ if p == "P" else sSQ)[q % 2][:, :]).then_inc(*aux_done.mark(t, i, p))
                    freed[b] = root.at(t, i, p)
                elif n == "v":
                    b = aux("aux", t, i, p)
                    for blk in range(blocks):
                        ins_ = turn(ps[b][0:rows, blk * P:(blk + 1) * P], src[:, blk * rows:(blk + 1) * rows])
                    ins_.then_inc(*aux_done.mark(t, i, p))
                    freed[b] = a_done.at(t, i, p)
                elif n == "ki":
                    b = aux("aux", t, i, p)
                    for blk in range(blocks):
                        turn(ps[b][0:rows, blk * ID:(blk + 1) * ID], src[0:ID, blk * rows:(blk + 1) * rows])
                    if p == "P":
                        for blk in range(BLOCKS):
                            ins_ = turn(ps[b][:, 256 + 8 * blk:264 + 8 * blk], src[ID:ID + IH, blk * P:(blk + 1) * P])
                        ins_.then_inc(*aux_done.mark(t, i, p))
                        freed[b] = a_done.at(t, i, p)
                    else:
                        pe.wait_ge(*w8_ready.at(t, p))
                        b2 = aux("w_rows", t)
                        for h in range(IH):
                            ins_ = mm(ps[b2][:, h * NS:(h + 1) * NS], ident[0:IH, h:h + 1].to_broadcast([IH, P]), sW8[:, 0:NS])
                        ins_.then_inc(*aux_done.mark(t, i, p))
                        freed[b] = a_done.at(t, i, p)
                        freed[b2] = a_done.at(t, i, p)

        def turn_keys(t, i):
            n, f = PROJ_A[i]
            if n != "k":
                return
            for p in parts(t):
                pe.wait_ge(*kt_ready.at(t, f, p))
                b = aux("kT", t, f, p)
                blocks, rows = (BLOCKS, P) if p == "P" else (1, NS)
                for blk in range(blocks):
                    src = KT[:, f, t * TILE + blk * P:t * TILE + (blk + 1) * P] if p == "P" else sKT[:, f, :]
                    ins_ = turn(ps[b][0:rows, blk * P:(blk + 1) * P], src)
                ins_.then_inc(*aux_done.mark(t, "kT", f, p))
                freed[b] = a_done.at(t, i, p)

        def index(t):
            for blk in index_blocks(t):
                for h in range(IH):
                    if h % 2 == 0:
                        pe.wait_ge(*a_done.at(t, PROJ_A.index(("qi", h // 2)), "P"))
                    for c, n in pieces(width(BLOCKS * t + blk)):
                        b = aux("idx", t, blk, h, c)
                        q = QI[:, h, blk * P:(blk + 1) * P]
                        mm(ps[b][:, 0:n], q, KIH[:, c:c + n], True, False)
                        mm(ps[b][:, 0:n], q, KIL[:, c:c + n], False, True).then_inc(*idx_done.mark(t, blk, h, c))
                        freed[b] = relu.at(relus[0])
                        relus[0] += 1

        relus = [0]

        def sample_index():
            for s in range(NSEQ):
                pe.wait_ge(*kx_dup.at(s))
                for c in range(4):
                    b = aux("kx", s, c)
                    for pg in range(4):
                        ins_ = turn(ps[b][:, pg * P:(pg + 1) * P], sKX[s % 2][:, 4 * c + pg, :])
                    ins_.then_inc(*kx_t.mark(s, c))
                    freed[b] = kx_split.at(s, c)
                    if c:
                        sample_logits(s, c - 1)
                sample_logits(s, 3)
            b = aux("snew")
            mm(ps[b][:, :], sKIH[:, :], sQI[:, :, :].rearrange("p h t -> p (h t)"), True, False)
            mm(ps[b][:, :], sKIL[:, :], sQI[:, :, :].rearrange("p h t -> p (h t)"), False, True).then_inc(*s_idx.mark("new"))
            freed[b] = s_sum.at("new")
            for c in range(5):
                b = aux("sst", c)
                pe.wait_ge(*s_sum.at("new"))
                for pg in range(4 if c < 4 else 1):
                    if c < 4:
                        ins_ = turn(ps[b][0:NS, pg * P:(pg + 1) * P], sST[:, 4 * c + pg, :])
                    else:
                        ins_ = turn(ps[b][0:NS, 0:NS], sST[0:NS, NPAGES, :])
                ins_.then_inc(*s_score_t.mark(c))
                freed[b] = s_bx_copy.at("sc", c)

        def sample_logits(s, c):
            n = 4 * s + c
            pe.wait_ge(*kx_split.at(s, c))
            b = aux("sidx", s, c)
            for pg in range(4):
                out = ps[b][:, pg * NS:(pg + 1) * NS]
                q = sQI[:, :, s * NNEW:(s + 1) * NNEW]
                mm(out, sKPH[n % 2][:, pg * P:(pg + 1) * P], q, True, False)
                ins_ = mm(out, sKPL[n % 2][:, pg * P:(pg + 1) * P], q, False, True)
            ins_.then_inc(*s_idx.mark(s, c))
            freed[b] = s_sum.at(s, c)

        def sample_attention():
            for u in PAIRS:
                for c in range(5):
                    n = TILE if c < 4 else NS
                    pe.wait_ge(*biased.at(0, "S"))
                    claim(c)
                    rows = by_slot(sSC[:, 0:PAST])[:, 4 * c:4 * c + 4, :] if c < 4 else sSC[:, PAST:PAST + NS]
                    mm(ps[c][:, 0:n], sSEL[u // 2][:, u % 2, :], rows).then_inc(*s_bx.mark(u, c))
                    freed[c] = s_bx_copy.at(u, c)

                def turn_page(m):
                    e, kv, c = KEY_GROUPS[m]
                    slot = page_slot("k", 2 * u + e)
                    pe.wait_ge(*pg_in[slot].at("k", 2 * u + e))
                    b = 5 + m % 2
                    claim(b)
                    for i in range(4):
                        ins_ = turn(ps[b][:, i * P:(i + 1) * P], sPG[slot][:, 4 * c + i, kv * HD:(kv + 1) * HD])
                    ins_.then_inc(*s_kt.mark(u, m))
                    freed[b] = s_kt_copy.at(u, m)

                turn_page(0)
                for c in range(5):
                    claim(c)
                for m, (e, kv, c) in enumerate(KEY_GROUPS):
                    if m + 1 < len(KEY_GROUPS):
                        turn_page(m + 1)
                    pe.wait_ge(*s_kt_copy.at(u, m))
                    r = first_row(e, kv)
                    q = sQ[:, 2 * u + e, 4 * kv:4 * kv + 4, :].rearrange("p h t -> p (h t)")
                    mm(ps[c][r:r + 32, :], q, sKPT[:, c * TILE:(c + 1) * TILE]).then_inc(*s_qk.mark(u, m))
                    if c == 3:
                        ins_ = mm(ps[4][r:r + 32, 0:NS], q, sKT[:, kv, :])
                ins_.then_inc(*s_qk.mark(u, "new"))
                for c in range(5):
                    freed[c] = s_logits.at(u)
                pe.wait_ge(*s_exp.at(u))
                for c in range(5):
                    b = 5 + c % 2
                    claim(b)
                    if c < 4:
                        for i in range(4):
                            ins_ = turn(ps[b][:, i * P:(i + 1) * P], sL[:, (4 * c + i) * P:(4 * c + i + 1) * P])
                    else:
                        ins_ = turn(ps[b][0:NS, 0:P], sL[:, PAST:PAST + NS])
                    ins_.then_inc(*s_pt.mark(u, c))
                    freed[b] = s_pt_copy.at(u, c)
                claim(7)
                pe.wait_ge(*s_pt_copy.at(u, 4))
                for e in range(2):
                    for kv in range(KV):
                        r = first_row(e, kv)
                        mm(ps[7][:, r:r + 32], sV[:, kv * HD:(kv + 1) * HD], sPTN[:, r:r + 32], True, True, skip_group_check=True)
                    slot = page_slot("v", 2 * u + e)
                    pe.wait_ge(*pg_in[slot].at("v", 2 * u + e))
                    for kv in range(KV):
                        r = first_row(e, kv)
                        for i in range(RUN):
                            ins_ = mm(ps[7][:, r:r + 32], sPG[slot][:, i, kv * HD:(kv + 1) * HD], sPT[:, i, r:r + 32],
                                      False, True, skip_group_check=True)
                    ins_.then_inc(*s_pv.mark(u, e))
                pe.wait_ge(*s_dg.at(u))
                mm(ps[7][:, P:2 * P], ones[:, :], DG[0][:, 0:P], skip_group_check=True).then_inc(*s_rb.mark(u))
                freed[7] = s_attn.at(u)

        ring = {"qk": 0, "tr": 0}

        def head_logits(t, u):
            blk, pr = UNITS[u]
            pe.wait_ge(*q_in[u % 2].at(t, u))
            for hh in range(2):
                for c, n in pieces(width(BLOCKS * t + blk)):
                    b = ring["qk"] % 3
                    ring["qk"] += 1
                    banks["qk", t, u, hh, c] = b
                    claim(b)
                    ins_ = mm(ps[b][:, 0:n], QL[u % 2][:, hh, :], KT[:, pr // 2, c:c + n])
                    ins_.then_inc(*qk.mark(t, u, hh, c))
                    freed[b] = logits.at(t, u, hh, c)
            qk.values[t, u] = qk.n

        def head_values(t, u):
            blk, pr = UNITS[u]
            n = BLOCKS * t + blk + 1
            acc = 6 + u % 2

            def turn_p(c):
                b = 3 + ring["tr"] % 3
                ring["tr"] += 1
                banks["tr", t, u, c] = b
                claim(b)
                for kk in range(min(2, n - 2 * c)):
                    for hh in range(2):
                        k = 2 * c + kk
                        ins_ = turn(ps[b][:, (2 * kk + hh) * P:(2 * kk + hh + 1) * P], LP[:, u % 2, hh, k * P:(k + 1) * P])
                ins_.then_inc(*p_t.mark(t, u, c))
                freed[b] = p_copied(t, u, c)

            groups = (n + 1) // 2
            for hh in range(2):
                pe.wait_ge(*expd.at(t, u, hh))
            turn_p(0)
            for c in range(groups):
                if c + 1 < groups:
                    turn_p(c + 1)
                pe.wait_ge(*p_copied(t, u, c))
                if c == 0:
                    claim(acc)
                for kk in range(min(2, n - 2 * c)):
                    k = 2 * c + kk
                    ins_ = mm(ps[acc][:, 0:256], V[:, k, (pr // 2) * HD:(pr // 2 + 1) * HD],
                              T[p_slot(t, u, c)][:, kk * 256:(kk + 1) * 256], k == 0, k == n - 1)
                ins_.then_inc(*pv.mark(t, u, c))
            pv.values[t, u] = pv.n
            pe.wait_ge(*diag.at(t, u))
            mm(ps[acc][:, 256:512], ones[:, :], DG[u % 2][:, :]).then_inc(*rb.mark(t, u))
            freed[acc] = attn.at(t, u)

        def turn_y(t, f, j):
            for p in parts(t):
                b = aux("y", t, f, p)
                if p == "P":
                    pe.wait_ge(*evac.at(j, p))
                    for blk in range(BLOCKS):
                        ins_ = turn(ps[b][:, blk * P:(blk + 1) * P], T[1 + f % 2][:, blk * P:(blk + 1) * P])
                else:
                    pe.wait_ge(*gated.at(f))
                    ins_ = turn(ps[b][0:NS, 0:P], sYT[f % 2][:, :])
                ins_.then_inc(*y_t.mark(t, f, p))
                freed[b] = y_sum.at(t, f, p)

        turn_x(0)
        modulation(range(16, 24))
        freed[3] = mod_ready.at("gate")
        for t in range(TILES):
            j = len(GEMMS) // TILES * t
            for i in range(len(PROJ_A)):
                products(j)
                if i:
                    after_a(t, i - 1, j - 1)
                if i >= 2:
                    turn_keys(t, i - 2)
                j += 1
            after_a(t, len(PROJ_A) - 1, j - 1)
            index(t)
            if t == 0:
                sample_index()
            for i in range(len(PROJ_B)):
                products(j)
                j += 1
            if t == 0:
                sample_attention()
            head_logits(t, 0)
            for u in range(len(UNITS)):
                if u + 1 < len(UNITS):
                    head_logits(t, u + 1)
                head_values(t, u)
            for f in range(KC):
                products(j)
                j += 1
            if t + 1 < TILES:
                turn_x(t + 1)
            for f in range(KC):
                products(j)
                if f:
                    turn_y(t, f - 1, j - 1)
                j += 1
            turn_y(t, KC - 1, j - 1)
            if t in (0, TILES - 1):
                p, src, n = ("S", sUK[:, :, :, :].rearrange("p k s w -> p k (s w)"), 16) if t == 0 else ("P", HALO[:, :, :], 2)
                for h in range(2):
                    b = aux("conv", p, h)
                    for k in range(4):
                        ins_ = turn(ps[b][0:n, k * P:(k + 1) * P], src[:, 4 * h + k, :])
                    freed[b] = conv_store.at(p)
                ins_.then_inc(*conv_t.mark(p))

    @block.vector
    def _(dve):
        def link(ins_):
            ins_.then_inc(*dve_step.mark(dve_step.n))
            dve.wait_ge(dve_step.sem, dve_step.n)

        dve.wait_ge(*prep_t.at("rows"))
        link(dve.tensor_copy(COL[:, :], ps[4][:, 0:58]))
        dve.tensor_scalar(COL[:, 56:57], COL[:, 56:57], float(HD) ** -0.5, None, ALU.mult).then_inc(*prep_c.mark("rows"))
        dve.wait_ge(*prep_t.at("state"))
        dve.tensor_copy(sHS[:, :, :, :].rearrange("p k s w -> p (k s w)"), ps[6][:, 0:128]).then_inc(*prep_c.mark("state"))
        dve.wait_ge(*prep_t.at("c"))
        dve.tensor_copy(SCT[:, :, :].rearrange("p k c -> p (k c)"), ps[5][:, 0:72]).then_inc(*prep_c.mark("c"))
        dve.memset(HALO[:, :, :], 0.0).then_inc(*constants_v.mark("halo"))
        dve.wait_ge(*constants.at("all"))
        for e in range(2):
            ins_ = dve.tensor_copy(PAIR[e * NS:(e + 1) * NS, :], ident[e * NS:(e + 1) * NS, e * NS:(e + 1) * NS])
        for u in PAIRS:
            tokens = ident[0:NS, 2 * u * NNEW:2 * (u + 1) * NNEW].rearrange("p (s t) -> p s t", s=2)
            ins_ = dve.tensor_copy(sSEL[u // 2][:, u % 2, :].rearrange("p (s h t) -> p s h t", s=2, h=HEADS),
                                   tokens.unsqueeze(2).to_broadcast([NS, 2, HEADS, NNEW]))
        ins_.then_inc(*constants_v.mark("sel"))
        dve.wait_ge(*piece.at())
        dve.wait_ge(*table_in.at(NSEQ - 1))
        dve.tensor_copy(TABLEF[:, :], TABLE[:, :])
        link(dve.tensor_scalar(PIECE[:, :], PIECE[:, :], PER_PAGE - 1, None, ALU.bitwise_and))
        link(dve.tensor_copy(PIECEF[:, :], PIECE[:, :]))
        link(dve.tensor_scalar(TABLEF[:, :], TABLEF[:, :], float(PER_PAGE), PIECEF[:, 0:1], ALU.mult, ALU.add))
        dve.tensor_copy(ROW[:, :], TABLEF[:, :]).then_inc(*table_row.mark())

        def norm(t):
            for p in parts(t):
                if p == "P":
                    s, v, rt, r1, r2, n = SS, SV, RT, R1, R2, P
                else:
                    s, v, rt, r1, r2, n = NEED[:, 0:1], NEED[:, 1:2], NEED[:, 2:3], NEED[:, 3:4], NEED[:, 4:5], NS
                s, v, rt, r1, r2 = s[0:n], v[0:n], rt[0:n], r1[0:n], r2[0:n]
                dve.wait_ge(*sumsq.at(t, p))
                dve.tensor_scalar(v, s, 1.0 / D, EPS, ALU.mult, ALU.add).then_inc(*var.mark(t, p))
                dve.wait_ge(*root_x.at(t, p))
                link(dve.reciprocal(r1, rt))
                link(dve.tensor_tensor(r2, r1, r1, ALU.mult))
                link(dve.tensor_tensor(r2, r2, v, ALU.mult))
                link(dve.tensor_scalar(r2, r2, -0.5, 1.5, ALU.mult, ALU.add))
                link(dve.tensor_tensor(r1, r1, r2, ALU.mult))
                if p == "P":
                    for b in range(BLOCKS):
                        ins_ = dve.tensor_scalar(XN[:, b, :], XN[:, b, :], r1[:, b:b + 1], None, ALU.mult)
                else:
                    ins_ = dve.tensor_scalar(sXN[:, :], sXN[:, :], r1, None, ALU.mult)
                ins_.then_inc(*xnorm.mark(t, p))

        def modulation_ready():
            dve.wait_ge(*mod_mm.at(15))
            link(dve.tensor_tensor(MOD[:, 0:16, :], ps[7][:, 0:144].rearrange("p (f c) -> p f c", c=9),
                                   COL[:, 8:24].unsqueeze(2).to_broadcast([P, 16, 9]), ALU.add))
            link(dve.tensor_scalar(AM[:, :, :], MOD[:, 8:16, :], 1.0, None, ALU.add))
            dve.tensor_tensor(AM[:, :, :], AM[:, :, :], COL[:, 0:8].unsqueeze(2).to_broadcast([P, 8, 9]), ALU.mult
                              ).then_inc(*mod_ready.mark("AM"))

        def modulate(t):
            for k in range(KC):
                dve.wait_ge(*x_mod.at(t, k))
                if t and k == 0:
                    dve.wait_ge(*product.at(len(GEMMS) // TILES * t - KC - 1, last_part(t - 1)))
                dve.tensor_copy(HTH[:, k, :], T[3 + k % 2][:, :]).then_inc(*h_high.mark(t, k, "P"))
            if t == 0:
                dve.wait_ge(*x_t.at(t, "S"))
                v4 = lambda ap: ap.rearrange("p (k s t) -> p k s t", k=KC, s=NSEQ)
                tmp = v4(T[0][:, :])
                bc = lambda ap: ap[:, :, 1:9].unsqueeze(3).to_broadcast([P, KC, NSEQ, NNEW])
                link(dve.tensor_tensor(tmp, v4(ps[bank("x_t", t, "S")][:, :]), bc(AM), ALU.mult))
                dve.tensor_tensor(tmp, tmp, bc(MOD[:, 0:8, :]), ALU.add).then_inc(*xs_mod.mark())
                dve.wait_ge(*xs_mod.at())
                dve.tensor_copy(sHTH[:, :, :], T[0][:, :].rearrange("p (k t) -> p k t", k=KC)).then_inc(*h_high.mark(t, "S"))

        def item_a(t, i, j):
            n, f = PROJ_A[i]
            for p in parts(t):
                prompt = p == "P"
                m, blocks = (TILE, BLOCKS) if prompt else (NS, 1)
                rows = m // blocks
                src = (AS if prompt else sAS)[:, i % 8, :]
                if n == "ki":
                    dve.wait_ge(*evac.at(j, p))
                    hi, lo = (KIH, KIL) if prompt else (sKIH, sKIL)
                    cols = [slice(t * TILE, (t + 1) * TILE)] if prompt else [slice(0, NS), slice(NS, 2 * NS)]
                    if not prompt:
                        dve.tensor_copy(sW8[:, :], src[ID:ID + IH, :]).then_inc(*w8_ready.mark(t, p))
                    for c in cols:
                        dve.tensor_copy(hi[ID:2 * ID, c], src[0:ID, :])
                        link(dve.tensor_copy(hi[0:ID, c], src[0:ID, :]))
                        dve.tensor_tensor(lo[0:ID, c], src[0:ID, :], hi[0:ID, c].bitcast(F32), ALU.subtract)
                        link(dve.tensor_tensor(lo[ID:2 * ID, c], src[0:ID, :], hi[0:ID, c].bitcast(F32), ALU.subtract))
                    dve.wait_ge(*aux_done.at(t, i, p))
                    b = bank("aux", t, i, p)
                    if prompt:
                        if t:
                            dve.wait_ge(*ki_out.at(t - 1))
                        dve.tensor_copy(KIO[:, :, :].rearrange("p b d -> p (b d)"), ps[b][:, 0:256])
                        ins_ = dve.tensor_scalar(WI[:, :, :].rearrange("p b h -> p (b h)"), ps[b][:, 256:288],
                                                 float(np.float32(float(IH) ** -0.5)) * float(ID) ** -0.5, None, ALU.mult)
                    else:
                        dve.tensor_copy(sKIO[:, :], ps[b][0:NS, 0:ID])
                        ins_ = dve.tensor_scalar(sWR[:, :, :, :].rearrange("p s h t -> p h s t"),
                                                 ps[bank("w_rows", t)][:, :].rearrange("p (h s t) -> p h s t", h=IH, s=NSEQ),
                                                 float(np.float32(float(IH) ** -0.5)) * float(ID) ** -0.5, None, ALU.mult)
                    ins_.then_inc(*a_done.mark(t, i, p))
                elif i in NORMED:
                    dve.wait_ge(*root.at(t, i, p))
                    rs = (RS if prompt else sRS)[NORMED.index(i) % 2][:, :]
                    link(dve.reciprocal(rs, rs))
                    col = COL[:, 57:58] if n == "k" else COL[:, 56:57]
                    if n == "k":
                        dst = KT[:, f, t * TILE:(t + 1) * TILE] if prompt else sKT[:, f, :]
                    else:
                        if prompt and (t or f >= 2):
                            dve.wait_ge(*(q_out[f % 2].at(t, f - 2) if f >= 2 else q_out[f % 2].at(t - 1, HEADS - 2 + f)))
                        dst = QO[f % 2][:, :] if prompt else sQT[:, :]
                    ins_ = dve.scalar_tensor_tensor(dst, src, col, rs, ALU.mult, ALU.mult)
                    if n == "k":
                        ins_.then_inc(*kt_ready.mark(t, f, p))
                        dve.wait_ge(*aux_done.at(t, "kT", f, p))
                        b = bank("kT", t, f, p)
                        if prompt:
                            if f:
                                dve.wait_ge(*k_out.at(t, f - 1))
                            elif t:
                                dve.wait_ge(*k_out.at(t - 1, 1))
                            dve.tensor_copy(KO[:, :, :].rearrange("p b d -> p (b d)"), ps[b][:, :]).then_inc(*a_done.mark(t, i, p))
                        else:
                            dve.tensor_copy(sKO[:, f * HD:(f + 1) * HD], ps[b][0:NS, 0:HD]).then_inc(*a_done.mark(t, i, p))
                    elif prompt:
                        ins_.then_inc(*a_done.mark(t, i, p))
                    else:
                        link(ins_)
                        dve.tensor_copy(sQ[:, :, f, :], s3(sQT[:, :])).then_inc(*a_done.mark(t, i, p))
                elif n == "v":
                    dve.wait_ge(*aux_done.at(t, i, p))
                    b = bank("aux", t, i, p)
                    if prompt:
                        ins_ = dve.tensor_copy(V[:, BLOCKS * t:BLOCKS * (t + 1), f * HD:(f + 1) * HD],
                                               ps[b][:, :].rearrange("p (b d) -> p b d", b=BLOCKS))
                    else:
                        ins_ = dve.tensor_copy(sV[:, f * HD:(f + 1) * HD], ps[b][0:NS, 0:HD])
                    ins_.then_inc(*a_done.mark(t, i, p))
                else:
                    dve.wait_ge(*evac.at(j, p))
                    hi = (T[1] if prompt else sT[1])[:, 0:m]
                    q = QI if prompt else sQI
                    if f:
                        dve.wait_ge(*a_done.at(t, i - 1, p))
                    link(dve.tensor_copy(hi.bitcast(F32R), src))
                    for e in range(2):
                        half = slice(e * ID, (e + 1) * ID)
                        dve.tensor_copy(q[0:ID, 2 * f + e, :], src[half])
                        ins_ = dve.tensor_tensor(q[ID:2 * ID, 2 * f + e, :], src[half], hi[half], ALU.subtract)
                    ins_.then_inc(*a_done.mark(t, i, p))

        relus = [0]

        def weigh(t):
            for blk in index_blocks(t):
                runs = pieces(width(BLOCKS * t + blk))
                for h in range(IH):
                    for c, n in runs:
                        r = relus[0]
                        relus[0] += 1
                        dve.wait_ge(*relu.at(r))
                        dst = scores(t)[:, blk, c:c + n]
                        x = T[1 + r % 4][:, 0:n]
                        w = WI[:, blk, h:h + 1]
                        if h == 0:
                            dve.tensor_scalar(dst, x, w, None, ALU.mult).then_inc(*scored.mark(r))
                        else:
                            dve.wait_ge(*scored.at(r - len(runs)))
                            dve.scalar_tensor_tensor(dst, x, w, dst, ALU.mult, ALU.add).then_inc(*scored.mark(r))

        def sample_index():
            def weigh_pages(s, c):
                n = 4 * s + c
                dve.wait_ge(*s_idx.at(s, c))
                rl = T[1 + n % 4][:, 0:4 * NS]
                link(dve.scalar_tensor_tensor(
                    rl.rearrange("p (g x) -> p g x", g=4), ps[bank("sidx", s, c)][:, 0:4 * NS].rearrange("p (g x) -> p g x", g=4), 0.0,
                    sWR[:, s, :, :].rearrange("p h t -> p (h t)").unsqueeze(1).to_broadcast([P, 4, NS]), ALU.max, ALU.mult))
                dve.tensor_reduce(sST[:, 4 * c:4 * c + 4, s * NNEW:(s + 1) * NNEW],
                                  rl.rearrange("p (g h t) -> p g t h", g=4, h=IH), AX_X, ALU.add).then_inc(*s_sum.mark(s, c))

            for s in range(NSEQ):
                for c in range(4):
                    n = 4 * s + c
                    dve.wait_ge(*kx_high.at(s, c))
                    dve.tensor_tensor(sKPL[n % 2][:, :], ps[bank("kx", s, c)][:, :], sKPH[n % 2][:, :].bitcast(F32), ALU.subtract
                                      ).then_inc(*kx_split.mark(s, c))
                    if c:
                        weigh_pages(s, c - 1)
                weigh_pages(s, 3)
            dve.wait_ge(*s_idx.at("new"))
            v4 = lambda ap: ap.rearrange("p (h s t) -> p h s t", h=IH, s=NSEQ)
            link(dve.tensor_scalar(T[1][:, :], ps[bank("snew")][:, :], 0.0, None, ALU.max))
            link(dve.tensor_tensor(v4(T[1][:, :]), v4(T[1][:, :]), sWR[:, :, :, :].rearrange("p s h t -> p h s t"), ALU.mult))
            dve.tensor_reduce(sST[0:NS, NPAGES, :], T[1][0:NS, :].rearrange("p (h t) -> p t h", h=IH), AX_X, ALU.add
                              ).then_inc(*s_sum.mark("new"))

        def select(t):
            rows = [(scores(t)[:, b, 0:width(BLOCKS * t + b)], P, b, b) for b in index_blocks(t)]
            if t == 0:
                rows.append((sSC[:, :], NS, 4, "S"))
            k = len(rows)
            c0 = rows[0][2]
            cs = slice(c0, rows[-1][2] + 1)
            if t == 0:
                link(dve.memset(ABS[:, :], 1.0))
                link(dve.memset(CNT[:, :], 0.0))
                dve.wait_ge(*s_bx_copy.at("sc", 4))
            dve.wait_ge(*scored.at(relus[0] - 1))
            for row, n, c, name in rows:
                ins_ = dve.tensor_reduce(ABS[0:n, c:c + 1], row, AX_X, ALU.max, apply_absolute_value=True)
                ins_.then_inc(*dve_step.mark(dve_step.n))
                abs_values[t, name] = dve_step.n
            dve.wait_ge(dve_step.sem, dve_step.n)
            link(dve.tensor_scalar(HI[:, cs], ABS[:, cs], 1.0 + 2.0 ** -20, 1e-25, ALU.mult, ALU.add))
            link(dve.tensor_scalar(LO[:, cs], HI[:, cs], -1.0, None, ALU.mult))
            link(dve.memset(MID[:, cs], 0.0))
            dve.wait_ge(*causal.at(t))
            for step in range(STEPS):
                for row, n, c, name in rows:
                    link(dve.tensor_scalar(JUNK[0:n, 0:row.shape[1]], row, MID[0:n, c:c + 1], 0.0, ALU.is_ge, ALU.add,
                                           accum_out=CNT[0:n, c:c + 1]))
                dve.tensor_scalar(GE[:, cs], CNT[:, cs], float(TOPK), None, ALU.is_ge)
                link(dve.tensor_scalar(LT[:, cs], CNT[:, cs], float(TOPK), None, ALU.is_lt))
                dve.copy_predicated(LO[:, cs], GE[:, cs], MID[:, cs])
                link(dve.copy_predicated(HI[:, cs], LT[:, cs], MID[:, cs]))
                link(dve.tensor_tensor(MID[:, cs], LO[:, cs], HI[:, cs], ALU.add))
                link(dve.tensor_scalar(MID[:, cs], MID[:, cs], 0.5, None, ALU.mult))
            for row, n, c, name in rows:
                hi, lo, need = HI[0:n, c:c + 1], LO[0:n, c:c + 1], NEED[0:n, c:c + 1]
                link(dve.tensor_scalar(JUNK[0:n, 0:row.shape[1]], row, hi, 0.0, ALU.is_ge, ALU.add, accum_out=CNT[0:n, c:c + 1]))
                link(dve.tensor_scalar(need, CNT[0:n, c:c + 1], -1.0, float(TOPK), ALU.mult, ALU.add))
                for a, m in pieces(row.shape[1]):
                    x, g, band, pre = row[:, a:a + m], GT[0:n, 0:m], BD[0:n, 0:m], PFX[0:n, 0:m]
                    if a:
                        link(dve.tensor_copy(CNT[0:n, c:c + 1], PFX[0:n, TILE - 1:TILE]))
                    link(dve.tensor_scalar(g, x, hi, None, ALU.is_ge))
                    link(dve.scalar_tensor_tensor(band, x, lo, g, ALU.is_ge, ALU.subtract))
                    link(dve.tensor_tensor_scan(pre, band, band, CNT[0:n, c:c + 1] if a else 0.0, ALU.add, ALU.bypass))
                    link(dve.scalar_tensor_tensor(band, pre, need, band, ALU.is_le, ALU.mult))
                    ins_ = dve.scalar_tensor_tensor(x, band, -1.0, g, ALU.add, ALU.add)
                ins_.then_inc(*mask.mark(t, name))

        def sample_attention():
            for u in PAIRS:
                dve.wait_ge(*s_bx_copy.at(u, 4))
                dve.wait_ge(*s_qk.at(u, "new"))
                if u:
                    dve.wait_ge(*s_pt.at(u - 1, 4))
                for c in range(5):
                    n = TILE if c < 4 else NS
                    ins_ = dve.tensor_tensor_reduce(sL[:, c * TILE:c * TILE + n], ps[c][:, 0:n], sBX[:, c * TILE:c * TILE + n],
                                                    1.0, -3e38, ALU.add, ALU.max, LO[:, c:c + 1])
                link(ins_)
                dve.tensor_reduce(NM[:, 0, 0:1], LO[:, 0:5], AX_X, ALU.max, negate=True).then_inc(*s_logits.mark(u))
                dve.wait_ge(*s_exp.at(u))
                link(dve.reciprocal(RIN[:, 0, 0:1], SUM[:, 0, 0:1]))
                if u:
                    dve.wait_ge(*s_rb.at(u - 1))
                dve.tensor_scalar(DG[0][:, 0:P], ident[:, :], RIN[:, 0, 0:1], None, ALU.mult).then_inc(*s_dg.mark(u))
                dve.wait_ge(*rb_copy.at("S", u))
                for kv in range(KV):
                    rows = lambda ap: ap.rearrange("p (s k g t) -> p s k g t", s=2, k=KV, g=4)[:, :, kv]
                    ins_ = dve.tensor_tensor(
                        sBB[:, 4 * kv:4 * kv + 4, 2 * u * NNEW:2 * (u + 1) * NNEW].rearrange("p g (s t) -> p s g t", s=2),
                        rows(ps[7][:, 0:P]), rows(RB[0][:, 0:P]), ALU.mult)
                ins_.then_inc(*s_attn.mark(u))

        def mask_logits(t, u):
            blk, pr = UNITS[u]
            runs = pieces(width(BLOCKS * t + blk))
            if u >= 2:
                dve.wait_ge(*pv.at(t, u - 2))
            for hh in range(2):
                for x, (c, n) in enumerate(runs):
                    dve.wait_ge(*qk.at(t, u, hh, c))
                    ins_ = dve.tensor_tensor_reduce(LP[:, u % 2, hh, c:c + n], ps[bank("qk", t, u, hh, c)][:, 0:n],
                                                    scores(t)[:, blk, c:c + n], 1.0, -3e38, ALU.add, ALU.max,
                                                    PM[:, u % 2, hh, x:x + 1])
                    ins_.then_inc(*logits.mark(t, u, hh, c))
                dve.wait_ge(*logits.at(t, u, hh, runs[-1][0]))
                dve.tensor_reduce(NM[:, u % 2, hh:hh + 1], PM[:, u % 2, hh, 0:len(runs)], AX_X, ALU.max, negate=True
                                  ).then_inc(*row_max.mark(t, u, hh))

        def finish(t, u):
            blk, pr = UNITS[u]
            dve.wait_ge(*rb_copy.at(t, u))
            dve.tensor_tensor(BB[:, 2 * pr:2 * pr + 2, blk * P:(blk + 1) * P],
                              ps[6 + u % 2][:, 0:256].rearrange("p (h q) -> p h q", h=2),
                              RB[u % 2][:, :].rearrange("p (h q) -> p h q", h=2), ALU.mult).then_inc(*attn.mark(t, u))

        def attend(t):
            dve.wait_ge(*gate_mul.at(t, KC - 1, "P"))
            dve.wait_ge(*biased.at(t, index_blocks(t)[-1]))
            dve.wait_ge(*product.at(len(GEMMS) // TILES * t + len(PROJ_A) + len(PROJ_B) - 1, last_part(t)))
            mask_logits(t, 0)
            for u in range(len(UNITS)):
                if u + 1 < len(UNITS):
                    mask_logits(t, u + 1)
                dve.wait_ge(*expd.at(t, u, 1))
                link(dve.reciprocal(RIN[:, u % 2, :], SUM[:, u % 2, :]))
                if u >= 2:
                    dve.wait_ge(*rb.at(t, u - 2))
                for hh in range(2):
                    ins_ = dve.tensor_scalar(DG[u % 2][:, hh * P:(hh + 1) * P], ident[:, :], RIN[:, u % 2, hh:hh + 1], None, ALU.mult)
                ins_.then_inc(*diag.mark(t, u))
                n = BLOCKS * t + UNITS[u][0] + 1
                for c in range((n + 1) // 2):
                    if on_act(c):
                        continue
                    dve.wait_ge(*p_t.at(t, u, c))
                    p_free(dve, t, u, c)
                    m = 256 * min(2, n - 2 * c)
                    dve.tensor_copy(T[p_slot(t, u, c)][:, 0:m], ps[bank("tr", t, u, c)][:, 0:m]).then_inc(*p_copy.mark(t, u, c))
                if u:
                    finish(t, u - 1)
            finish(t, len(UNITS) - 1)

        def merge(t, f, j):
            for p in parts(t):
                x = (T if p == "P" else sT)[3 + f % 2][:, :]
                gate = (GB if p == "P" else sGB)[:, f, :]
                dve.wait_ge(*evac.at(j, p))
                link(dve.tensor_tensor(x, x, gate, ALU.mult))
                if p == "P":
                    dve.wait_ge(*ma_in[f % 2].at(t, f))
                link(dve.tensor_tensor(x, x, T[1 + f % 2][:, :] if p == "P" else sMA[:, f, :], ALU.add))
                dve.tensor_copy((MGH if p == "P" else sMGH)[:, f, :], x).then_inc(*merged.mark(t, f, p))

        def residual(t, f):
            for p in parts(t):
                dve.wait_ge(*y_t.at(t, f, p))
                b = bank("y", t, f, p)
                if p == "P":
                    dve.wait_ge(*xr_in[f % 2].at(t, f))
                    if f >= 2:
                        dve.wait_ge(*y_out[f % 2].at(t, f - 2))
                    dve.tensor_tensor(YO[f % 2][:, :, :].rearrange("p b d -> p (b d)"), ps[b][:, :],
                                      XR[f % 2][:, :, :].rearrange("p b d -> p (b d)"), ALU.add).then_inc(*y_sum.mark(t, f, p))
                else:
                    dve.wait_ge(*xs_in.at())
                    dve.tensor_tensor(sYO[:, f * P:(f + 1) * P], ps[b][0:NS, 0:P], sXR[:, f * P:(f + 1) * P], ALU.add
                                      ).then_inc(*y_sum.mark(t, f, p))

        def gate_sample(f, j):
            dve.wait_ge(*evac.at(j, "S"))
            dve.tensor_tensor(s3(sYT[f % 2][:, :]), s3(sYT[f % 2][:, :]),
                              MOD[:, 16 + f, 1:9].unsqueeze(2).to_broadcast([P, NSEQ, NNEW]), ALU.mult).then_inc(*gated.mark(f))

        norm(0)
        modulation_ready()
        modulate(0)
        dve.wait_ge(*mod_mm.at(23))
        dve.tensor_tensor(MOD[:, 16:24, :], ps[3][:, 144:216].rearrange("p (f c) -> p f c", c=9),
                          COL[:, 24:32].unsqueeze(2).to_broadcast([P, 8, 9]), ALU.add).then_inc(*mod_ready.mark("gate"))
        for t in range(TILES):
            j = len(GEMMS) // TILES * t
            for i in range(len(PROJ_A)):
                item_a(t, i, j)
                j += 1
            weigh(t)
            if t == 0:
                sample_index()
            select(t)
            if t == 0:
                sample_attention()
            attend(t)
            j += len(PROJ_B)
            for f in range(KC):
                merge(t, f, j)
                if f == 4 and t + 1 < TILES:
                    norm(t + 1)
                j += 1
            if t + 1 < TILES:
                modulate(t + 1)
            for f in range(KC):
                if t == 0:
                    gate_sample(f, j)
                if f:
                    residual(t, f - 1)
                j += 1
            residual(t, KC - 1)

    @block.gpsimd
    def _(pool):
        def link(ins_):
            ins_.then_inc(*pool_step.mark(pool_step.n))
            pool.wait_ge(pool_step.sem, pool_step.n)

        link(pool.memset(ident[:, :], 0.0))
        pool.affine_select(out=ident[:, :], in_=ident[:, :], compare_op=ALU.not_equal, fill=1.0, base=0,
                           pattern=[[-1, P]], channel_multiplier=1).then_inc(*constants.mark("ident"))
        pool.memset(EPSC, EPS)
        pool.iota(PIECE[:, :], [[0, 1]], base=0, channel_multiplier=1).then_inc(*piece.mark())
        pool.memset(ones[:, :], 1.0).then_inc(*constants.mark("all"))

        def split_low(j):
            if j < len(GEMMS):
                pool.wait_ge(*w_high.at(j))
                pool.tensor_tensor(WL[j % 3][:, :, :], WR[j % 3][:, :, :], WH[j % 3][:, :, :].bitcast(F32), ALU.subtract
                                   ).then_inc(*w_split.mark(j))

        def gather(out, cache, s, sig):
            rows = cache.rearrange("n (c r) d -> (n c) (r d)", c=PER_PAGE)
            pool.indirect_dma_start(out, None, rows, bass.IndirectOffsetOnAxis(ap=ROW[:, s:s + 1], axis=0)).then_inc(*sig)

        def gather_index_keys(s):
            if s == 0:
                pool.wait_ge(*table_row.at())
                pool.wait_ge(*mod_mm.at(23))
            if s >= 2:
                pool.wait_ge(*kx_dup.at(s - 2))
            gather(sKR[s % 2][:, :, :].rearrange("p i d -> p (i d)"), ins["cache_kidx"][0], s, kx_in[s % 2].mark(s))

        def gather_pages(n):
            what, s = PAGE_USES[n]
            if n < 3:
                pool.wait_ge(*product.at(AFTER_PAGES[0] - 1, "S"))
            else:
                before, q = PAGE_USES[n - 3]
                pool.wait_ge(*(s_kt.at(q // 2, 8 * (q % 2) + 7) if before == "k" else s_pv.at(q // 2, q % 2)))
            gather(sPG[n % 3][:, :, :].rearrange("p i d -> p (i d)"), ins["cache_" + what][0].rearrange("n p h d -> n p (h d)"),
                   s, pg_in[n % 3].mark(what, s))

        def h_low(t):
            for k in range(KC):
                pool.wait_ge(*h_high.at(t, k, "P"))
                pool.tensor_tensor(HTL[:, k, :], T[3 + k % 2][:, :], HTH[:, k, :].bitcast(F32), ALU.subtract
                                   ).then_inc(*h_ready.mark(t, k, "P"))
            if t == 0:
                pool.wait_ge(*h_high.at(t, "S"))
                pool.tensor_tensor(sHTL[:, :, :], T[0][:, :].rearrange("p (k t) -> p k t", k=KC),
                                   sHTH[:, :, :].bitcast(F32), ALU.subtract).then_inc(*h_ready.mark(t, "S"))

        def fill_future(t):
            for b in range(BLOCKS):
                i = BLOCKS * t + b
                row = scores(t)[:, b, 0:width(i)]
                if b in index_blocks(t):
                    pool.wait_ge(dve_step.sem, abs_values[t, b] if known else 1)
                else:
                    link(pool.memset(row, 0.0))
                pool.affine_select(out=row[:, i * P:], in_=row[:, i * P:], compare_op=ALU.is_ge, fill=NEG, base=0,
                                   pattern=[[-1, P]], channel_multiplier=1).then_inc(*causal.mark(t, b))
            if t == 0:
                pool.wait_ge(dve_step.sem, abs_values[t, "S"] if known else 1)
                new = sSC[:, PAST:PAST + NS]
                v = new.rearrange("p (s t) -> p s t", s=NSEQ)
                link(pool.affine_select(out=new, in_=new, compare_op=ALU.is_ge, fill=NEG, base=0, pattern=[[-1, NS]],
                                        channel_multiplier=1))
                pool.affine_select(out=v, in_=v, compare_op=ALU.is_ge, fill=NEG, base=NNEW - 1, pattern=[[NNEW, NSEQ], [0, NNEW]],
                                   channel_multiplier=-1).then_inc(*causal.mark(t, "S"))
            causal.values[t,] = causal.n

        def conv_input(f, j):
            for p in parts(t):
                pool.wait_ge(*evac.at(j, p))
                if f:
                    pool.wait_ge(*taps.at(t, f - 1, p))
                if p == "P":
                    pool.tensor_copy(U[:, 0:2], HALO[:, f, :])
                    link(pool.tensor_tensor(U[:, 2:TILE + 2], T[2][:, :], T[1][:, :], ALU.mult))
                    pool.tensor_copy(HALO[:, f, :], U[:, TILE:TILE + 2]).then_inc(*u_ready.mark(t, f, p))
                else:
                    pool.tensor_copy(sU[:, :, 0:2], sHS[:, f, :, :])
                    link(pool.tensor_tensor(sU[:, :, 2:NNEW + 2], s3(sT[2][:, :]), s3(sT[1][:, :]), ALU.mult))
                    pool.tensor_copy(sUK[:, f, :, :], sU[:, :, NNEW:NNEW + 2]).then_inc(*u_ready.mark(t, f, p))

        def convolve(f, j):
            for p in parts(t):
                x = [a[:, :] for a in (T if p == "P" else sT)]
                pool.wait_ge(*taps.at(t, f, p))
                link(pool.tensor_tensor(x[0], x[0], x[2], ALU.add))
                link(pool.tensor_tensor(x[0], x[0], x[1], ALU.add))
                link(pool.tensor_tensor(x[0], x[0], x[3], ALU.mult))
                pool.wait_ge(*evac.at(j, p))
                pool.tensor_tensor(x[0], x[0], x[4], ALU.mult).then_inc(*conv.mark(t, f, p))

        def branch_low(f):
            for p in parts(t):
                pool.wait_ge(*ba_high.at(t, f, p))
                if p == "P":
                    pool.tensor_tensor(BAL[:, f, :], T[0][:, :], BAH[:, f, :].bitcast(F32), ALU.subtract).then_inc(*ba_ready.mark(t, f, p))
                else:
                    pool.tensor_tensor(sBAL[:, f, :], sT[0][:, :], sBAH[:, f, :].bitcast(F32), ALU.subtract
                                       ).then_inc(*ba_ready.mark(t, f, p))

        def gate_a(f, j):
            for p in parts(t):
                pool.wait_ge(*evac.at(j, p))
                tt = T if p == "P" else sT
                g, x = tt[1 + f % 2][:, :], tt[3 + f % 2][:, :]
                pool.tensor_tensor(x if p == "P" else sMA[:, f, :], x, g, ALU.mult).then_inc(*gate_mul.mark(t, f, p))

        def attn_gate(t):
            for u, (blk, pr) in enumerate(UNITS):
                pool.wait_ge(*attn.at(t, u))
                x = BB[:, 2 * pr:2 * pr + 2, blk * P:(blk + 1) * P]
                pool.tensor_tensor(x, x, SZB[:, 2 * pr:2 * pr + 2, blk * P:(blk + 1) * P], ALU.mult
                                   ).then_inc(*attn_z.mark(t, UNITS[u]))

        def attn_low(t):
            for k in range(KC):
                pool.wait_ge(*bb_high.at(t, k, "P"))
                pool.tensor_tensor(BBL[:, k, :], BB[:, k, :], BBH[:, k, :].bitcast(F32), ALU.subtract).then_inc(*bb_ready.mark(t, k, "P"))
                if t == 0:
                    pool.wait_ge(*bb_high.at(t, k, "S"))
                    pool.tensor_tensor(sBBL[:, k, :], sBB[:, k, :], sBBH[:, k, :].bitcast(F32), ALU.subtract
                                       ).then_inc(*bb_ready.mark(t, k, "S"))

        def merge_low(t, f):
            for p in parts(t):
                pool.wait_ge(*merged.at(t, f, p))
                x = (T if p == "P" else sT)[3 + f % 2][:, :]
                hi, lo = (MGH, MGL) if p == "P" else (sMGH, sMGL)
                pool.tensor_tensor(lo[:, f, :], x, hi[:, f, :].bitcast(F32), ALU.subtract).then_inc(*mg_ready.mark(t, f, p))

        pool.wait_ge(*prep_c.at("state"))
        pool.wait_ge(*constants_v.at("halo"))
        split_low(0)
        split_low(1)
        h_low(0)
        gather_index_keys(0)
        gather_index_keys(1)
        for t in range(TILES):
            j = len(GEMMS) // TILES * t
            for i in range(len(PROJ_A)):
                split_low(j + 2)
                j += 1
            if t == 0:
                for s in range(2, NSEQ):
                    gather_index_keys(s)
            for i in range(len(PROJ_B)):
                if j + 2 not in AFTER_PAGES:
                    split_low(j + 2)
                if i == 1:
                    fill_future(t)
                n, f = PROJ_B[i]
                if n == "uc":
                    conv_input(f, j)
                if n == "za":
                    convolve(f, j)
                if n == "uh" and f:
                    branch_low(f - 1)
                if n == "za" and f == KC - 1:
                    branch_low(f)
                if n == "pa":
                    gate_a(f, j)
                j += 1
            if t == 0:
                for n in range(len(PAGE_USES)):
                    gather_pages(n)
                split_low(AFTER_PAGES[0])
                split_low(AFTER_PAGES[1])
                pool.wait_ge(*s_attn.at(PAIRS[-1]))
                pool.tensor_tensor(sBB[:, :, :], sBB[:, :, :], sSZB[:, :, :], ALU.mult).then_inc(*s_attn_z.mark())
            attn_gate(t)
            attn_low(t)
            for f in range(KC):
                split_low(j + 2)
                merge_low(t, f)
                j += 1
            if t + 1 < TILES:
                h_low(t + 1)
            for f in range(KC):
                split_low(j + 2)
                j += 1

    ctx.close()

_INS = ["x_prompt", "x_sample", "c_prompt", "c_sample", "cache_k", "cache_v", "cache_kidx", "state_conv", "page_table",
        "norm_g", "w_mod", "b_mod", "w_in", "conv_w", "q_norm", "k_norm", "w_proj_a", "w_proj_b", "w_out"]
_OUTS = [("y_prompt", (1, SEQ, D)), ("y_sample", (NSEQ, NNEW, D)), ("k_prompt", (1, 1, SEQ, KV, HD)),
         ("v_prompt", (1, 1, SEQ, KV, HD)), ("kidx_prompt", (1, 1, SEQ, ID)), ("conv_prompt", (1, 1, 2, D)),
         ("k_sample", (1, NSEQ, NNEW, KV, HD)), ("v_sample", (1, NSEQ, NNEW, KV, HD)), ("kidx_sample", (1, NSEQ, NNEW, ID)),
         ("conv_sample", (1, NSEQ, 2, D))]


def declare(nc, arrays):
    ins = {n: nc.dram_tensor("in_" + n, a.shape, mybir.dt.from_np(a.dtype), kind="ExternalInput").ap() for n, a in arrays.items()}
    outs = {n: nc.dram_tensor("out_" + n, shape, F32, kind="ExternalOutput").ap() for n, shape in _OUTS}
    return ins, outs


def kernel(**inputs):
    import concourse.bacc as bacc
    from concourse.bass_utils import run_bass_kernel_spmd as run

    arrays = {n: np.ascontiguousarray(inputs[n]) for n in _INS}
    plan = {}
    draft = bacc.Bacc("TRN2", target_bir_lowering=False, num_devices=1)
    program(draft, *declare(draft, arrays), plan)
    nc = bacc.Bacc("TRN2", target_bir_lowering=False, num_devices=1)
    program(nc, *declare(nc, arrays), plan)
    r = run(nc, [{"in_" + n: a for n, a in arrays.items()}], core_ids=[0])
    return tuple(r.results[0]["out_" + n] for n, _ in _OUTS)
```

```python
from contextlib import ExitStack

import numpy as np

import concourse.bass as bass
from concourse import mybir

F32, F32R = mybir.dt.float32, mybir.dt.float32r
BF16, F16 = mybir.dt.bfloat16, mybir.dt.float16
U32, I32 = mybir.dt.uint32, mybir.dt.int32
ALU = mybir.AluOpType
ACT = mybir.ActivationFunctionType
AX_X = mybir.AxisListType.X

P = 128
D = 1024
SEQ = 2048
NSEQ, NNEW = 8, 8
PAGE = 128
NPAGES = 16
PAST = NPAGES * PAGE
RUN = PAST // P
PER_PAGE = PAGE // RUN
HEADS, KV, HD = 8, 2, 128
IH, ID = 8, 64
TOPK = 256
EPS = 1e-6
NEG = -1e30
TILE = 512
TILES = SEQ // TILE
BLOCKS = TILE // P
KC = D // P
NS = NSEQ * NNEW
STEPS = 28
ACT_COPIES = 3
LATE_COPIES = SEQ // (2 * P)

SIZES = [("uh", 1024), ("ub", 1024), ("uc", 1024), ("za", 1024), ("q", 1024), ("k", 256), ("v", 256),
         ("qi", 512), ("ki", 64), ("wi", 8), ("zb", 1024), ("ga", 1024), ("gb", 1024)]
OFFSET = {}
_at = 0
for _name, _size in SIZES:
    OFFSET[_name] = _at
    _at += _size

PROJ_A = [("ki", 0)] + [("k", h) for h in range(KV)] + [("v", h) for h in range(KV)] \
    + [("q", h) for h in range(HEADS)] + [("qi", i) for i in range(IH // 2)]
PROJ_B = [(n, f) for f in range(KC) for n in ("uh", "uc", "ub", "za")] \
    + [(n, f) for f in range(KC) for n in ("ga", "pa")] \
    + [("gb", f) for f in range(KC)] + [("zb", f) for f in range(KC)]
OUT_B = [("pb", f) for f in range(KC)]
OUT_Y = [("wo", f) for f in range(KC)]
GEMMS = [(t, n, f) for t in range(TILES) for n, f in PROJ_A + PROJ_B + OUT_B + OUT_Y]


def parts(t):
    return ("P", "S") if t == 0 else ("P",)


PRODUCTS = [(j, p) for j, (t, n, f) in enumerate(GEMMS) for p in parts(t)]
PBANK = {jp: i % 4 for i, jp in enumerate(PRODUCTS)}


class Signal:

    def __init__(self, sem, values, known, by=1):
        self.sem, self.values, self.known, self.by, self.n = sem, values, known, by, 0

    def mark(self, *event):
        self.n += self.by
        self.values[event] = self.n
        return self.sem, self.by

    def at(self, *event):
        return self.sem, self.values[event] if self.known else 1

    def end(self):
        return self.sem, max(self.values.values(), default=1)


def program(nc, ins, outs, plan):
    known = bool(plan)
    ctx = ExitStack()

    def signal(name, by=1):
        return Signal(ctx.enter_context(nc.semaphore(name)), plan.setdefault(name, {}), known, by)

    banks = plan.setdefault("banks", {})

    def bank(*key):
        return banks[key] if known else 4

    base = (nc.sbuf_base + 63) // 64 * 64
    cursor = [base]

    def region(size):
        at = cursor[0]
        cursor[0] += (size + 63) // 64 * 64
        assert cursor[0] <= nc.sbuf_usable_end, (cursor[0], nc.sbuf_usable_end)
        return at

    def at(name, shape, dt, offset):
        return nc.alloc_sbuf_tensor_at(name, shape, dt, offset=offset)

    def own(name, shape, dt=F32):
        size = int(np.prod(shape[1:])) * (2 if dt in (BF16, F16) else 4)
        return at(name, shape, dt, region(size))

    rKT, rV, rKH, rKL = region(16384), region(16384), region(8192), region(8192)
    rH, rW, rB, rM, rS = region(32768), region(24576), region(32768), region(16384), region(32768)
    KT = at("KT", [P, KV, SEQ], F32, rKT)
    V = at("V", [P, SEQ // P, KV * HD], F32, rV)
    KIH = at("KIH", [P, SEQ], F32R, rKH)
    KIL = at("KIL", [P, SEQ], F32R, rKL)
    HTH = at("HTH", [P, KC, TILE], F32R, rH)
    HTL = at("HTL", [P, KC, TILE], F32R, rH + 16384)
    LP = at("LP", [P, 2, 2, SEQ], F32, rH)
    BBH = at("BBH", [P, KC, TILE], F32R, rH)
    BBL = at("BBL", [P, KC, TILE], F32R, rH + 16384)
    WR = [at(f"WR{i}", [P, KC, P], F32, rW + 8192 * i) for i in range(3)]
    WLH = [at(f"WLH{i}", [P, 2, KC, P], F32R, rW + 8192 * i) for i in range(3)]
    WL, WH = ([a[:, part] for a in WLH] for part in range(2))
    XN = at("XN", [P, BLOCKS, D], F32, rB)
    SQ = [at(f"SQ{i}", [P, TILE], F32, rB + 2048 * i) for i in range(2)]
    RS = [at(f"RS{i}", [P, TILE], F32, rB + 2048 * (2 + i)) for i in range(2)]
    QO = [at(f"QO{i}", [P, TILE], F32, rB + 2048 * (4 + i)) for i in range(2)]
    KO = at("KO", [P, BLOCKS, P], F32, rB + 2048 * 6)
    KIO = at("KIO", [P, BLOCKS, ID], F32, rB + 2048 * 7)
    AS = at("AS", [P, 8, TILE], F32, rB + 16384)
    BAH = at("BAH", [P, KC, TILE], F32R, rB)
    BAL = at("BAL", [P, KC, TILE], F32R, rB + 16384)
    SZB = at("SZB", [P, KC, TILE], F32, rB)
    GB = at("GB", [P, KC, TILE], F32, rB + 16384)
    KLOW = at("KLOW", [P, KV, SEQ], F32R, rKT)
    KHIGH = at("KHIGH", [P, KV, SEQ], F32R, rB + 16384)
    XR = [at(f"XR{i}", [P, BLOCKS, P], F32, rB + 16384 + 2048 * i) for i in range(2)]
    YO = [at(f"YO{i}", [P, BLOCKS, P], F32, rB + 20480 + 2048 * i) for i in range(2)]
    QI = at("QI", [P, IH, TILE], F32R, rM)
    BB = at("BB", [P, HEADS, TILE], F32, rM)
    SC = at("SC", [P, BLOCKS, SEQ], F32, rS)
    MGH = at("MGH", [P, KC, TILE], F32R, rS)
    MGL = at("MGL", [P, KC, TILE], F32R, rS + 16384)
    MW = [at(f"MW{i}", [P, KC, P], F32, rS + 4096 * i) for i in range(8)]

    U = own("U", [P, TILE + 2])
    rT = region(5 * 2048)
    T = [at(f"T{i}", [P, TILE], F32, rT + 2048 * i) for i in range(5)]
    QU = [at(f"QU{i}", [P, 2, P], F32, rT + 3 * 2048 + 2048 * i) for i in range(2)]
    QLOW = [at(f"QLOW{i}", [P, 2, P], F32R, rT + 3 * 2048 + 2048 * i) for i in range(2)]
    QHIGH = [at(f"QHIGH{i}", [P, 2, P], F32R, rT + 3 * 2048 + 1024 + 2048 * i) for i in range(2)]
    rJ = region(4224)
    JUNK = at("JUNK", [P, PAST + NS], BF16, rJ)
    RB = [at(f"RB{i}", [P, 256], F32, rJ + 1024 * i) for i in range(2)]
    DG = [at(f"DG{i}", [P, 256], F32, rJ + 2048 + 1024 * i) for i in range(2)]
    GT = own("GT", [P, TILE], F16)
    BD = own("BD", [P, TILE], F16)
    ident = own("ident", [P, P])
    ones = own("ones", [P, P])
    COL = own("COL", [P, 58])
    MOD = own("MOD", [P, 24, 9])
    AM = own("AM", [P, KC, 9])
    WI = own("WI", [P, BLOCKS, IH])
    HALO = own("HALO", [P, KC, 2])
    SMALL = own("SMALL", [P, 96])
    PFX = own("PFX", [P, TILE])
    MROW = [PFX, T[1]]

    def small(a, n):
        return SMALL[:, a:a + n]

    SS, SV, RT, R1, R2 = small(0, 4), small(4, 4), small(8, 4), small(12, 4), small(16, 4)
    EPSC = small(20, 1)
    LO, HI, MID, CNT, NEED, ABS = (small(24 + 6 * i, 5) for i in range(6))
    PM = small(60, 16).rearrange("p (u h c) -> p u h c", u=2, h=2)
    NM = small(76, 4).rearrange("p (u h) -> p u h", u=2)
    SUM = small(80, 4).rearrange("p (u h) -> p u h", u=2)
    RIN = small(84, 4).rearrange("p (u h) -> p u h", u=2)
    GE = own("GE", [P, 5], U32)
    LT = own("LT", [P, 5], U32)

    free_k = [rKT + 2048, rKT + 4096, rKT + 6144, rKT + 10240, rKT + 12288, rKT + 14336,
              rKH + 2048, rKH + 4096, rKH + 6144, rKL + 2048, rKL + 4096, rKL + 6144]
    sHT, sMG = at("sHT", [P, KC, 2 * NS], F32R, free_k[0]), at("sMG", [P, KC, 2 * NS], F32R, free_k[0])
    sBA, sBB2 = at("sBA", [P, KC, 2 * NS], F32R, free_k[3]), at("sBB2", [P, KC, 2 * NS], F32R, free_k[3])
    (sHTH, sHTL), (sMGH, sMGL), (sBAH, sBAL), (sBBH, sBBL) = (
        (a[:, :, 0:NS], a[:, :, NS:2 * NS]) for a in (sHT, sMG, sBA, sBB2))
    sSZB, sGB = at("sSZB", [P, KC, NS], F32, free_k[2]), at("sGB", [P, KC, NS], F32, free_k[5])
    sMA, sBB = at("sMA", [P, KC, NS], F32, free_k[6]), at("sBB", [P, KC, NS], F32, free_k[7])
    sQ = at("sQ", [P, NSEQ, HEADS, NNEW], F32, free_k[8])
    sKT, sKIH, sKIL = (at("sKT", [P, KV, NS], F32, free_k[9]),
                       at("sKIH", [P, P], F32R, free_k[9] + 512), at("sKIL", [P, P], F32R, free_k[9] + 1024))
    sQI = at("sQI", [P, IH, NS], F32R, free_k[10])
    sWR = at("sWR", [P, NSEQ, IH, NNEW], F32, free_k[11])
    sV = at("sV", [NS, KV * HD], F32, rV + 4096)
    sSEL = [at("sSEL0", [NS, 2, P], F32, rV + 5120), at("sSEL1", [NS, 2, P], F32, rV + 11136)]
    sHS = at("sHS", [P, KC, NSEQ, 2], F32, rV + 6144)
    sUK = at("sUK", [P, KC, NSEQ, 2], F32, rV + 6656)
    sT = [at(f"sT{i}", [P, NS], F32, rV + 7168 + 256 * i) for i in range(5)]
    sU = at("sU", [P, NSEQ, NNEW + 2], F32, rV + 8448)
    sYT = [at(f"sYT{i}", [P, NS], F32, rV + 8832 + 256 * i) for i in range(2)]
    sKO = at("sKO", [NS, KV * HD], F32, rV + 9344)
    sKIO = at("sKIO", [NS, ID], F32, rV + 10368)
    sQT = at("sQT", [P, NS], F32, rV + 10624)
    sW8 = at("sW8", [IH, NS], F32, rV + 10880)
    sCO = at("sCO", [2 * NSEQ, D], F32, rM + 8192)
    CO = at("CO", [2, D], F32, rM + 12288)
    sSQ = [at(f"sSQ{i}", [P, NS], F32, rV + 13184 + 256 * i) for i in range(2)]
    sRS = [at(f"sRS{i}", [P, NS], F32, rV + 13696 + 256 * i) for i in range(2)]
    sAS = at("sAS", [P, 8, NS], F32, rV + 14208)
    sRAW = at("sRAW", [P, 2, P], F32, rV + 12160)
    PAIR = at("PAIR", [P, NS], F32, free_k[9] + 1536)
    sXN = at("sXN", [NS, D], F32, rM)
    sYO = at("sYO", [NS, D], F32, rM)
    SC0 = at("SC0", [P, BLOCKS, TILE], F32, rS)
    sST = at("sST", [P, RUN + 1, NS], F32, rS + 8192)
    sSC = at("sSC", [NS, PAST + NS], F32, rS + 8192 + 4352)
    sBX = at("sBX", [P, PAST + NS], F32, rS + 8192 + 4352 + 8448)
    sKR = [at(f"sKR{i}", [P, RUN, ID], F32, rS + 8192 + 4352 + 8448 + 4096 * i) for i in range(2)]
    sKX = [at(f"sKX{i}", [P, RUN, P], F32, rM + 8192 * i) for i in range(2)]
    sKPH = [at(f"sKPH{i}", [P, TILE], F32R, rS + 8192 + 4352 + 4096 * i) for i in range(2)]
    sKPL = [at(f"sKPL{i}", [P, TILE], F32R, rS + 8192 + 4352 + 2048 + 4096 * i) for i in range(2)]
    sPG = [at(f"sPG{i}", [P, RUN, KV * HD], F32, a) for i, a in enumerate((rH, rH + 16384, rW))]
    sKPT = at("sKPT", [P, PAST], F32, rW + 16384)
    sL = at("sL", [P, PAST + NS], F32, rM)
    sPT = at("sPT", [P, RUN, P], F32, rT)
    sPTN = at("sPTN", [NS, P], F32, rT + 8192)
    sXR = at("sXR", [NS, D], F32, rM + 4096)
    ROWS = at("ROWS", [58, P], F32, rT)
    C9 = at("C9", [9, D], F32, rM + 4096)
    ST16 = at("ST16", [2 * NSEQ, D], F32, rM + 8192)
    SCT = at("SCT", [P, KC, 9], F32, rM + 12288)
    TABLE = own("TABLE", [P, NSEQ], I32)
    PIECE = own("PIECE", [P, 1], I32)
    TABLEF = own("TABLEF", [P, NSEQ])
    PIECEF = own("PIECEF", [P, 1])
    ROW = own("ROW", [P, NSEQ], U32)
    ps = [ctx.enter_context(nc.psum_tensor(f"ps{i}", [P, TILE], F32)) for i in range(8)]
    rows_in = signal("rows_in", 16)
    mw_in = [signal(f"mw_in{i}", 16) for i in range(8)]
    x_in, xs_in = signal("x_in", 16), signal("xs_in", 16)
    biased, conv_t, conv_store, constants_v, xs_mod = (
        signal(n) for n in ("biased", "conv_t", "conv_store", "constants_v", "xs_mod"))
    abs_values = plan.setdefault("abs_values", {})
    PAIRS = range(NSEQ // 2)
    PAGE_USES = [(what, 2 * u + e) for u in PAIRS for what in "kv" for e in range(2)]
    page_slot = lambda *use: PAGE_USES.index(use) % 3
    KEY_GROUPS = [(e, kv, c) for e in range(2) for kv in range(KV) for c in range(4)]
    first_row = lambda e, kv: 64 * e + 32 * kv
    by_slot = lambda row: row.rearrange("t (q i) -> t i q", i=RUN)
    SAMPLE_ITEMS = NSEQ * 4 // 2
    sample_groups = lambda i: [divmod(n, 4) for n in (2 * i, 2 * i + 1)] if 0 <= i < SAMPLE_ITEMS else []
    AFTER_PAGES = range(len(PROJ_A) + len(PROJ_B), len(PROJ_A) + len(PROJ_B) + 3)
    w_in_ = [signal(f"w_in{i}", 16) for i in range(3)]
    q_in = [signal(f"q_in{i}", 16) for i in range(2)]
    ma_in = [signal(f"ma_in{i}", 16) for i in range(2)]
    xr_in = [signal(f"xr_in{i}", 16) for i in range(2)]
    table_in, table_row, piece, kx_dup = signal("table_in", 16), signal("table_row"), signal("piece"), signal("kx_dup")
    kx_in = [signal(f"kx_in{i}", 16) for i in range(2)]
    pg_in = [signal(f"pg_in{i}", 16) for i in range(3)]
    q_out = [signal(f"q_out{i}", 16) for i in range(2)]
    ma_out = [signal(f"ma_out{i}", 16) for i in range(2)]
    y_out = [signal(f"y_out{i}", 16) for i in range(2)]
    k_out, ki_out, v_out, s_out = (signal(n, 16) for n in ("k_out", "ki_out", "v_out", "s_out"))
    constants = signal("constants")
    dve_step, pool_step, act_step = signal("dve_step"), signal("pool_step"), signal("act_step")
    silu_c, prep_t, prep_c = signal("silu_c"), signal("prep_t"), signal("prep_c")
    mod_mm, mod_row, mod_t, mod_ready = signal("mod_mm"), signal("mod_row"), signal("mod_t"), signal("mod_ready")
    sumsq, var, root_x, xnorm = (signal(n) for n in ("sumsq", "var", "root_x", "xnorm"))
    x_t, x_mod, h_high, h_ready = (signal(n) for n in ("x_t", "x_mod", "h_high", "h_ready"))
    w_high, w_split = signal("w_high"), signal("w_split")
    product, evac = signal("product"), signal("evac")
    s_parts, s_parts_copy = signal("s_parts"), signal("s_parts_copy")
    aux_done, root, kt_ready, w8_ready, a_done = (
        signal(n) for n in ("aux_done", "root", "kt_ready", "w8_ready", "a_done"))
    idx_done, relu, scored, causal, mask = (signal(n) for n in ("idx_done", "relu", "scored", "causal", "mask"))
    kx_t, kx_high, kx_split, s_idx, s_sum, s_score_t = (
        signal(n) for n in ("kx_t", "kx_high", "kx_split", "s_idx", "s_sum", "s_score_t"))
    u_ready, taps, conv, ba_high, ba_ready, gate_mul = (
        signal(n) for n in ("u_ready", "taps", "conv", "ba_high", "ba_ready", "gate_mul"))
    qk, logits, row_max, expd, diag, p_t, p_copy, p_copy_a, pv, rb, rb_copy, attn, attn_z = (
        signal(n) for n in ("qk", "logits", "row_max", "expd", "diag", "p_t", "p_copy", "p_copy_a", "pv", "rb",
                            "rb_copy", "attn", "attn_z"))
    k_high, k_split, k_whole = (signal(n) for n in ("k_high", "k_split", "k_whole"))
    q_high, q_split = signal("q_high"), signal("q_split")
    gb_out, gb_in = signal("gb_out", 16), [signal(f"gb_in{i}", 16) for i in range(2)]
    bb_high, bb_low_pool, bb_low_dve = signal("bb_high"), signal("bb_low_pool"), signal("bb_low_dve")
    bb_ready_at = lambda t, k, p: (bb_low_dve if p == "P" and k % 2 else bb_low_pool).at(t, k if p == "P" else 0, p)
    merged, mg_ready = signal("merged"), signal("mg_ready")
    gated, y_t, y_sum = signal("gated"), signal("y_t"), signal("y_sum")
    s_bx, s_bx_copy, s_kt, s_kt_copy, s_qk, s_logits, s_exp, s_pt, s_pt_copy, s_scaled, s_pv, s_turned, s_attn, s_attn_z = (
        signal(n) for n in ("s_bx", "s_bx_copy", "s_kt", "s_kt_copy", "s_qk", "s_logits", "s_exp", "s_pt",
                            "s_pt_copy", "s_scaled", "s_pv", "s_turned", "s_attn", "s_attn_z"))

    q_scratch = nc.dram_tensor("q_scratch", [TILES, P, HEADS, TILE], F32).ap()
    gb_scratch = nc.dram_tensor("gb_scratch", [TILES, KC, P, TILE], F32).ap()
    ma_scratch = nc.dram_tensor("ma_scratch", [TILES, KC, P, TILE], F32).ap()

    def width(i):
        return (i + 1) * P

    def pieces(w):
        return [(c, min(TILE, w - c)) for c in range(0, w, TILE)]

    def weights(t, n, f):
        if n in ("pa", "pb", "wo"):
            src, col = ins[{"pa": "w_proj_a", "pb": "w_proj_b", "wo": "w_out"}[n]], f * P
        else:
            src, col = ins["w_in"], OFFSET[n] + f * P
        return src[0].rearrange("(k p) n -> p k n", p=P)[:, :, col:col + P]

    key_quarter = lambda t, f: (f // 4, slice(f % 4 * (t + 1) * P, (f % 4 + 1) * (t + 1) * P))
    key_quarters = lambda n, f: {1: [0, 1], 2: [2, 3], 3: [4], 4: [5], 5: [6], 6: [7]}.get(f, []) if n == "zb" else []
    UNITS = [(b, pr) for b in range(BLOCKS) for pr in range(HEADS // 2)]
    PT_USES = [(t, u, c) for t in range(TILES) for u, (b, pr) in enumerate(UNITS) for c in range((BLOCKS * t + b + 2) // 2)]
    PT_NUMBER = {use: n for n, use in enumerate(PT_USES)}
    p_use = lambda *use: PT_NUMBER[use]
    p_slot = lambda *use: PT_NUMBER[use] % 3
    on_act = lambda t, u, c: c < (LATE_COPIES if late_runs(t, u) else ACT_COPIES)
    p_copied = lambda t, u, c: (p_copy_a if on_act(t, u, c) else p_copy).at(t, u, c)

    def p_free(engine, t, u, c):
        before = p_use(t, u, c) - 3
        if before >= 0 and PT_USES[before][0] == t:
            engine.wait_ge(*pv.at(*PT_USES[before]))

    scores = lambda t: SC0 if t == 0 else SC
    late_blocks = lambda t: (2, 3) if t == TILES - 1 else ()
    late_runs = lambda t, u: [(b, r) for b in late_blocks(t) for r in range(4) if u == 4 * (b - 2) + r]
    index_blocks = lambda t: [b for b in range(BLOCKS) if width(BLOCKS * t + b) > TOPK]
    NORMED = [i for i, (n, f) in enumerate(PROJ_A) if n in ("k", "q")]
    s3 = lambda ap: ap.rearrange("p (s t) -> p s t", s=NSEQ)
    last_part = lambda t: parts(t)[-1]

    block = ctx.enter_context(nc.Block())

    @block.sync
    def _(sp):
        def load_w(j):
            if j >= len(GEMMS):
                return
            if j >= 3:
                sp.wait_ge(*product.at(j - 3, last_part(GEMMS[j - 3][0])))
            sp.dma_start(WR[j % 3][:, :, :], weights(*GEMMS[j])).then_inc(*w_in_[j % 3].mark(j))

        def load_mw(f):
            if f >= 8:
                sp.wait_ge(*mod_mm.at(f - 8))
            sp.dma_start(MW[f % 8][:, :, :], ins["w_mod"][0].rearrange("(k p) n -> p k n", p=P)[:, :, f * P:f * P + P]
                         ).then_inc(*mw_in[f % 8].mark(f))

        def load_x(t):
            if t:
                sp.wait_ge(*attn_z.at(t - 1, UNITS[-1]))
            sp.dma_start(XN[:, :, :], ins["x_prompt"][0, t * TILE:(t + 1) * TILE].rearrange("(b p) d -> p b d", p=P)
                         ).then_inc(*x_in.mark(t, "P"))
            if t == 0:
                sp.dma_start(sXN[:, :], ins["x_sample"].rearrange("s t d -> (s t) d")).then_inc(*x_in.mark(t, "S"))

        def row(name):
            a = ins[name]
            return a.rearrange("a (k p) -> (a k) p", p=P)

        for a, n, src in ((0, 8, row("norm_g")), (8, 24, row("b_mod")),
                          (32, 24, ins["conv_w"][0].rearrange("w (k p) -> (w k) p", p=P)),
                          (56, 1, ins["q_norm"]), (57, 1, ins["k_norm"])):
            sp.dma_start(ROWS[a:a + n, :], src).then_inc(*rows_in.mark(a))
        sp.dma_start(C9[0:1, :], ins["c_prompt"]).then_inc(*rows_in.mark("c0"))
        sp.dma_start(C9[1:9, :], ins["c_sample"]).then_inc(*rows_in.mark("c1"))
        sp.dma_start(ST16[:, :], ins["state_conv"][0].rearrange("s w d -> (s w) d")).then_inc(*rows_in.mark("all"))
        for f in range(8):
            load_mw(f)
        load_x(0)
        for s in range(NSEQ):
            sp.dma_start(TABLE[:, s:s + 1], ins["page_table"][s].unsqueeze(1).to_broadcast([NPAGES, PER_PAGE]).unsqueeze(2),
                         allow_slow_non_contiguous=True).then_inc(*table_in.mark(s))
        for f in range(8, 16):
            load_mw(f)
        for j in range(3):
            load_w(j)
        for f in range(16, 24):
            load_mw(f)

        def store_a(t, i):
            n, f = PROJ_A[i]
            r = slice(t * TILE, (t + 1) * TILE)
            if n == "ki":
                sp.wait_ge(*a_done.at(t, i, "P"))
                sp.dma_start(outs["kidx_prompt"][0, 0, r].rearrange("(b p) d -> p b d", p=P), KIO[:, :, :]
                             ).then_inc(*ki_out.mark(t))
            if n == "k":
                sp.wait_ge(*a_done.at(t, i, "P"))
                sp.dma_start(outs["k_prompt"][0, 0, r, f].rearrange("(b p) d -> p b d", p=P), KO[:, :, :]
                             ).then_inc(*k_out.mark(t, f))
            if n == "v":
                sp.wait_ge(*a_done.at(t, i, "P"))
                sp.dma_start(outs["v_prompt"][0, 0, r, f].rearrange("(b p) d -> p b d", p=P),
                             V[:, BLOCKS * t:BLOCKS * (t + 1), f * HD:(f + 1) * HD]).then_inc(*v_out.mark(t, f))
            if n == "q":
                sp.wait_ge(*a_done.at(t, i, "P"))
                sp.dma_start(q_scratch[t, :, f], QO[f % 2][:, :]).then_inc(*q_out[f % 2].mark(t, f))
            if t == 0 and n in ("k", "v") and f == 1:
                sp.wait_ge(*a_done.at(t, i, "S"))
                name, src = ("k_sample", sKO) if n == "k" else ("v_sample", sV)
                sp.dma_start(outs[name][0].rearrange("s t h d -> (s t) (h d)"), src[:, :]).then_inc(*s_out.mark(n))
            if t == 0 and n == "ki":
                sp.wait_ge(*a_done.at(t, i, "S"))
                sp.dma_start(outs["kidx_sample"][0].rearrange("s t d -> (s t) d"), sKIO[:, :]).then_inc(*s_out.mark(n))

        def load_q(t, u):
            b, pr = UNITS[u]
            if u >= 2:
                sp.wait_ge(*qk.at(t, u - 2))
            elif u == 0:
                sp.wait_ge(*gate_mul.at(t, KC - 1, "P"))
                sp.wait_ge(*ma_out[0].at(t, KC - 2))
                sp.wait_ge(*ma_out[1].at(t, KC - 1))
                sp.wait_ge(*q_out[0].at(t, 6))
                sp.wait_ge(*q_out[1].at(t, 7))
                if t == 0:
                    sp.wait_ge(*s_pv.at(PAIRS[-1], 1))
            sp.dma_start(QU[u % 2][:, :, :], q_scratch[t, :, 2 * pr:2 * pr + 2, b * P:(b + 1) * P]
                         ).then_inc(*q_in[u % 2].mark(t, u))

        def load_gate(t, f):
            sp.dma_start(GB[:, f, :], gb_scratch[t, f]).then_inc(*gb_in[f % 2].mark(t, f))

        def store_y(t, f):
            sp.wait_ge(*y_sum.at(t, f, "P"))
            sp.dma_start(outs["y_prompt"][0, t * TILE:(t + 1) * TILE, f * P:(f + 1) * P].rearrange("(b p) d -> p b d", p=P),
                         YO[f % 2][:, :, :]).then_inc(*y_out[f % 2].mark(t, f))

        for t in range(TILES):
            first = t * (len(GEMMS) // TILES)
            for i in range(len(PROJ_A)):
                load_w(first + i + 3)
                if i >= 3:
                    store_a(t, i - 3)
            for i in range(len(PROJ_A) - 3, len(PROJ_A)):
                store_a(t, i)
            for i in range(len(PROJ_B)):
                j = first + len(PROJ_A) + i
                if j + 3 not in AFTER_PAGES:
                    load_w(j + 3)
                if t and i == len(PROJ_B) - 4:
                    load_q(t, 0)
                    load_q(t, 1)
                n, f = GEMMS[j - 2][1:]
                if n == "pa":
                    sp.wait_ge(*gate_mul.at(t, f, "P"))
                    sp.dma_start(ma_scratch[t, f], T[3 + f % 2][:, :]).then_inc(*ma_out[f % 2].mark(t, f))
                n, f = GEMMS[j - 1][1:]
                if n == "gb":
                    sp.wait_ge(*evac.at(j - 1, "P"))
                    sp.dma_start(gb_scratch[t, f], GB[:, f, :]).then_inc(*gb_out.mark(t, f))
            for u in range(len(UNITS)):
                if u >= 2 or t == 0:
                    load_q(t, u)
                if (t, u) == (0, 1):
                    sp.wait_ge(*s_turned.at(PAIRS[-1]))
                    for j in AFTER_PAGES:
                        load_w(j)
            sp.wait_ge(*(k_whole.at(t) if t + 1 < TILES else qk.at(t, len(UNITS) - 1)))
            load_gate(t, 0)
            load_gate(t, 1)
            if t + 1 < TILES:
                load_x(t + 1)
            j = first + len(PROJ_A) + len(PROJ_B)
            for f in range(KC):
                if f >= 2:
                    sp.wait_ge(*merged.at(t, f - 2, "P"))
                else:
                    sp.wait_ge(*pv.at(t, len(UNITS) - 1))
                    sp.wait_ge(*ma_out[f].at(t, KC - 2 + f))
                sp.dma_start(T[1 + f % 2][:, :], ma_scratch[t, f]).then_inc(*ma_in[f % 2].mark(t, f))
                if f >= 2:
                    load_gate(t, f)
                load_w(j + f + 3)
            for f in range(KC):
                if f >= 2:
                    sp.wait_ge(*y_sum.at(t, f - 2, "P"))
                else:
                    sp.wait_ge(*merged.at(t, KC - 1, "P"))
                sp.dma_start(XR[f % 2][:, :, :], ins["x_prompt"][0, t * TILE:(t + 1) * TILE, f * P:(f + 1) * P]
                             .rearrange("(b p) d -> p b d", p=P)).then_inc(*xr_in[f % 2].mark(t, f))
                if t == 0 and f == 0:
                    sp.wait_ge(*bb_ready_at(t, KC - 1, "P"))
                    sp.dma_start(sXR[:, :], ins["x_sample"].rearrange("s t d -> (s t) d")).then_inc(*xs_in.mark())
                load_w(j + KC + f + 3)
                if f >= 2:
                    store_y(t, f - 2)
            for f in range(KC - 2, KC):
                store_y(t, f)
            if t == 0:
                sp.wait_ge(*y_sum.at(t, KC - 1, "S"))
                sp.dma_start(outs["y_sample"].rearrange("s t d -> (s t) d"), sYO[:, :]).then_inc(*s_out.mark("y"))
                sp.wait_ge(*conv_store.at("S"))
                sp.dma_start(outs["conv_sample"][0].rearrange("s w d -> (s w) d"), sCO[:, :]).then_inc(*s_out.mark("conv"))
        sp.wait_ge(*conv_store.at("P"))
        sp.dma_start(outs["conv_prompt"][0, 0], CO[:, :]).then_inc(*s_out.mark("last"))
        for sig in (*q_out, *ma_out, *y_out, k_out, ki_out, v_out, s_out):
            sp.wait_ge(*sig.end())


    @block.scalar
    def _(act):
        def link(ins_):
            ins_.then_inc(*act_step.mark(act_step.n))
            act.wait_ge(act_step.sem, act_step.n)

        def split_high(j):
            if j < len(GEMMS):
                act.wait_ge(*w_in_[j % 3].at(j))
                act.activation(WH[j % 3][:, :, :], WR[j % 3][:, :, :], ACT.Copy).then_inc(*w_high.mark(j))

        act.wait_ge(*rows_in.at("all"))
        act.activation(C9[:, :], C9[:, :], ACT.Silu).then_inc(*silu_c.mark())

        def norm(t):
            act.wait_ge(*x_in.at(t, last_part(t)))
            for b in range(BLOCKS - 1):
                link(act.activation(JUNK[:, 0:D], XN[:, b, :], ACT.Square, accum_out=SS[:, b:b + 1]))
            b = BLOCKS - 1
            act.activation(JUNK[:, 0:D], XN[:, b, :], ACT.Square, accum_out=SS[:, b:b + 1]).then_inc(*sumsq.mark(t, "P"))
            if t == 0:
                act.wait_ge(*sumsq.at(t, "P"))
                act.activation(JUNK[0:NS, 0:D], sXN[:, :], ACT.Square, accum_out=NEED[0:NS, 0:1]).then_inc(*sumsq.mark(t, "S"))
            for p in parts(t):
                v, r, n = (SV, RT, P) if p == "P" else (NEED[:, 1:2], NEED[:, 2:3], NS)
                act.wait_ge(*var.at(t, p))
                act.activation(r[0:n], v[0:n], ACT.Sqrt).then_inc(*root_x.mark(t, p))

        def modulate(t):
            if t == 0:
                act.wait_ge(*mod_ready.at("AM"))
            for k in range(KC):
                act.wait_ge(*x_t.at(t, k))
                if k >= 2:
                    act.wait_ge(*h_ready.at(t, k - 2, "P"))
                elif t:
                    act.wait_ge(*mg_ready.at(t - 1, KC - 2 + k, "P"))
                act.activation(T[3 + k % 2][:, :], ps[bank("x_t", t, k)][:, :], ACT.Identity,
                               bias=MOD[:, k, 0:1], scale=AM[:, k, 0:1]).then_inc(*x_mod.mark(t, k))

        def parts_out(t, j):
            if t == 0:
                act.wait_ge(*s_parts.at(j))
                act.activation(sRAW[:, :, :].rearrange("p l c -> p (l c)"), ps[bank("parts", j)][:, 0:2 * P], ACT.Copy
                               ).then_inc(*s_parts_copy.mark(j))

        def evac_a(t, i, j):
            parts_out(t, j)
            n, f = PROJ_A[i]
            for p in parts(t):
                m = TILE if p == "P" else NS
                dst = (AS if p == "P" else sAS)[:, i % 8, :]
                act.wait_ge(*product.at(j, p))
                if i >= 8:
                    act.wait_ge(*a_done.at(t, i - 8, p))
                elif t and i == 0:
                    for f_ in range(2):
                        act.wait_ge(*y_out[f_].at(t - 1, KC - 2 + f_))
                src = ps[PBANK[j, p]][:, 0:m]
                if i in NORMED:
                    act.activation(dst, src, ACT.Copy)
                    q = NORMED.index(i)
                    if q >= 2:
                        act.wait_ge(*aux_done.at(t, NORMED[q - 2], p))
                    sq = (SQ if p == "P" else sSQ)[q % 2][:, :]
                    act.activation(sq, src, ACT.Square).then_inc(*evac.mark(j, p))
                else:
                    act.activation(dst, src, ACT.Copy).then_inc(*evac.mark(j, p))

        def root_a(t, i):
            if i not in NORMED:
                return
            q = NORMED.index(i)
            for p in parts(t):
                act.wait_ge(*aux_done.at(t, i, p))
                if q >= 2:
                    act.wait_ge(*a_done.at(t, NORMED[q - 2], p))
                m = TILE if p == "P" else NS
                rs = (RS if p == "P" else sRS)[q % 2][:, :]
                act.activation(rs, ps[bank("aux", t, i, p)][:, 0:m], ACT.Sqrt, bias=EPSC, scale=1.0 / HD
                               ).then_inc(*root.mark(t, i, p))

        relus = [0]

        def index_relu(t):
            act.wait_ge(*a_done.at(t, len(PROJ_A) - 1, last_part(t)))
            for b in index_blocks(t):
                for h in range(IH):
                    for c, n in pieces(width(BLOCKS * t + b)):
                        r = relus[0]
                        relus[0] += 1
                        act.wait_ge(*idx_done.at(t, b, h, c))
                        if r >= 4:
                            act.wait_ge(*scored.at(r - 4))
                        act.activation(T[1 + r % 4][:, 0:n], ps[bank("idx", t, b, h, c)][:, 0:n], ACT.Relu
                                       ).then_inc(*relu.mark(r))

        def conv_taps(f):
            for p in parts(t):
                act.wait_ge(*u_ready.at(t, f, p))
                for w in (2, 1, 0):
                    if w == 0:
                        if f:
                            act.wait_ge(*ba_ready.at(t, f - 1, p))
                    if p == "P":
                        src, dst = U[:, w:w + TILE], (T[0], T[2], T[1])[w][:, :]
                    else:
                        src, dst = sU[:, :, w:w + NNEW], s3((sT[0], sT[2], sT[1])[w][:, :])
                    ins_ = act.activation(dst, src, ACT.Copy, scale=COL[:, 32 + 8 * w + f:33 + 8 * w + f])
                ins_.then_inc(*taps.mark(t, f, p))

        def branch_high(f):
            for p in parts(t):
                act.wait_ge(*conv.at(t, f, p))
                if f == 0 and p == "P":
                    act.wait_ge(*q_out[0].at(t, HEADS - 2))
                    act.wait_ge(*q_out[1].at(t, HEADS - 1))
                    act.wait_ge(*k_out.at(t, 1))
                    act.wait_ge(*ki_out.at(t))
                    act.wait_ge(*a_done.at(t, len(PROJ_A) - 1, last_part(t)))
                if p == "P":
                    act.activation(BAH[:, f, :], T[0][:, :], ACT.Copy).then_inc(*ba_high.mark(t, f, p))
                else:
                    act.activation(sBAH[:, f, :], sT[0][:, :], ACT.Copy).then_inc(*ba_high.mark(t, f, p))

        def evac_b(t, i, j):
            parts_out(t, j)
            n, f = PROJ_B[i]
            for p in parts(t):
                m = TILE if p == "P" else NS
                src = ps[PBANK[j, p]][:, 0:m]
                act.wait_ge(*product.at(j, p))
                tt = T if p == "P" else sT
                func = ACT.Copy
                if n == "uh":
                    if f:
                        act.wait_ge(*conv.at(t, f - 1, p))
                    elif p == "P":
                        act.wait_ge(*scored.at(relus[0] - 1))
                    dst = tt[1][:, :]
                elif n == "uc":
                    dst = tt[2][:, :]
                elif n == "ub":
                    dst = tt[3][:, :]
                elif n == "za":
                    dst, func = tt[4][:, :], ACT.Silu
                elif n == "ga":
                    if f >= 2:
                        act.wait_ge(*gate_mul.at(t, f - 2, p))
                    else:
                        act.wait_ge(*ba_ready.at(t, KC - 1, p))
                    dst, func = tt[1 + f % 2][:, :], ACT.Sigmoid
                elif n == "pa":
                    if f >= 2 and p == "P":
                        act.wait_ge(*ma_out[f % 2].at(t, f - 2))
                    dst = tt[3 + f % 2][:, :]
                elif n == "zb":
                    dst, func = (SZB if p == "P" else sSZB)[:, f, :], ACT.Silu
                else:
                    dst, func = (GB if p == "P" else sGB)[:, f, :], ACT.Sigmoid
                act.activation(dst, src, func).then_inc(*evac.mark(j, p))

        def duplicate(s):
            if s < NSEQ:
                act.wait_ge(*kx_in[s % 2].at(s))
                if s >= 2:
                    act.wait_ge(*kx_t.at(s - 2, 3))
                act.activation(sKX[s % 2][:, :, :].rearrange("p i (c d) -> p i c d", c=2),
                               sKR[s % 2][:, :, :].unsqueeze(2).to_broadcast([P, RUN, 2, ID]), ACT.Copy).then_inc(*kx_dup.mark(s))

        def sample_keys(i):
            if i % 2 == 0 and i < SAMPLE_ITEMS:
                duplicate(i // 2 + 1)
            for s, c in sample_groups(i):
                n = 4 * s + c
                act.wait_ge(*kx_t.at(s, c))
                if n >= 2:
                    act.wait_ge(*s_idx.at(*divmod(n - 2, 4)))
                act.activation(sKPH[n % 2][:, :], ps[bank("kx", s, c)][:, :], ACT.Copy).then_inc(*kx_high.mark(s, c))

        def sample_scores_out():
            for c in range(5):
                act.wait_ge(*s_score_t.at(c))
                src = ps[bank("sst", c)][0:NS, :]
                if c < 4:
                    ins_ = act.activation(by_slot(sSC[:, 0:PAST])[:, 4 * c:4 * c + 4, :], src.rearrange("t (i q) -> t i q", i=4), ACT.Copy)
                else:
                    ins_ = act.activation(sSC[:, PAST:PAST + NS], src[:, 0:NS], ACT.Copy)
                ins_.then_inc(*s_bx_copy.mark("sc", c))

        def block_mask(t, b):
            act.wait_ge(*mask.at(t, b))
            row = scores(t)[:, b, 0:width(BLOCKS * t + b)]
            act.activation(row, row, ACT.Copy, scale=-NEG).then_inc(*biased.mark(t, b))

        def masks(t):
            for b in index_blocks(t):
                if b not in late_blocks(t):
                    block_mask(t, b)
            if t == 0:
                act.wait_ge(*mask.at(t, "S"))
                act.activation(sSC[:, :], sSC[:, :], ACT.Copy, scale=-NEG).then_inc(*biased.mark(t, "S"))

        def sample_mask(u):
            for c in range(5):
                n = TILE if c < 4 else NS
                act.wait_ge(*s_bx.at(u, c))
                act.activation(sBX[:, c * TILE:c * TILE + n], ps[c][:, 0:n], ACT.Copy).then_inc(*s_bx_copy.mark(u, c))

        def sample_attention():
            sample_mask(0)
            for u in PAIRS:
                for m, (e, kv, c) in enumerate(KEY_GROUPS):
                    act.wait_ge(*s_kt.at(u, m))
                    if m >= 4:
                        act.wait_ge(*s_qk.at(u, m - 4))
                    elif u:
                        act.wait_ge(*s_qk.at(u - 1, 12 + m))
                    act.activation(sKPT[:, c * TILE:(c + 1) * TILE], ps[5 + m % 2][:, :], ACT.Copy).then_inc(*s_kt_copy.mark(u, m))
                act.wait_ge(*s_logits.at(u))
                act.activation(sL[:, :], sL[:, :], ACT.Exp, bias=NM[:, 0, 0:1], accum_out=SUM[:, 0, 0:1]).then_inc(*s_exp.mark(u))
                for c in range(5):
                    act.wait_ge(*s_pt.at(u, c))
                    if c < 4:
                        ins_ = act.activation(sPT[:, 4 * c:4 * c + 4, :], ps[5 + c % 2][:, :].rearrange("p (a b) -> p a b", a=4), ACT.Copy)
                    else:
                        ins_ = act.activation(sPTN[:, :], ps[5][0:NS, 0:P], ACT.Copy)
                    ins_.then_inc(*s_pt_copy.mark(u, c))
                if u + 1 in PAIRS:
                    sample_mask(u + 1)

        def key_high(t, f):
            kv, cols = key_quarter(t, f)
            if f == 0:
                act.wait_ge(*gb_out.at(t, KC - 1))
            act.activation(KHIGH[:, kv, cols], KT[:, kv, cols], ACT.Copy).then_inc(*k_high.mark(t, f))

        def query_high(t, u):
            act.wait_ge(*q_in[u % 2].at(t, u))
            act.activation(QHIGH[u % 2][:, :, :], QU[u % 2][:, :, :], ACT.Copy).then_inc(*q_high.mark(t, u))

        def attend(t):
            for u in range(len(UNITS) + 1):
                if u < len(UNITS):
                    w = width(BLOCKS * t + UNITS[u][0])
                    for hh in range(2):
                        act.wait_ge(*row_max.at(t, u, hh))
                        row = LP[:, u % 2, hh, 0:w]
                        ins_ = act.activation(row, row, ACT.Exp, bias=NM[:, u % 2, hh:hh + 1],
                                              accum_out=SUM[:, u % 2, hh:hh + 1])
                        ins_.then_inc(*expd.mark(t, u, hh))
                if u >= 1:
                    v = u - 1
                    act.wait_ge(*rb.at(t, v))
                    if v >= 2:
                        act.wait_ge(*attn.at(t, v - 2))
                    act.activation(RB[v % 2][:, :], ps[6 + v % 2][:, 256:512], ACT.Copy).then_inc(*rb_copy.mark(t, v))
                if u + 2 < len(UNITS):
                    query_high(t, u + 2)
                if t == 0 and u in (4, 5):
                    split_high(AFTER_PAGES[u - 4])
                if u < len(UNITS):
                    n = BLOCKS * t + UNITS[u][0] + 1
                    for c in range((n + 1) // 2):
                        if on_act(t, u, c):
                            act.wait_ge(*p_t.at(t, u, c))
                            if u == 0 and c == 0:
                                act.wait_ge(*ma_out[0].at(t, KC - 2))
                                act.wait_ge(*ma_out[1].at(t, KC - 1))
                            p_free(act, t, u, c)
                            m = 256 * min(2, n - 2 * c)
                            act.activation(T[p_slot(t, u, c)][:, 0:m], ps[bank("tr", t, u, c)][:, 0:m], ACT.Copy
                                           ).then_inc(*p_copy_a.mark(t, u, c))
                if u == len(UNITS) - 1:
                    if t == 0:
                        act.wait_ge(*s_attn_z.at())
                        act.activation(sBBH, sBB[:, :, :], ACT.Copy).then_inc(*bb_high.mark(t, 0, "S"))
                    attn_high(t, range(KC - 2))
                for b, r in late_runs(t, u - 1):
                    if r == 3:
                        block_mask(t, b)

        def attn_high(t, ks):
            for k in ks:
                act.wait_ge(*attn_z.at(t, (BLOCKS - 1, k // 2)))
                if k == 0:
                    act.wait_ge(*pv.at(t, len(UNITS) - 2))
                act.activation(BBH[:, k, :], BB[:, k, :], ACT.Copy).then_inc(*bb_high.mark(t, k, "P"))

        def evac_c(t, n, f, j):
            parts_out(t, j)
            for p in parts(t):
                m = TILE if p == "P" else NS
                src = ps[PBANK[j, p]][:, 0:m]
                act.wait_ge(*product.at(j, p))
                if n == "pb":
                    if f >= 2:
                        act.wait_ge(*mg_ready.at(t, f - 2, p))
                    act.activation((T if p == "P" else sT)[3 + f % 2][:, :], src, ACT.Copy).then_inc(*evac.mark(j, p))
                elif p == "P":
                    if f >= 2:
                        act.wait_ge(*y_t.at(t, f - 2, p))
                    act.activation(T[1 + f % 2][:, :], src, ACT.Copy, scale=MOD[:, 16 + f, 0:1]).then_inc(*evac.mark(j, p))
                else:
                    if f >= 2:
                        act.wait_ge(*y_t.at(t, f - 2, p))
                    act.activation(sYT[f % 2][:, :], src, ACT.Copy).then_inc(*evac.mark(j, p))

        norm(0)
        split_high(0)
        split_high(1)
        modulate(0)
        for t in range(TILES):
            j = len(GEMMS) // TILES * t
            for i in range(len(PROJ_A)):
                split_high(j + 2)
                evac_a(t, i, j)
                if i:
                    root_a(t, i - 1)
                j += 1
            root_a(t, len(PROJ_A) - 1)
            index_relu(t)
            if t == 0:
                duplicate(0)
            for i in range(len(PROJ_B)):
                if t and i == len(PROJ_B) - 1:
                    query_high(t, 0)
                    query_high(t, 1)
                if j + 2 not in AFTER_PAGES:
                    split_high(j + 2)
                n, f = PROJ_B[i]
                evac_b(t, i, j)
                if n == "ub":
                    conv_taps(f)
                if n == "uh" and f:
                    branch_high(f - 1)
                if n == "za" and f == KC - 1:
                    branch_high(f)
                for quarter in key_quarters(n, f):
                    key_high(t, quarter)
                if t == 0:
                    sample_keys(i)
                    if i == SAMPLE_ITEMS + 2:
                        sample_scores_out()
                j += 1
            masks(t)
            if t == 0:
                sample_attention()
                query_high(t, 0)
                query_high(t, 1)
            attend(t)
            attn_high(t, range(KC - 2, KC))
            for f in range(KC):
                split_high(j + 2)
                evac_c(t, "pb", f, j)
                if f == 4 and t + 1 < TILES:
                    norm(t + 1)
                j += 1
            if t + 1 < TILES:
                modulate(t + 1)
            for f in range(KC):
                split_high(j + 2)
                evac_c(t, "wo", f, j)
                j += 1
            if t == 0:
                act.wait_ge(*conv_t.at("S"))
                for h in range(2):
                    ins_ = act.activation(sCO[:, h * TILE:(h + 1) * TILE], ps[bank("conv", "S", h)][0:2 * NSEQ, :], ACT.Copy)
                ins_.then_inc(*conv_store.mark("S"))
        act.wait_ge(*conv_t.at("P"))
        for h in range(2):
            ins_ = act.activation(CO[:, h * TILE:(h + 1) * TILE], ps[bank("conv", "P", h)][0:2, :], ACT.Copy)
        ins_.then_inc(*conv_store.mark("P"))

    @block.tensor
    def _(pe):
        freed = {}
        count = [0]

        def claim(b):
            if b in freed:
                pe.wait_ge(*freed.pop(b))

        def aux(*key):
            b = 4 + count[0] % 4
            count[0] += 1
            banks[key] = b
            claim(b)
            return b

        def mm(out, lhsT, rhs, start=True, stop=True, **more):
            return pe.matmul(out, lhsT, rhs, start=start, stop=stop, **more)

        def turn(out, in_):
            n = in_.shape[0]
            a = in_.base_partition() if callable(in_.base_partition) else in_.base_partition
            return pe.transpose(out, in_, ident[a:a + n, a:a + n])

        pe.wait_ge(*constants.at("all"))
        pe.wait_ge(*rows_in.at("all"))
        turn(ps[4][:, 0:58], ROWS[:, :]).then_inc(*prep_t.mark("rows"))
        for k in range(KC):
            ins_ = turn(ps[6][:, 16 * k:16 * k + 16], ST16[:, k * P:(k + 1) * P])
        ins_.then_inc(*prep_t.mark("state"))
        pe.wait_ge(*silu_c.at())
        for k in range(KC):
            ins_ = turn(ps[5][:, 9 * k:9 * k + 9], C9[:, k * P:(k + 1) * P])
        ins_.then_inc(*prep_t.mark("c"))
        pe.wait_ge(*prep_c.at("c"))

        def modulation(g):
            b = g % 3
            claim(b)
            for f in range(4 * g, 4 * g + 4):
                pe.wait_ge(*mw_in[f % 8].at(f))
                for k in range(KC):
                    ins_ = mm(ps[b][0:9, (f % 4) * P:(f % 4 + 1) * P], SCT[:, k, :], MW[f % 8][:, k, :], k == 0, k == KC - 1)
                ins_.then_inc(*mod_mm.mark(f))
            freed[b] = mod_row.at(g)

        def turn_modulation(g):
            pe.wait_ge(*mod_row.at(g))
            for f in range(4 * g, 4 * g + 4):
                ins_ = turn(ps[7 if f < 16 else 3][:, 9 * f:9 * f + 9], MROW[g % 2][0:9, (f % 4) * P:(f % 4 + 1) * P])
            ins_.then_inc(*mod_t.mark(g))

        for g in range(4):
            modulation(g)
            if g:
                turn_modulation(g - 1)
        turn_modulation(3)
        freed[4] = prep_c.at("rows")
        freed[5] = prep_c.at("c")
        freed[6] = prep_c.at("state")
        freed[7] = mod_ready.at("AM")

        def turn_x(t):
            pe.wait_ge(*xnorm.at(t, last_part(t)))
            for k in range(KC):
                b = aux("x_t", t, k)
                for blk in range(BLOCKS):
                    ins_ = turn(ps[b][:, blk * P:(blk + 1) * P], XN[:, blk, k * P:(k + 1) * P])
                ins_.then_inc(*x_t.mark(t, k))
                freed[b] = x_mod.at(t, k)
            if t == 0:
                b = aux("x_t", t, "S")
                for k in range(KC):
                    ins_ = turn(ps[b][:, k * NS:(k + 1) * NS], sXN[:, k * P:(k + 1) * P])
                ins_.then_inc(*x_t.mark(t, "S"))
                freed[b] = xs_mod.at()

        def operand_ready(t, n, k, p):
            return bb_ready_at(t, k, p) if n == "pb" else {"pa": ba_ready, "wo": mg_ready}[n].at(t, k, p)

        def products(j):
            t, n, f = GEMMS[j]
            pe.wait_ge(*w_split.at(j))
            if t == 0:
                operand = {"pa": sBA, "pb": sBB2, "wo": sMG}.get(n, sHT)
                b = aux("parts", j)
                for k in range(KC):
                    if (n, f) == PROJ_A[0]:
                        pe.wait_ge(*h_ready.at(t, "S"))
                    elif f == 0 and n in ("pa", "pb", "wo"):
                        pe.wait_ge(*operand_ready(t, n, k, "S"))
                    ins_ = mm(ps[b][:, 0:2 * P], operand[:, k, :], WLH[j % 3][:, :, k, :], k == 0, k == KC - 1)
                ins_.then_inc(*s_parts.mark(j))
                freed[b] = s_parts_copy.at(j)
            hi, lo = {"pa": (BAH, BAL), "pb": (BBH, BBL), "wo": (MGH, MGL)}.get(n, (HTH, HTL))
            b = PBANK[j, "P"]
            claim(b)
            for k in range(KC):
                if (n, f) == PROJ_A[0]:
                    pe.wait_ge(*h_ready.at(t, k, "P"))
                elif f == 0 and n in ("pa", "pb", "wo"):
                    pe.wait_ge(*operand_ready(t, n, k, "P"))
                out = ps[b][:, :]
                mm(out, WH[j % 3][:, k, :], hi[:, k, :], k == 0, False)
                mm(out, WH[j % 3][:, k, :], lo[:, k, :], False, False)
                ins_ = mm(out, WL[j % 3][:, k, :], hi[:, k, :], False, k == KC - 1)
            ins_.then_inc(*product.mark(j, "P"))
            freed[b] = evac.at(j, "P")
            if t == 0:
                pe.wait_ge(*s_parts_copy.at(j))
                b = PBANK[j, "S"]
                claim(b)
                mm(ps[b][:, 0:NS], sRAW[:, 0, :], PAIR[:, :], True, False)
                mm(ps[b][:, 0:NS], sRAW[:, 1, :], PAIR[:, :], False, True).then_inc(*product.mark(j, "S"))
                freed[b] = evac.at(j, "S")

        def after_a(t, i, j):
            n, f = PROJ_A[i]
            for p in parts(t):
                m, blocks = (TILE, BLOCKS) if p == "P" else (NS, 1)
                src = (AS if p == "P" else sAS)[:, i % 8, :]
                rows = m // blocks
                pe.wait_ge(*evac.at(j, p))
                if i in NORMED:
                    b = aux("aux", t, i, p)
                    q = NORMED.index(i)
                    mm(ps[b][:, 0:m], ones[:, :], (SQ if p == "P" else sSQ)[q % 2][:, :]).then_inc(*aux_done.mark(t, i, p))
                    freed[b] = root.at(t, i, p)
                elif n == "v":
                    b = aux("aux", t, i, p)
                    for blk in range(blocks):
                        ins_ = turn(ps[b][0:rows, blk * P:(blk + 1) * P], src[:, blk * rows:(blk + 1) * rows])
                    ins_.then_inc(*aux_done.mark(t, i, p))
                    freed[b] = a_done.at(t, i, p)
                elif n == "ki":
                    b = aux("aux", t, i, p)
                    for blk in range(blocks):
                        turn(ps[b][0:rows, blk * ID:(blk + 1) * ID], src[0:ID, blk * rows:(blk + 1) * rows])
                    if p == "P":
                        for blk in range(BLOCKS):
                            ins_ = turn(ps[b][:, 256 + 8 * blk:264 + 8 * blk], src[ID:ID + IH, blk * P:(blk + 1) * P])
                        ins_.then_inc(*aux_done.mark(t, i, p))
                        freed[b] = a_done.at(t, i, p)
                    else:
                        pe.wait_ge(*w8_ready.at(t, p))
                        b2 = aux("w_rows", t)
                        for h in range(IH):
                            ins_ = mm(ps[b2][:, h * NS:(h + 1) * NS], ident[0:IH, h:h + 1].to_broadcast([IH, P]), sW8[:, 0:NS])
                        ins_.then_inc(*aux_done.mark(t, i, p))
                        freed[b] = a_done.at(t, i, p)
                        freed[b2] = a_done.at(t, i, p)

        def turn_keys(t, i):
            n, f = PROJ_A[i]
            if n != "k":
                return
            for p in parts(t):
                pe.wait_ge(*kt_ready.at(t, f, p))
                b = aux("kT", t, f, p)
                blocks, rows = (BLOCKS, P) if p == "P" else (1, NS)
                for blk in range(blocks):
                    src = KT[:, f, t * TILE + blk * P:t * TILE + (blk + 1) * P] if p == "P" else sKT[:, f, :]
                    ins_ = turn(ps[b][0:rows, blk * P:(blk + 1) * P], src)
                ins_.then_inc(*aux_done.mark(t, "kT", f, p))
                freed[b] = a_done.at(t, i, p)

        def index(t):
            for blk in index_blocks(t):
                for h in range(IH):
                    if h % 2 == 0:
                        pe.wait_ge(*a_done.at(t, PROJ_A.index(("qi", h // 2)), "P"))
                    for c, n in pieces(width(BLOCKS * t + blk)):
                        b = aux("idx", t, blk, h, c)
                        q = QI[:, h, blk * P:(blk + 1) * P]
                        mm(ps[b][:, 0:n], q, KIH[:, c:c + n], True, False)
                        mm(ps[b][:, 0:n], q, KIL[:, c:c + n], False, True).then_inc(*idx_done.mark(t, blk, h, c))
                        freed[b] = relu.at(relus[0])
                        relus[0] += 1

        relus = [0]

        def sample_index(i):
            for s, c in sample_groups(i - 1):
                sample_logits(s, c)
            for s, c in sample_groups(i):
                pe.wait_ge(*kx_dup.at(s))
                b = aux("kx", s, c)
                for pg in range(4):
                    ins_ = turn(ps[b][:, pg * P:(pg + 1) * P], sKX[s % 2][:, 4 * c + pg, :])
                ins_.then_inc(*kx_t.mark(s, c))
                freed[b] = kx_split.at(s, c)
            if i == SAMPLE_ITEMS:
                b = aux("snew")
                mm(ps[b][:, :], sKIH[:, :], sQI[:, :, :].rearrange("p h t -> p (h t)"), True, False)
                mm(ps[b][:, :], sKIL[:, :], sQI[:, :, :].rearrange("p h t -> p (h t)"), False, True).then_inc(*s_idx.mark("new"))
                freed[b] = s_sum.at("new")
            if i == SAMPLE_ITEMS + 2:
                for c in range(5):
                    b = aux("sst", c)
                    pe.wait_ge(*s_sum.at("new"))
                    for k in range(4 if c < 4 else 1):
                        if c < 4:
                            ins_ = turn(ps[b][0:NS, k * P:(k + 1) * P], sST[:, 4 * c + k, :])
                        else:
                            ins_ = turn(ps[b][0:NS, 0:NS], sST[0:NS, RUN, :])
                    ins_.then_inc(*s_score_t.mark(c))
                    freed[b] = s_bx_copy.at("sc", c)

        def sample_logits(s, c):
            n = 4 * s + c
            pe.wait_ge(*kx_split.at(s, c))
            b = aux("sidx", s, c)
            for pg in range(4):
                out = ps[b][:, pg * NS:(pg + 1) * NS]
                q = sQI[:, :, s * NNEW:(s + 1) * NNEW]
                mm(out, sKPH[n % 2][:, pg * P:(pg + 1) * P], q, True, False)
                ins_ = mm(out, sKPL[n % 2][:, pg * P:(pg + 1) * P], q, False, True)
            ins_.then_inc(*s_idx.mark(s, c))
            freed[b] = s_sum.at(s, c)

        def sample_mask(u):
            for c in range(5):
                n = TILE if c < 4 else NS
                pe.wait_ge(*biased.at(0, "S"))
                claim(c)
                rows = by_slot(sSC[:, 0:PAST])[:, 4 * c:4 * c + 4, :] if c < 4 else sSC[:, PAST:PAST + NS]
                mm(ps[c][:, 0:n], sSEL[u // 2][:, u % 2, :], rows).then_inc(*s_bx.mark(u, c))
                freed[c] = s_bx_copy.at(u, c)

        def sample_attention():
            sample_mask(0)
            for u in PAIRS:
                def turn_page(m):
                    e, kv, c = KEY_GROUPS[m]
                    slot = page_slot("k", 2 * u + e)
                    pe.wait_ge(*pg_in[slot].at("k", 2 * u + e))
                    b = 5 + m % 2
                    claim(b)
                    for i in range(4):
                        ins_ = turn(ps[b][:, i * P:(i + 1) * P], sPG[slot][:, 4 * c + i, kv * HD:(kv + 1) * HD])
                    ins_.then_inc(*s_kt.mark(u, m))
                    freed[b] = s_kt_copy.at(u, m)

                turn_page(0)
                for c in range(5):
                    claim(c)
                for m, (e, kv, c) in enumerate(KEY_GROUPS):
                    if m + 1 < len(KEY_GROUPS):
                        turn_page(m + 1)
                    pe.wait_ge(*s_kt_copy.at(u, m))
                    r = first_row(e, kv)
                    q = sQ[:, 2 * u + e, 4 * kv:4 * kv + 4, :].rearrange("p h t -> p (h t)")
                    mm(ps[c][r:r + 32, :], q, sKPT[:, c * TILE:(c + 1) * TILE]).then_inc(*s_qk.mark(u, m))
                    if c == 3:
                        ins_ = mm(ps[4][r:r + 32, 0:NS], q, sKT[:, kv, :])
                ins_.then_inc(*s_qk.mark(u, "new"))
                for c in range(5):
                    freed[c] = s_logits.at(u)
                if u + 1 in PAIRS:
                    sample_mask(u + 1)
                pe.wait_ge(*s_exp.at(u))
                for c in range(5):
                    b = 5 + c % 2
                    claim(b)
                    if c < 4:
                        for i in range(4):
                            ins_ = turn(ps[b][:, i * P:(i + 1) * P], sL[:, (4 * c + i) * P:(4 * c + i + 1) * P])
                    else:
                        ins_ = turn(ps[b][0:NS, 0:P], sL[:, PAST:PAST + NS])
                    ins_.then_inc(*s_pt.mark(u, c))
                    freed[b] = s_pt_copy.at(u, c)
                claim(7)
                pe.wait_ge(*s_pt_copy.at(u, 4))
                for e in range(2):
                    for kv in range(KV):
                        r = first_row(e, kv)
                        mm(ps[7][r:r + 32, 0:HD], sPTN[:, r:r + 32], sV[:, kv * HD:(kv + 1) * HD], True, True, skip_group_check=True)
                    slot = page_slot("v", 2 * u + e)
                    pe.wait_ge(*pg_in[slot].at("v", 2 * u + e))
                    for kv in range(KV):
                        r = first_row(e, kv)
                        for i in range(RUN):
                            ins_ = mm(ps[7][r:r + 32, 0:HD], sPT[:, i, r:r + 32], sPG[slot][:, i, kv * HD:(kv + 1) * HD],
                                      False, True, skip_group_check=True)
                    ins_.then_inc(*s_pv.mark(u, e))
                pe.wait_ge(*s_scaled.at(u))
                turn(ps[7][:, P:2 * P], RB[0][:, 0:P]).then_inc(*s_turned.mark(u))
                freed[7] = s_attn.at(u)

        ring = {"qk": 0, "tr": 0}

        def turn_p(t, u, c):
            n = BLOCKS * t + UNITS[u][0] + 1
            b = 3 + ring["tr"] % 3
            ring["tr"] += 1
            banks["tr", t, u, c] = b
            claim(b)
            for kk in range(min(2, n - 2 * c)):
                for hh in range(2):
                    k = 2 * c + kk
                    ins_ = turn(ps[b][:, (2 * kk + hh) * P:(2 * kk + hh + 1) * P], LP[:, u % 2, hh, k * P:(k + 1) * P])
            ins_.then_inc(*p_t.mark(t, u, c))
            freed[b] = p_copied(t, u, c)

        def head_logits(t, u):
            blk, pr = UNITS[u]
            if u == 0:
                pe.wait_ge(*k_split.at(t, KC - 1))
            pe.wait_ge(*q_split.at(t, u))
            for hh in range(2):
                for c, n in pieces(width(BLOCKS * t + blk)):
                    b = ring["qk"] % 3
                    ring["qk"] += 1
                    banks["qk", t, u, hh, c] = b
                    claim(b)
                    if hh and c + n == width(BLOCKS * t + blk) and u:
                        for e in range(2):
                            pe.wait_ge(*expd.at(t, u - 1, e))
                        turn_p(t, u - 1, 0)
                    out = ps[b][:, 0:n]
                    mm(out, QHIGH[u % 2][:, hh, :], KHIGH[:, pr // 2, c:c + n], True, False)
                    mm(out, QHIGH[u % 2][:, hh, :], KLOW[:, pr // 2, c:c + n], False, False)
                    mm(out, QLOW[u % 2][:, hh, :], KHIGH[:, pr // 2, c:c + n], False, True).then_inc(*qk.mark(t, u, hh, c))
                    freed[b] = logits.at(t, u, hh, c)
            qk.values[t, u] = qk.n

        def head_values(t, u):
            blk, pr = UNITS[u]
            n = BLOCKS * t + blk + 1
            acc = 6 + u % 2
            groups = (n + 1) // 2
            if u == len(UNITS) - 1:
                for hh in range(2):
                    pe.wait_ge(*expd.at(t, u, hh))
                turn_p(t, u, 0)
            for c in range(groups):
                if c + 1 < groups:
                    turn_p(t, u, c + 1)
                pe.wait_ge(*p_copied(t, u, c))
                if c == 0:
                    claim(acc)
                for kk in range(min(2, n - 2 * c)):
                    k = 2 * c + kk
                    ins_ = mm(ps[acc][:, 0:256], V[:, k, (pr // 2) * HD:(pr // 2 + 1) * HD],
                              T[p_slot(t, u, c)][:, kk * 256:(kk + 1) * 256], k == 0, k == n - 1)
                ins_.then_inc(*pv.mark(t, u, c))
            pv.values[t, u] = pv.n
            pe.wait_ge(*diag.at(t, u))
            mm(ps[acc][:, 256:512], ones[:, :], DG[u % 2][:, :]).then_inc(*rb.mark(t, u))
            freed[acc] = attn.at(t, u)

        def turn_y(t, f, j):
            for p in parts(t):
                b = aux("y", t, f, p)
                if p == "P":
                    pe.wait_ge(*evac.at(j, p))
                    for blk in range(BLOCKS):
                        ins_ = turn(ps[b][:, blk * P:(blk + 1) * P], T[1 + f % 2][:, blk * P:(blk + 1) * P])
                else:
                    pe.wait_ge(*gated.at(f))
                    ins_ = turn(ps[b][0:NS, 0:P], sYT[f % 2][:, :])
                ins_.then_inc(*y_t.mark(t, f, p))
                freed[b] = y_sum.at(t, f, p)

        turn_x(0)
        modulation(4)
        modulation(5)
        turn_modulation(4)
        turn_modulation(5)
        freed[3] = mod_ready.at("gate")
        for t in range(TILES):
            j = len(GEMMS) // TILES * t
            for i in range(len(PROJ_A)):
                products(j)
                if i:
                    after_a(t, i - 1, j - 1)
                if i >= 2:
                    turn_keys(t, i - 2)
                j += 1
            after_a(t, len(PROJ_A) - 1, j - 1)
            index(t)
            for i in range(len(PROJ_B)):
                products(j)
                if t == 0:
                    sample_index(i)
                j += 1
            if t == 0:
                sample_attention()
            head_logits(t, 0)
            for u in range(len(UNITS)):
                if u + 1 < len(UNITS):
                    head_logits(t, u + 1)
                head_values(t, u)
            for f in range(KC):
                products(j)
                j += 1
            if t + 1 < TILES:
                turn_x(t + 1)
            for f in range(KC):
                products(j)
                if f:
                    turn_y(t, f - 1, j - 1)
                j += 1
            turn_y(t, KC - 1, j - 1)
            if t in (0, TILES - 1):
                p, src, n = ("S", sUK[:, :, :, :].rearrange("p k s w -> p k (s w)"), 16) if t == 0 else ("P", HALO[:, :, :], 2)
                for h in range(2):
                    b = aux("conv", p, h)
                    for k in range(4):
                        ins_ = turn(ps[b][0:n, k * P:(k + 1) * P], src[:, 4 * h + k, :])
                    freed[b] = conv_store.at(p)
                ins_.then_inc(*conv_t.mark(p))

    @block.vector
    def _(dve):
        def link(ins_):
            ins_.then_inc(*dve_step.mark(dve_step.n))
            dve.wait_ge(dve_step.sem, dve_step.n)

        dve.wait_ge(*prep_t.at("rows"))
        link(dve.tensor_copy(COL[:, :], ps[4][:, 0:58]))
        dve.tensor_scalar(COL[:, 56:57], COL[:, 56:57], float(HD) ** -0.5, None, ALU.mult).then_inc(*prep_c.mark("rows"))
        dve.wait_ge(*prep_t.at("state"))
        dve.tensor_copy(sHS[:, :, :, :].rearrange("p k s w -> p (k s w)"), ps[6][:, 0:128]).then_inc(*prep_c.mark("state"))
        dve.wait_ge(*prep_t.at("c"))
        dve.tensor_copy(SCT[:, :, :].rearrange("p k c -> p (k c)"), ps[5][:, 0:72]).then_inc(*prep_c.mark("c"))
        dve.memset(HALO[:, :, :], 0.0).then_inc(*constants_v.mark("halo"))
        dve.wait_ge(*constants.at("all"))
        for e in range(2):
            ins_ = dve.tensor_copy(PAIR[e * NS:(e + 1) * NS, :], ident[e * NS:(e + 1) * NS, e * NS:(e + 1) * NS])
        for u in PAIRS:
            tokens = ident[0:NS, 2 * u * NNEW:2 * (u + 1) * NNEW].rearrange("p (s t) -> p s t", s=2)
            ins_ = dve.tensor_copy(sSEL[u // 2][:, u % 2, :].rearrange("p (s h t) -> p s h t", s=2, h=HEADS),
                                   tokens.unsqueeze(2).to_broadcast([NS, 2, HEADS, NNEW]))
        ins_.then_inc(*constants_v.mark("sel"))
        dve.wait_ge(*piece.at())
        dve.wait_ge(*table_in.at(NSEQ - 1))
        dve.tensor_copy(TABLEF[:, :], TABLE[:, :])
        link(dve.tensor_scalar(PIECE[:, :], PIECE[:, :], PER_PAGE - 1, None, ALU.bitwise_and))
        link(dve.tensor_copy(PIECEF[:, :], PIECE[:, :]))
        link(dve.tensor_scalar(TABLEF[:, :], TABLEF[:, :], float(PER_PAGE), PIECEF[:, 0:1], ALU.mult, ALU.add))
        dve.tensor_copy(ROW[:, :], TABLEF[:, :]).then_inc(*table_row.mark())

        def norm(t):
            for p in parts(t):
                if p == "P":
                    s, v, rt, r1, r2, n = SS, SV, RT, R1, R2, P
                else:
                    s, v, rt, r1, r2, n = NEED[:, 0:1], NEED[:, 1:2], NEED[:, 2:3], NEED[:, 3:4], NEED[:, 4:5], NS
                s, v, rt, r1, r2 = s[0:n], v[0:n], rt[0:n], r1[0:n], r2[0:n]
                dve.wait_ge(*sumsq.at(t, p))
                dve.tensor_scalar(v, s, 1.0 / D, EPS, ALU.mult, ALU.add).then_inc(*var.mark(t, p))
                dve.wait_ge(*root_x.at(t, p))
                link(dve.reciprocal(r1, rt))
                link(dve.tensor_tensor(r2, r1, r1, ALU.mult))
                link(dve.tensor_tensor(r2, r2, v, ALU.mult))
                link(dve.tensor_scalar(r2, r2, -0.5, 1.5, ALU.mult, ALU.add))
                link(dve.tensor_tensor(r1, r1, r2, ALU.mult))
                if p == "P":
                    for b in range(BLOCKS):
                        ins_ = dve.tensor_scalar(XN[:, b, :], XN[:, b, :], r1[:, b:b + 1], None, ALU.mult)
                else:
                    ins_ = dve.tensor_scalar(sXN[:, :], sXN[:, :], r1, None, ALU.mult)
                ins_.then_inc(*xnorm.mark(t, p))

        def modulation_ready():
            dve.wait_ge(*mod_t.at(3))
            link(dve.tensor_tensor(MOD[:, 0:16, :], ps[7][:, 0:144].rearrange("p (f c) -> p f c", c=9),
                                   COL[:, 8:24].unsqueeze(2).to_broadcast([P, 16, 9]), ALU.add))
            link(dve.tensor_scalar(AM[:, :, :], MOD[:, 8:16, :], 1.0, None, ALU.add))
            dve.tensor_tensor(AM[:, :, :], AM[:, :, :], COL[:, 0:8].unsqueeze(2).to_broadcast([P, 8, 9]), ALU.mult
                              ).then_inc(*mod_ready.mark("AM"))

        def modulate(t):
            for k in range(KC):
                dve.wait_ge(*x_mod.at(t, k))
                if t and k == 0:
                    dve.wait_ge(*product.at(len(GEMMS) // TILES * t - KC - 1, last_part(t - 1)))
                dve.tensor_copy(HTH[:, k, :], T[3 + k % 2][:, :]).then_inc(*h_high.mark(t, k, "P"))
            if t == 0:
                dve.wait_ge(*x_t.at(t, "S"))
                v4 = lambda ap: ap.rearrange("p (k s t) -> p k s t", k=KC, s=NSEQ)
                tmp = v4(T[0][:, :])
                bc = lambda ap: ap[:, :, 1:9].unsqueeze(3).to_broadcast([P, KC, NSEQ, NNEW])
                link(dve.tensor_tensor(tmp, v4(ps[bank("x_t", t, "S")][:, :]), bc(AM), ALU.mult))
                dve.tensor_tensor(tmp, tmp, bc(MOD[:, 0:8, :]), ALU.add).then_inc(*xs_mod.mark())
                dve.wait_ge(*xs_mod.at())
                dve.tensor_copy(sHTH[:, :, :], T[0][:, :].rearrange("p (k t) -> p k t", k=KC)).then_inc(*h_high.mark(t, "S"))

        def item_a(t, i, j):
            n, f = PROJ_A[i]
            for p in parts(t):
                prompt = p == "P"
                m, blocks = (TILE, BLOCKS) if prompt else (NS, 1)
                rows = m // blocks
                src = (AS if prompt else sAS)[:, i % 8, :]
                if n == "ki":
                    dve.wait_ge(*evac.at(j, p))
                    hi, lo = (KIH, KIL) if prompt else (sKIH, sKIL)
                    cols = [slice(t * TILE, (t + 1) * TILE)] if prompt else [slice(0, NS), slice(NS, 2 * NS)]
                    if not prompt:
                        dve.tensor_copy(sW8[:, :], src[ID:ID + IH, :]).then_inc(*w8_ready.mark(t, p))
                    for c in cols:
                        dve.tensor_copy(hi[ID:2 * ID, c], src[0:ID, :])
                        link(dve.tensor_copy(hi[0:ID, c], src[0:ID, :]))
                        dve.tensor_tensor(lo[0:ID, c], src[0:ID, :], hi[0:ID, c].bitcast(F32), ALU.subtract)
                        link(dve.tensor_tensor(lo[ID:2 * ID, c], src[0:ID, :], hi[0:ID, c].bitcast(F32), ALU.subtract))
                    dve.wait_ge(*aux_done.at(t, i, p))
                    b = bank("aux", t, i, p)
                    if prompt:
                        if t:
                            dve.wait_ge(*ki_out.at(t - 1))
                        dve.tensor_copy(KIO[:, :, :].rearrange("p b d -> p (b d)"), ps[b][:, 0:256])
                        ins_ = dve.tensor_scalar(WI[:, :, :].rearrange("p b h -> p (b h)"), ps[b][:, 256:288],
                                                 float(np.float32(float(IH) ** -0.5)) * float(ID) ** -0.5, None, ALU.mult)
                    else:
                        dve.tensor_copy(sKIO[:, :], ps[b][0:NS, 0:ID])
                        ins_ = dve.tensor_scalar(sWR[:, :, :, :].rearrange("p s h t -> p h s t"),
                                                 ps[bank("w_rows", t)][:, :].rearrange("p (h s t) -> p h s t", h=IH, s=NSEQ),
                                                 float(np.float32(float(IH) ** -0.5)) * float(ID) ** -0.5, None, ALU.mult)
                    ins_.then_inc(*a_done.mark(t, i, p))
                elif i in NORMED:
                    dve.wait_ge(*root.at(t, i, p))
                    rs = (RS if prompt else sRS)[NORMED.index(i) % 2][:, :]
                    link(dve.reciprocal(rs, rs))
                    col = COL[:, 57:58] if n == "k" else COL[:, 56:57]
                    if n == "k":
                        dst = KT[:, f, t * TILE:(t + 1) * TILE] if prompt else sKT[:, f, :]
                    else:
                        if prompt and (t or f >= 2):
                            dve.wait_ge(*(q_out[f % 2].at(t, f - 2) if f >= 2 else q_out[f % 2].at(t - 1, HEADS - 2 + f)))
                        dst = QO[f % 2][:, :] if prompt else sQT[:, :]
                    ins_ = dve.scalar_tensor_tensor(dst, src, col, rs, ALU.mult, ALU.mult)
                    if n == "k":
                        ins_.then_inc(*kt_ready.mark(t, f, p))
                        dve.wait_ge(*aux_done.at(t, "kT", f, p))
                        b = bank("kT", t, f, p)
                        if prompt:
                            if f:
                                dve.wait_ge(*k_out.at(t, f - 1))
                            elif t:
                                dve.wait_ge(*k_out.at(t - 1, 1))
                            dve.tensor_copy(KO[:, :, :].rearrange("p b d -> p (b d)"), ps[b][:, :]).then_inc(*a_done.mark(t, i, p))
                        else:
                            dve.tensor_copy(sKO[:, f * HD:(f + 1) * HD], ps[b][0:NS, 0:HD]).then_inc(*a_done.mark(t, i, p))
                    elif prompt:
                        ins_.then_inc(*a_done.mark(t, i, p))
                    else:
                        link(ins_)
                        dve.tensor_copy(sQ[:, :, f, :], s3(sQT[:, :])).then_inc(*a_done.mark(t, i, p))
                elif n == "v":
                    dve.wait_ge(*aux_done.at(t, i, p))
                    b = bank("aux", t, i, p)
                    if prompt:
                        ins_ = dve.tensor_copy(V[:, BLOCKS * t:BLOCKS * (t + 1), f * HD:(f + 1) * HD],
                                               ps[b][:, :].rearrange("p (b d) -> p b d", b=BLOCKS))
                    else:
                        ins_ = dve.tensor_copy(sV[:, f * HD:(f + 1) * HD], ps[b][0:NS, 0:HD])
                    ins_.then_inc(*a_done.mark(t, i, p))
                else:
                    dve.wait_ge(*evac.at(j, p))
                    hi = (T[1] if prompt else sT[1])[:, 0:m]
                    q = QI if prompt else sQI
                    if f:
                        dve.wait_ge(*a_done.at(t, i - 1, p))
                    link(dve.tensor_copy(hi.bitcast(F32R), src))
                    for e in range(2):
                        half = slice(e * ID, (e + 1) * ID)
                        dve.tensor_copy(q[0:ID, 2 * f + e, :], src[half])
                        ins_ = dve.tensor_tensor(q[ID:2 * ID, 2 * f + e, :], src[half], hi[half], ALU.subtract)
                    ins_.then_inc(*a_done.mark(t, i, p))

        relus = [0]

        def weigh(t):
            for blk in index_blocks(t):
                runs = pieces(width(BLOCKS * t + blk))
                for h in range(IH):
                    for c, n in runs:
                        r = relus[0]
                        relus[0] += 1
                        dve.wait_ge(*relu.at(r))
                        dst = scores(t)[:, blk, c:c + n]
                        x = T[1 + r % 4][:, 0:n]
                        w = WI[:, blk, h:h + 1]
                        if h == 0:
                            dve.tensor_scalar(dst, x, w, None, ALU.mult).then_inc(*scored.mark(r))
                        else:
                            dve.wait_ge(*scored.at(r - len(runs)))
                            dve.scalar_tensor_tensor(dst, x, w, dst, ALU.mult, ALU.add).then_inc(*scored.mark(r))

        def sample_index():
            def weigh_pages(s, c):
                n = 4 * s + c
                dve.wait_ge(*s_idx.at(s, c))
                rl = PFX[:, 4 * NS * (n % 2):4 * NS * (n % 2 + 1)]
                link(dve.scalar_tensor_tensor(
                    rl.rearrange("p (g x) -> p g x", g=4), ps[bank("sidx", s, c)][:, 0:4 * NS].rearrange("p (g x) -> p g x", g=4), 0.0,
                    sWR[:, s, :, :].rearrange("p h t -> p (h t)").unsqueeze(1).to_broadcast([P, 4, NS]), ALU.max, ALU.mult))
                dve.tensor_reduce(sST[:, 4 * c:4 * c + 4, s * NNEW:(s + 1) * NNEW],
                                  rl.rearrange("p (g h t) -> p g t h", g=4, h=IH), AX_X, ALU.add).then_inc(*s_sum.mark(s, c))

            for s in range(NSEQ):
                for c in range(4):
                    n = 4 * s + c
                    dve.wait_ge(*kx_high.at(s, c))
                    dve.tensor_tensor(sKPL[n % 2][:, :], ps[bank("kx", s, c)][:, :], sKPH[n % 2][:, :].bitcast(F32), ALU.subtract
                                      ).then_inc(*kx_split.mark(s, c))
                    if (s, c) != (0, 0):
                        weigh_pages(*divmod(4 * s + c - 1, 4))
            weigh_pages(NSEQ - 1, 3)
            dve.wait_ge(*s_idx.at("new"))
            dve.wait_ge(*s_sum.at(NSEQ - 1, 3))
            v4 = lambda ap: ap.rearrange("p (h s t) -> p h s t", h=IH, s=NSEQ)
            link(dve.tensor_scalar(PFX[:, :], ps[bank("snew")][:, :], 0.0, None, ALU.max))
            link(dve.tensor_tensor(v4(PFX[:, :]), v4(PFX[:, :]), sWR[:, :, :, :].rearrange("p s h t -> p h s t"), ALU.mult))
            dve.tensor_reduce(sST[0:NS, NPAGES, :], PFX[0:NS, :].rearrange("p (h t) -> p t h", h=IH), AX_X, ALU.add
                              ).then_inc(*s_sum.mark("new"))

        def select(t):
            rows = [(scores(t)[:, b, 0:width(BLOCKS * t + b)], P, b, b) for b in index_blocks(t)]
            if t == 0:
                rows.append((sSC[:, :], NS, 4, "S"))
            k = len(rows)
            c0 = rows[0][2]
            cs = slice(c0, rows[-1][2] + 1)
            if t == 0:
                link(dve.memset(ABS[:, :], 1.0))
                link(dve.memset(CNT[:, :], 0.0))
                dve.wait_ge(*s_bx_copy.at("sc", 4))
            dve.wait_ge(*scored.at(relus[0] - 1))
            for row, n, c, name in rows:
                ins_ = dve.tensor_reduce(ABS[0:n, c:c + 1], row, AX_X, ALU.max, apply_absolute_value=True)
                ins_.then_inc(*dve_step.mark(dve_step.n))
                abs_values[t, name] = dve_step.n
            dve.wait_ge(dve_step.sem, dve_step.n)
            link(dve.tensor_scalar(HI[:, cs], ABS[:, cs], 1.0 + 2.0 ** -20, 1e-25, ALU.mult, ALU.add))
            link(dve.tensor_scalar(LO[:, cs], HI[:, cs], -1.0, None, ALU.mult))
            link(dve.memset(MID[:, cs], 0.0))
            dve.wait_ge(*causal.at(t))
            for step in range(STEPS):
                for row, n, c, name in rows:
                    link(dve.tensor_scalar(JUNK[0:n, 0:row.shape[1]], row, MID[0:n, c:c + 1], 0.0, ALU.is_ge, ALU.add,
                                           accum_out=CNT[0:n, c:c + 1]))
                dve.tensor_scalar(GE[:, cs], CNT[:, cs], float(TOPK), None, ALU.is_ge)
                link(dve.tensor_scalar(LT[:, cs], CNT[:, cs], float(TOPK), None, ALU.is_lt))
                dve.copy_predicated(LO[:, cs], GE[:, cs], MID[:, cs])
                link(dve.copy_predicated(HI[:, cs], LT[:, cs], MID[:, cs]))
                link(dve.tensor_tensor(MID[:, cs], LO[:, cs], HI[:, cs], ALU.add))
                link(dve.tensor_scalar(MID[:, cs], MID[:, cs], 0.5, None, ALU.mult))
            for row, n, c, name in rows:
                link(dve.tensor_scalar(JUNK[0:n, 0:row.shape[1]], row, HI[0:n, c:c + 1], 0.0, ALU.is_ge, ALU.add,
                                       accum_out=CNT[0:n, c:c + 1]))
                link(dve.tensor_scalar(NEED[0:n, c:c + 1], CNT[0:n, c:c + 1], -1.0, float(TOPK), ALU.mult, ALU.add))
            for row, n, c, name in rows:
                if name not in late_blocks(t):
                    for r in range(len(pieces(row.shape[1]))):
                        choose(t, row, n, c, name, r)

        def choose(t, row, n, c, name, r):
            hi, lo, need = HI[0:n, c:c + 1], LO[0:n, c:c + 1], NEED[0:n, c:c + 1]
            runs = pieces(row.shape[1])
            a, m = runs[r]
            x, g, band, pre = row[:, a:a + m], GT[0:n, 0:m], BD[0:n, 0:m], PFX[0:n, 0:m]
            link(dve.tensor_scalar(g, x, hi, None, ALU.is_ge))
            link(dve.scalar_tensor_tensor(band, x, lo, g, ALU.is_ge, ALU.subtract))
            link(dve.tensor_tensor_scan(pre, band, band, CNT[0:n, c:c + 1] if a else 0.0, ALU.add, ALU.bypass))
            if r + 1 < len(runs):
                link(dve.tensor_copy(CNT[0:n, c:c + 1], PFX[0:n, TILE - 1:TILE]))
            link(dve.scalar_tensor_tensor(band, pre, need, band, ALU.is_le, ALU.mult))
            ins_ = dve.scalar_tensor_tensor(x, band, -1.0, g, ALU.add, ALU.add)
            if r + 1 < len(runs):
                link(ins_)
            else:
                ins_.then_inc(*mask.mark(t, name))
                dve.wait_ge(*mask.at(t, name))

        def sample_attention():
            for u in PAIRS:
                dve.wait_ge(*s_bx_copy.at(u, 4))
                dve.wait_ge(*s_qk.at(u, "new"))
                if u:
                    dve.wait_ge(*s_pt.at(u - 1, 4))
                for c in range(5):
                    n = TILE if c < 4 else NS
                    ins_ = dve.tensor_tensor_reduce(sL[:, c * TILE:c * TILE + n], ps[c][:, 0:n], sBX[:, c * TILE:c * TILE + n],
                                                    1.0, -3e38, ALU.add, ALU.max, LO[:, c:c + 1])
                link(ins_)
                dve.tensor_reduce(NM[:, 0, 0:1], LO[:, 0:5], AX_X, ALU.max, negate=True).then_inc(*s_logits.mark(u))
                dve.wait_ge(*s_exp.at(u))
                link(dve.reciprocal(RIN[:, 0, 0:1], SUM[:, 0, 0:1]))
                dve.wait_ge(*s_pv.at(u, 1))
                dve.tensor_scalar(RB[0][:, 0:P], ps[7][:, 0:P], RIN[:, 0, 0:1], None, ALU.mult).then_inc(*s_scaled.mark(u))
                dve.wait_ge(*s_turned.at(u))
                for kv in range(KV):
                    ins_ = dve.tensor_copy(
                        sBB[:, 4 * kv:4 * kv + 4, 2 * u * NNEW:2 * (u + 1) * NNEW].rearrange("p g (s t) -> p s g t", s=2),
                        ps[7][:, P:2 * P].rearrange("p (s k g t) -> p s k g t", s=2, k=KV, g=4)[:, :, kv])
                ins_.then_inc(*s_attn.mark(u))

        def mask_logits(t, u):
            blk, pr = UNITS[u]
            runs = pieces(width(BLOCKS * t + blk))
            if u >= 2:
                dve.wait_ge(*pv.at(t, u - 2))
            if pr == 0:
                dve.wait_ge(*(biased if blk in index_blocks(t) else causal).at(t, blk))
            for hh in range(2):
                for x, (c, n) in enumerate(runs):
                    dve.wait_ge(*qk.at(t, u, hh, c))
                    ins_ = dve.tensor_tensor_reduce(LP[:, u % 2, hh, c:c + n], ps[bank("qk", t, u, hh, c)][:, 0:n],
                                                    scores(t)[:, blk, c:c + n], 1.0, -3e38, ALU.add, ALU.max,
                                                    PM[:, u % 2, hh, x:x + 1])
                    ins_.then_inc(*logits.mark(t, u, hh, c))
                dve.wait_ge(*logits.at(t, u, hh, runs[-1][0]))
                dve.tensor_reduce(NM[:, u % 2, hh:hh + 1], PM[:, u % 2, hh, 0:len(runs)], AX_X, ALU.max, negate=True
                                  ).then_inc(*row_max.mark(t, u, hh))

        def finish(t, u):
            blk, pr = UNITS[u]
            dve.wait_ge(*rb_copy.at(t, u))
            dve.tensor_tensor(BB[:, 2 * pr:2 * pr + 2, blk * P:(blk + 1) * P],
                              ps[6 + u % 2][:, 0:256].rearrange("p (h q) -> p h q", h=2),
                              RB[u % 2][:, :].rearrange("p (h q) -> p h q", h=2), ALU.mult).then_inc(*attn.mark(t, u))

        def attend(t):
            dve.wait_ge(*gate_mul.at(t, KC - 1, "P"))
            dve.wait_ge(*product.at(len(GEMMS) // TILES * t + len(PROJ_A) + len(PROJ_B) - 1, last_part(t)))
            mask_logits(t, 0)
            for u in range(len(UNITS)):
                if u + 1 < len(UNITS):
                    mask_logits(t, u + 1)
                dve.wait_ge(*expd.at(t, u, 1))
                link(dve.reciprocal(RIN[:, u % 2, :], SUM[:, u % 2, :]))
                if u >= 2:
                    dve.wait_ge(*rb.at(t, u - 2))
                for hh in range(2):
                    ins_ = dve.tensor_scalar(DG[u % 2][:, hh * P:(hh + 1) * P], ident[:, :], RIN[:, u % 2, hh:hh + 1], None, ALU.mult)
                ins_.then_inc(*diag.mark(t, u))
                n = BLOCKS * t + UNITS[u][0] + 1
                for c in range((n + 1) // 2):
                    if on_act(t, u, c):
                        continue
                    dve.wait_ge(*p_t.at(t, u, c))
                    p_free(dve, t, u, c)
                    m = 256 * min(2, n - 2 * c)
                    dve.tensor_copy(T[p_slot(t, u, c)][:, 0:m], ps[bank("tr", t, u, c)][:, 0:m]).then_inc(*p_copy.mark(t, u, c))
                if u:
                    finish(t, u - 1)
                for b, r in late_runs(t, u):
                    choose(t, scores(t)[:, b, 0:width(BLOCKS * t + b)], P, b, b, r)
            attn_low(t, 1)
            finish(t, len(UNITS) - 1)

        def attn_low(t, k):
            if k == 1:
                dve.wait_ge(*pv.at(t, len(UNITS) - 1))
            dve.wait_ge(*bb_high.at(t, k, "P"))
            dve.tensor_tensor(BBL[:, k, :], BB[:, k, :], BBH[:, k, :].bitcast(F32), ALU.subtract).then_inc(*bb_low_dve.mark(t, k, "P"))

        def merge(t, f, j):
            for p in parts(t):
                x = (T if p == "P" else sT)[3 + f % 2][:, :]
                gate = (GB if p == "P" else sGB)[:, f, :]
                dve.wait_ge(*evac.at(j, p))
                if p == "P":
                    dve.wait_ge(*gb_in[f % 2].at(t, f))
                link(dve.tensor_tensor(x, x, gate, ALU.mult))
                if p == "P":
                    dve.wait_ge(*ma_in[f % 2].at(t, f))
                link(dve.tensor_tensor(x, x, T[1 + f % 2][:, :] if p == "P" else sMA[:, f, :], ALU.add))
                dve.tensor_copy((MGH if p == "P" else sMGH)[:, f, :], x).then_inc(*merged.mark(t, f, p))

        def residual(t, f):
            for p in parts(t):
                dve.wait_ge(*y_t.at(t, f, p))
                b = bank("y", t, f, p)
                if p == "P":
                    dve.wait_ge(*xr_in[f % 2].at(t, f))
                    if f >= 2:
                        dve.wait_ge(*y_out[f % 2].at(t, f - 2))
                    dve.tensor_tensor(YO[f % 2][:, :, :].rearrange("p b d -> p (b d)"), ps[b][:, :],
                                      XR[f % 2][:, :, :].rearrange("p b d -> p (b d)"), ALU.add).then_inc(*y_sum.mark(t, f, p))
                else:
                    dve.wait_ge(*xs_in.at())
                    dve.tensor_tensor(sYO[:, f * P:(f + 1) * P], ps[b][0:NS, 0:P], sXR[:, f * P:(f + 1) * P], ALU.add
                                      ).then_inc(*y_sum.mark(t, f, p))

        def gate_sample(f, j):
            dve.wait_ge(*evac.at(j, "S"))
            dve.tensor_tensor(s3(sYT[f % 2][:, :]), s3(sYT[f % 2][:, :]),
                              MOD[:, 16 + f, 1:9].unsqueeze(2).to_broadcast([P, NSEQ, NNEW]), ALU.mult).then_inc(*gated.mark(f))

        def modulation_row(g):
            dve.wait_ge(*mod_mm.at(4 * g + 3))
            if g >= 2:
                dve.wait_ge(*mod_t.at(g - 2))
            dve.tensor_copy(MROW[g % 2][0:9, :], ps[g % 3][0:9, :]).then_inc(*mod_row.mark(g))

        modulation_row(0)
        norm(0)
        for g in range(1, 4):
            modulation_row(g)
        modulation_ready()
        modulate(0)
        modulation_row(4)
        modulation_row(5)
        dve.wait_ge(*mod_t.at(5))
        dve.tensor_tensor(MOD[:, 16:24, :], ps[3][:, 144:216].rearrange("p (f c) -> p f c", c=9),
                          COL[:, 24:32].unsqueeze(2).to_broadcast([P, 8, 9]), ALU.add).then_inc(*mod_ready.mark("gate"))
        for t in range(TILES):
            j = len(GEMMS) // TILES * t
            for i in range(len(PROJ_A)):
                item_a(t, i, j)
                j += 1
            weigh(t)
            if t == 0:
                sample_index()
            select(t)
            if t == 0:
                sample_attention()
            attend(t)
            for k in (3, 5, 7):
                attn_low(t, k)
            j += len(PROJ_B)
            for f in range(KC):
                merge(t, f, j)
                if f == 4 and t + 1 < TILES:
                    norm(t + 1)
                j += 1
            if t + 1 < TILES:
                modulate(t + 1)
            for f in range(KC):
                if t == 0:
                    gate_sample(f, j)
                if f:
                    residual(t, f - 1)
                j += 1
            residual(t, KC - 1)

    @block.gpsimd
    def _(pool):
        def link(ins_):
            ins_.then_inc(*pool_step.mark(pool_step.n))
            pool.wait_ge(pool_step.sem, pool_step.n)

        link(pool.memset(ident[:, :], 0.0))
        pool.affine_select(out=ident[:, :], in_=ident[:, :], compare_op=ALU.not_equal, fill=1.0, base=0,
                           pattern=[[-1, P]], channel_multiplier=1).then_inc(*constants.mark("ident"))
        pool.memset(EPSC, EPS)
        pool.iota(PIECE[:, :], [[0, 1]], base=0, channel_multiplier=1).then_inc(*piece.mark())
        pool.memset(ones[:, :], 1.0).then_inc(*constants.mark("all"))

        def split_low(j):
            if j < len(GEMMS):
                pool.wait_ge(*w_high.at(j))
                pool.tensor_tensor(WL[j % 3][:, :, :], WR[j % 3][:, :, :], WH[j % 3][:, :, :].bitcast(F32), ALU.subtract
                                   ).then_inc(*w_split.mark(j))

        def gather(out, cache, s, sig):
            rows = cache.rearrange("n (c r) d -> (n c) (r d)", c=PER_PAGE)
            pool.indirect_dma_start(out, None, rows, bass.IndirectOffsetOnAxis(ap=ROW[:, s:s + 1], axis=0)).then_inc(*sig)

        def gather_index_keys(s):
            if s == 0:
                pool.wait_ge(*table_row.at())
                pool.wait_ge(*mod_mm.at(23))
            if s >= 2:
                pool.wait_ge(*kx_dup.at(s - 2))
            gather(sKR[s % 2][:, :, :].rearrange("p i d -> p (i d)"), ins["cache_kidx"][0], s, kx_in[s % 2].mark(s))

        def gather_pages(n):
            what, s = PAGE_USES[n]
            if n < 3:
                pool.wait_ge(*product.at(AFTER_PAGES[0] - 1, "S"))
            else:
                before, q = PAGE_USES[n - 3]
                pool.wait_ge(*(s_kt.at(q // 2, 8 * (q % 2) + 7) if before == "k" else s_pv.at(q // 2, q % 2)))
            gather(sPG[n % 3][:, :, :].rearrange("p i d -> p (i d)"), ins["cache_" + what][0].rearrange("n p h d -> n p (h d)"),
                   s, pg_in[n % 3].mark(what, s))

        def h_low(t):
            for k in range(KC):
                pool.wait_ge(*h_high.at(t, k, "P"))
                pool.tensor_tensor(HTL[:, k, :], T[3 + k % 2][:, :], HTH[:, k, :].bitcast(F32), ALU.subtract
                                   ).then_inc(*h_ready.mark(t, k, "P"))
            if t == 0:
                pool.wait_ge(*h_high.at(t, "S"))
                pool.tensor_tensor(sHTL[:, :, :], T[0][:, :].rearrange("p (k t) -> p k t", k=KC),
                                   sHTH[:, :, :].bitcast(F32), ALU.subtract).then_inc(*h_ready.mark(t, "S"))

        def fill_future(t):
            for b in range(BLOCKS):
                i = BLOCKS * t + b
                row = scores(t)[:, b, 0:width(i)]
                if b in index_blocks(t):
                    pool.wait_ge(dve_step.sem, abs_values[t, b] if known else 1)
                else:
                    link(pool.memset(row, 0.0))
                pool.affine_select(out=row[:, i * P:], in_=row[:, i * P:], compare_op=ALU.is_ge, fill=NEG, base=0,
                                   pattern=[[-1, P]], channel_multiplier=1).then_inc(*causal.mark(t, b))
            if t == 0:
                pool.wait_ge(dve_step.sem, abs_values[t, "S"] if known else 1)
                new = sSC[:, PAST:PAST + NS]
                v = new.rearrange("p (s t) -> p s t", s=NSEQ)
                link(pool.affine_select(out=new, in_=new, compare_op=ALU.is_ge, fill=NEG, base=0, pattern=[[-1, NS]],
                                        channel_multiplier=1))
                pool.affine_select(out=v, in_=v, compare_op=ALU.is_ge, fill=NEG, base=NNEW - 1, pattern=[[NNEW, NSEQ], [0, NNEW]],
                                   channel_multiplier=-1).then_inc(*causal.mark(t, "S"))
            causal.values[t,] = causal.n

        def conv_input(f, j):
            for p in parts(t):
                pool.wait_ge(*evac.at(j, p))
                if f:
                    pool.wait_ge(*taps.at(t, f - 1, p))
                if p == "P":
                    pool.tensor_copy(U[:, 0:2], HALO[:, f, :])
                    link(pool.tensor_tensor(U[:, 2:TILE + 2], T[2][:, :], T[1][:, :], ALU.mult))
                    pool.tensor_copy(HALO[:, f, :], U[:, TILE:TILE + 2]).then_inc(*u_ready.mark(t, f, p))
                else:
                    pool.tensor_copy(sU[:, :, 0:2], sHS[:, f, :, :])
                    link(pool.tensor_tensor(sU[:, :, 2:NNEW + 2], s3(sT[2][:, :]), s3(sT[1][:, :]), ALU.mult))
                    pool.tensor_copy(sUK[:, f, :, :], sU[:, :, NNEW:NNEW + 2]).then_inc(*u_ready.mark(t, f, p))

        def convolve(f, j):
            for p in parts(t):
                x = [a[:, :] for a in (T if p == "P" else sT)]
                pool.wait_ge(*taps.at(t, f, p))
                link(pool.tensor_tensor(x[0], x[0], x[2], ALU.add))
                link(pool.tensor_tensor(x[0], x[0], x[1], ALU.add))
                link(pool.tensor_tensor(x[0], x[0], x[3], ALU.mult))
                pool.wait_ge(*evac.at(j, p))
                pool.tensor_tensor(x[0], x[0], x[4], ALU.mult).then_inc(*conv.mark(t, f, p))

        def branch_low(f):
            for p in parts(t):
                pool.wait_ge(*ba_high.at(t, f, p))
                if p == "P":
                    pool.tensor_tensor(BAL[:, f, :], T[0][:, :], BAH[:, f, :].bitcast(F32), ALU.subtract).then_inc(*ba_ready.mark(t, f, p))
                else:
                    pool.tensor_tensor(sBAL[:, f, :], sT[0][:, :], sBAH[:, f, :].bitcast(F32), ALU.subtract
                                       ).then_inc(*ba_ready.mark(t, f, p))

        def gate_a(f, j):
            for p in parts(t):
                pool.wait_ge(*evac.at(j, p))
                tt = T if p == "P" else sT
                g, x = tt[1 + f % 2][:, :], tt[3 + f % 2][:, :]
                pool.tensor_tensor(x if p == "P" else sMA[:, f, :], x, g, ALU.mult).then_inc(*gate_mul.mark(t, f, p))

        def key_low(t, f):
            kv, cols = key_quarter(t, f)
            pool.wait_ge(*k_high.at(t, f))
            pool.tensor_tensor(KLOW[:, kv, cols], KT[:, kv, cols], KHIGH[:, kv, cols].bitcast(F32), ALU.subtract
                               ).then_inc(*k_split.mark(t, f))

        def whole_keys(t):
            pool.wait_ge(*qk.at(t, len(UNITS) - 1))
            for f in range(KC):
                kv, cols = key_quarter(t, f)
                ins_ = pool.tensor_tensor(KT[:, kv, cols], KLOW[:, kv, cols].bitcast(F32), KHIGH[:, kv, cols].bitcast(F32), ALU.add)
            ins_.then_inc(*k_whole.mark(t))

        def query_low(t, u):
            pool.wait_ge(*q_high.at(t, u))
            pool.tensor_tensor(QLOW[u % 2][:, :, :], QU[u % 2][:, :, :], QHIGH[u % 2][:, :, :].bitcast(F32), ALU.subtract
                               ).then_inc(*q_split.mark(t, u))

        def attn_gate(t, u):
            blk, pr = UNITS[u]
            pool.wait_ge(*attn.at(t, u))
            x = BB[:, 2 * pr:2 * pr + 2, blk * P:(blk + 1) * P]
            pool.tensor_tensor(x, x, SZB[:, 2 * pr:2 * pr + 2, blk * P:(blk + 1) * P], ALU.mult).then_inc(*attn_z.mark(t, UNITS[u]))

        def sample_low(t):
            pool.wait_ge(*bb_high.at(t, 0, "S"))
            pool.tensor_tensor(sBBL, sBB[:, :, :], sBBH.bitcast(F32), ALU.subtract).then_inc(*bb_low_pool.mark(t, 0, "S"))

        def attn_low(t, k):
            if k == 0:
                pool.wait_ge(*pv.at(t, len(UNITS) - 1))
            pool.wait_ge(*bb_high.at(t, k, "P"))
            pool.tensor_tensor(BBL[:, k, :], BB[:, k, :], BBH[:, k, :].bitcast(F32), ALU.subtract).then_inc(*bb_low_pool.mark(t, k, "P"))

        def merge_low(t, f):
            for p in parts(t):
                pool.wait_ge(*merged.at(t, f, p))
                x = (T if p == "P" else sT)[3 + f % 2][:, :]
                hi, lo = (MGH, MGL) if p == "P" else (sMGH, sMGL)
                pool.tensor_tensor(lo[:, f, :], x, hi[:, f, :].bitcast(F32), ALU.subtract).then_inc(*mg_ready.mark(t, f, p))

        pool.wait_ge(*prep_c.at("state"))
        pool.wait_ge(*constants_v.at("halo"))
        split_low(0)
        split_low(1)
        h_low(0)
        gather_index_keys(0)
        gather_index_keys(1)
        for t in range(TILES):
            j = len(GEMMS) // TILES * t
            for i in range(len(PROJ_A)):
                split_low(j + 2)
                j += 1
            for i in range(len(PROJ_B)):
                if t and i == len(PROJ_B) - 1:
                    query_low(t, 0)
                    query_low(t, 1)
                if j + 2 not in AFTER_PAGES:
                    split_low(j + 2)
                if t == 0 and i % 2 and i // 2 + 2 < NSEQ:
                    gather_index_keys(i // 2 + 2)
                if i == (SAMPLE_ITEMS + 3 if t == 0 else 1):
                    fill_future(t)
                n, f = PROJ_B[i]
                if n == "uc":
                    conv_input(f, j)
                if n == "za":
                    convolve(f, j)
                if n == "uh" and f:
                    branch_low(f - 1)
                if n == "za" and f == KC - 1:
                    branch_low(f)
                if n == "pa":
                    gate_a(f, j)
                for quarter in key_quarters(n, f):
                    key_low(t, quarter)
                j += 1
            if t == 0:
                for n in range(len(PAGE_USES)):
                    gather_pages(n)
            if t == 0:
                query_low(t, 0)
                query_low(t, 1)
                pool.wait_ge(*s_attn.at(PAIRS[-1]))
                pool.tensor_tensor(sBB[:, :, :], sBB[:, :, :], sSZB[:, :, :], ALU.mult).then_inc(*s_attn_z.mark())
            for u in range(len(UNITS)):
                if u + 2 < len(UNITS):
                    query_low(t, u + 2)
                if t == 0 and u in (4, 5):
                    split_low(AFTER_PAGES[u - 4])
                if u:
                    attn_gate(t, u - 1)
                if u == len(UNITS) - 2 and t + 1 < TILES:
                    whole_keys(t)
            if t == 0:
                sample_low(t)
            attn_low(t, 0)
            attn_low(t, 2)
            attn_gate(t, len(UNITS) - 1)
            attn_low(t, 4)
            attn_low(t, 6)
            for f in range(KC):
                split_low(j + 2)
                merge_low(t, f)
                j += 1
            if t + 1 < TILES:
                h_low(t + 1)
            for f in range(KC):
                split_low(j + 2)
                j += 1

    ctx.close()

_INS = ["x_prompt", "x_sample", "c_prompt", "c_sample", "cache_k", "cache_v", "cache_kidx", "state_conv", "page_table",
        "norm_g", "w_mod", "b_mod", "w_in", "conv_w", "q_norm", "k_norm", "w_proj_a", "w_proj_b", "w_out"]
_OUTS = [("y_prompt", (1, SEQ, D)), ("y_sample", (NSEQ, NNEW, D)), ("k_prompt", (1, 1, SEQ, KV, HD)),
         ("v_prompt", (1, 1, SEQ, KV, HD)), ("kidx_prompt", (1, 1, SEQ, ID)), ("conv_prompt", (1, 1, 2, D)),
         ("k_sample", (1, NSEQ, NNEW, KV, HD)), ("v_sample", (1, NSEQ, NNEW, KV, HD)), ("kidx_sample", (1, NSEQ, NNEW, ID)),
         ("conv_sample", (1, NSEQ, 2, D))]


def declare(nc, arrays):
    ins = {n: nc.dram_tensor("in_" + n, a.shape, mybir.dt.from_np(a.dtype), kind="ExternalInput").ap() for n, a in arrays.items()}
    outs = {n: nc.dram_tensor("out_" + n, shape, F32, kind="ExternalOutput").ap() for n, shape in _OUTS}
    return ins, outs


def kernel(**inputs):
    import concourse.bacc as bacc
    from concourse.bass_utils import run_bass_kernel_spmd as run

    arrays = {n: np.ascontiguousarray(inputs[n]) for n in _INS}
    plan = {}
    draft = bacc.Bacc("TRN2", target_bir_lowering=False, num_devices=1)
    program(draft, *declare(draft, arrays), plan)
    nc = bacc.Bacc("TRN2", target_bir_lowering=False, num_devices=1)
    program(nc, *declare(nc, arrays), plan)
    r = run(nc, [{"in_" + n: a for n, a in arrays.items()}], core_ids=[0])
    return tuple(r.results[0]["out_" + n] for n, _ in _OUTS)
```
